# Optimizing a Trainium2 kernel written in Bass

```python
import jax
import jax.numpy as jnp
from jax import lax
import numpy as np

D_MODEL = 1024
BATCH = 1
SEQ = 512
DEPTH = 2
DEC_BATCH = 8
DEC_SEQ = 1
PAST_LEN = 256
PAGE_SIZE = 128

N_SUB = 3
POOL_WINDOWS = (2, 4, 8, 16)
POOL_GROUPS = 4
POOL_GROUP_DIM = D_MODEL // 16
POOL_WIDTH = POOL_GROUPS * POOL_GROUP_DIM
POOL_STATE = max(POOL_WINDOWS) - 1
HGRN_HEADS = 4
HGRN_K = 128
HGRN_V = D_MODEL // 16
HGRN_F_WIDTH = HGRN_HEADS * HGRN_K
HGRN_I_WIDTH = HGRN_HEADS * HGRN_V
HGRN_CHUNK = 64
F_FLOOR = 1e-30
N_HEADS = 8
N_KV_HEADS = 2
HEAD_DIM = 64
GROUP = N_HEADS // N_KV_HEADS
ATTN_WIDTH = N_HEADS * HEAD_DIM
KV_WIDTH = N_KV_HEADS * HEAD_DIM
IDX_HEADS = 4
IDX_DIM = 64
TOPK_MAX = 256
Q_BLOCK = 128
ROPE_THETA = 10000.0
ATTN_SCALE = HEAD_DIM ** -0.5
IDX_SCALE = (IDX_DIM * IDX_HEADS) ** -0.5
NEG_BIG = -1e30
N_BRANCH = 3
D_FF = 2816
EPS = 1e-6
IN_SPLITS = (POOL_WIDTH, HGRN_F_WIDTH, HGRN_F_WIDTH, HGRN_I_WIDTH, HGRN_I_WIDTH,
             ATTN_WIDTH, KV_WIDTH, KV_WIDTH, IDX_HEADS * IDX_DIM, IDX_DIM, IDX_HEADS,
             N_BRANCH * D_MODEL)
IN_WIDTH = sum(IN_SPLITS)

kernel_name = 'hybrid_pool_hgrn2_dsa_macaron_step'

def _rmsnorm(x, g=None):
    xf = x.astype(jnp.float32)
    y = xf * lax.rsqrt(jnp.mean(xf * xf, axis=-1, keepdims=True) + EPS)
    if g is not None:
        y = y * g.astype(jnp.float32)
    return y.astype(x.dtype)

def _swiglu(h, wg, wu, wd):
    return (jax.nn.silu(h @ wg) * (h @ wu)) @ wd

def _split_in(p):
    parts, off = [], 0
    for n in IN_SPLITS:
        parts.append(p[..., off:off + n])
        off += n
    return parts

def _rope(x, pos):
    half = x.shape[-1] // 2
    inv = ROPE_THETA ** (-jnp.arange(half, dtype=jnp.float32) / half)
    ang = pos.astype(jnp.float32)[:, None] * inv[None, :]
    cos = jnp.cos(ang)[:, None, :]
    sin = jnp.sin(ang)[:, None, :]
    xf = x.astype(jnp.float32)
    x1, x2 = xf[..., :half], xf[..., half:]
    return jnp.concatenate([x1 * cos - x2 * sin, x2 * cos + x1 * sin], axis=-1).astype(x.dtype)

def _gather_pages(pool, page_table):
    g = pool[page_table]
    return g.reshape((g.shape[0], g.shape[1] * g.shape[2]) + g.shape[3:])

def _lower_bounds(p):
    sm = jax.nn.softmax(p.astype(jnp.float32), axis=0)
    return jnp.cumsum(sm, axis=0) - sm[0:1]

def _pool_mix(u, u_prev, p0, w, scale):
    B, T, _ = u.shape
    ue = jnp.concatenate([u_prev.astype(u.dtype), u], axis=1).astype(jnp.float32)
    cs = jnp.pad(jnp.cumsum(ue, axis=1), ((0, 0), (1, 0), (0, 0)))
    hi = cs[:, POOL_STATE + 1:POOL_STATE + 1 + T]
    n_avail = (p0 + 1 + jnp.arange(T)).astype(jnp.float32)
    parts = []
    for gi, wdw in enumerate(POOL_WINDOWS):
        sl = slice(gi * POOL_GROUP_DIM, (gi + 1) * POOL_GROUP_DIM)
        lo = cs[:, POOL_STATE + 1 - wdw:POOL_STATE + 1 - wdw + T, sl]
        cnt = jnp.minimum(n_avail, float(wdw))
        parts.append((hi[..., sl] - lo) / cnt[None, :, None])
    pooled = jnp.concatenate(parts, axis=-1) - ue[:, POOL_STATE:]
    pooled = pooled.reshape(B, T, POOL_GROUPS, POOL_GROUP_DIM).astype(u.dtype)
    y = jnp.einsum('btgc,gcd->btgd', pooled, w).reshape(B, T, POOL_WIDTH) * scale
    return y, ue[:, T:].astype(u.dtype)

def _hgrn_scan(q, g, k, i, s0):
    B, T, H, K = q.shape
    V = i.shape[-1]
    C = min(HGRN_CHUNK, T)
    n = -(-T // C)
    pad = n * C - T

    def chunks(a):
        a = jnp.pad(a, ((0, 0), (0, pad), (0, 0), (0, 0)))
        return a.reshape(B, n, C, H, a.shape[-1]).swapaxes(0, 1)

    causal = jnp.tril(jnp.ones((C, C), dtype=bool))[None, :, :, None, None]

    def step(s, inp):
        qc, gc, kc, ic = inp
        b = jnp.cumsum(gc, axis=1)
        diff = jnp.where(causal, b[:, :, None] - b[:, None, :], 0.0)
        rel = jnp.where(causal, jnp.exp(diff), 0.0)
        att = jnp.einsum('bthk,btshk,bshk->bhts', qc, rel, kc)
        o = jnp.einsum('bhts,bshv->bthv', att, ic) + jnp.einsum('bthk,bhkv->bthv', qc * jnp.exp(b), s)
        b_end = b[:, -1]
        s_new = jnp.exp(b_end)[..., None] * s + jnp.einsum('bshk,bshv->bhkv', kc * jnp.exp(b_end[:, None] - b), ic)
        return s_new, o

    s_fin, o = lax.scan(step, s0, (chunks(q), chunks(g), chunks(k), chunks(i)))
    o = o.swapaxes(0, 1).reshape(B, n * C, H, V)[:, :T]
    return o, s_fin

def _dsa(q, qi, wi, pos, k_all, v_all, ki_all, n_sel):
    B, T = q.shape[:2]
    L = k_all.shape[1]
    qb = Q_BLOCK if T % Q_BLOCK == 0 else T
    nb = T // qb
    kpos = jnp.arange(L, dtype=jnp.int32)
    bidx = jnp.arange(B)[:, None, None]

    def blocks(a):
        return a.reshape((B, nb, qb) + a.shape[2:]).swapaxes(0, 1)

    def one(args):
        q_b, qi_b, wi_b, pos_b = args
        allowed = kpos[None, :] <= pos_b[:, None]
        rel = jax.nn.relu(jnp.einsum('bqhd,bsd->bqhs', qi_b, ki_all).astype(jnp.float32))
        score = jnp.einsum('bqh,bqhs->bqs', wi_b.astype(jnp.float32), rel) * IDX_SCALE
        score = jnp.where(allowed[None], score, NEG_BIG)
        top_val, top_idx = lax.top_k(score, n_sel)
        valid = top_val > 0.5 * NEG_BIG
        kg = k_all[bidx, top_idx]
        vg = v_all[bidx, top_idx]
        qg = q_b.reshape(B, qb, N_KV_HEADS, GROUP, HEAD_DIM)
        logits = jnp.einsum('bqngd,bqknd->bqngk', qg, kg).astype(jnp.float32) * ATTN_SCALE
        logits = jnp.where(valid[:, :, None, None, :], logits, NEG_BIG)
        p = jax.nn.softmax(logits, axis=-1).astype(v_all.dtype)
        o = jnp.einsum('bqngk,bqknd->bqngd', p, vg)
        return o.reshape(B, qb, ATTN_WIDTH)

    out = lax.map(one, (blocks(q), blocks(qi), blocks(wi), pos.reshape(nb, qb)))
    return out.swapaxes(0, 1).reshape(B, T, ATTN_WIDTH)

def _trunk(x, c, pool_prev, hgrn_prev, past, p0, n_sel, P):
    B, T, _ = x.shape
    pos = p0 + jnp.arange(T, dtype=jnp.int32)
    lbs = _lower_bounds(P['hgrn_lb'])
    c_act = jax.nn.silu(c)
    ks, vs, kis, pools, states = [], [], [], [], []
    for l in range(DEPTH):
        mod = (c_act @ P['ada_w'][l] + P['ada_b'][l]).reshape(B, 1, 3 * N_SUB, D_MODEL)

        def pre(y, j):
            return _rmsnorm(y, P['norm_g'][l, j]) * (1 + mod[:, :, 3 * j + 1]) + mod[:, :, 3 * j]

        x = x + 0.5 * mod[:, :, 2] * _swiglu(pre(x, 0), P['ffn_wg'][l, 0], P['ffn_wu'][l, 0], P['ffn_wd'][l, 0])

        h = pre(x, 1)
        (u_pool, hq, hf, hi, hg, aq, ak, av, iq, ik, iw, gl) = _split_in(h @ P['w_in'][l])

        ya, pool_new = _pool_mix(u_pool, pool_prev[l], p0, P['pool_w'][l], P['pool_scale'][l])

        lb = lbs[l]
        f = lb + (1.0 - lb) * jax.nn.sigmoid(hf.astype(jnp.float32))
        f = f.reshape(B, T, HGRN_HEADS, HGRN_K)
        f_log = jnp.log(jnp.maximum(f, F_FLOOR))
        o_b, s_new = _hgrn_scan(hq.astype(jnp.float32).reshape(B, T, HGRN_HEADS, HGRN_K), f_log,
                                1.0 - f, hi.astype(jnp.float32).reshape(B, T, HGRN_HEADS, HGRN_V),
                                hgrn_prev[l].astype(jnp.float32))
        yb = (_rmsnorm(o_b.astype(x.dtype), P['hgrn_onorm'][l])
              * jax.nn.silu(hg.reshape(B, T, HGRN_HEADS, HGRN_V))).reshape(B, T, HGRN_I_WIDTH)

        q = _rope(_rmsnorm(aq.reshape(B, T, N_HEADS, HEAD_DIM), P['q_norm'][l]), pos)
        k = _rope(_rmsnorm(ak.reshape(B, T, N_KV_HEADS, HEAD_DIM), P['k_norm'][l]), pos)
        v = av.reshape(B, T, N_KV_HEADS, HEAD_DIM)
        qi = _rope(iq.reshape(B, T, IDX_HEADS, IDX_DIM), pos)
        ki = _rope(_rmsnorm(ik)[:, :, None, :], pos)[:, :, 0]
        if past is None:
            k_all, v_all, ki_all = k, v, ki
        else:
            cache_k, cache_v, cache_ki, page_table = past
            k_all = jnp.concatenate([_gather_pages(cache_k[l], page_table).astype(k.dtype), k], axis=1)
            v_all = jnp.concatenate([_gather_pages(cache_v[l], page_table).astype(v.dtype), v], axis=1)
            ki_all = jnp.concatenate([_gather_pages(cache_ki[l], page_table).astype(ki.dtype), ki], axis=1)
        yc = _dsa(q, qi, iw, pos, k_all, v_all, ki_all, n_sel)

        gate = jax.nn.sigmoid(gl).reshape(B, T, N_BRANCH, D_MODEL)
        merged = (gate[:, :, 0] * (ya @ P['w_ba'][l]) + gate[:, :, 1] * (yb @ P['w_bb'][l])
                  + gate[:, :, 2] * (yc @ P['w_bc'][l]))
        x = x + mod[:, :, 5] * (merged @ P['w_out'][l])

        x = x + 0.5 * mod[:, :, 8] * _swiglu(pre(x, 2), P['ffn_wg'][l, 1], P['ffn_wu'][l, 1], P['ffn_wd'][l, 1])

        ks.append(k)
        vs.append(v)
        kis.append(ki)
        pools.append(pool_new)
        states.append(s_new.astype(hgrn_prev.dtype))
    return x, jnp.stack(ks), jnp.stack(vs), jnp.stack(kis), jnp.stack(pools), jnp.stack(states)

def setup_inputs(seed: int = 0) -> dict:
    key = jax.random.key(seed)
    kk = jax.random.split(key, 32)
    n_pages = PAST_LEN // PAGE_SIZE
    n_used = DEC_BATCH * n_pages
    n_phys = n_used + n_used // 4

    def nrm(k, shape, scale=1.0):
        return jax.random.normal(k, shape, jnp.float32) * scale

    page_table = jax.random.permutation(kk[7], n_phys)[:n_used].reshape(DEC_BATCH, n_pages).astype(jnp.int32)
    return {
        'x_prompt': nrm(kk[0], (BATCH, SEQ, D_MODEL)),
        'x_sample': nrm(kk[1], (DEC_BATCH, DEC_SEQ, D_MODEL)),
        'c_prompt': nrm(kk[2], (BATCH, D_MODEL)),
        'c_sample': nrm(kk[3], (DEC_BATCH, D_MODEL)),
        'cache_k': nrm(kk[4], (DEPTH, n_phys, PAGE_SIZE, N_KV_HEADS, HEAD_DIM)),
        'cache_v': nrm(kk[5], (DEPTH, n_phys, PAGE_SIZE, N_KV_HEADS, HEAD_DIM)),
        'cache_ki': nrm(kk[6], (DEPTH, n_phys, PAGE_SIZE, IDX_DIM)),
        'page_table': page_table,
        'state_pool': nrm(kk[8], (DEPTH, DEC_BATCH, POOL_STATE, POOL_WIDTH)),
        'state_hgrn': nrm(kk[9], (DEPTH, DEC_BATCH, HGRN_HEADS, HGRN_K, HGRN_V), 0.5),
        'ada_w': nrm(kk[10], (DEPTH, D_MODEL, 3 * N_SUB * D_MODEL), D_MODEL ** -0.5),
        'ada_b': nrm(kk[11], (DEPTH, 3 * N_SUB * D_MODEL), 0.02),
        'norm_g': 1.0 + nrm(kk[12], (DEPTH, N_SUB, D_MODEL), 0.02),
        'ffn_wg': nrm(kk[13], (DEPTH, 2, D_MODEL, D_FF), D_MODEL ** -0.5),
        'ffn_wu': nrm(kk[14], (DEPTH, 2, D_MODEL, D_FF), D_MODEL ** -0.5),
        'ffn_wd': nrm(kk[15], (DEPTH, 2, D_FF, D_MODEL), D_FF ** -0.5),
        'w_in': nrm(kk[16], (DEPTH, D_MODEL, IN_WIDTH), D_MODEL ** -0.5),
        'pool_w': nrm(kk[17], (DEPTH, POOL_GROUPS, POOL_GROUP_DIM, POOL_GROUP_DIM), POOL_GROUP_DIM ** -0.5),
        'pool_scale': 1.0 + nrm(kk[18], (DEPTH, POOL_WIDTH), 0.02),
        'hgrn_lb': nrm(kk[19], (DEPTH, HGRN_F_WIDTH)),
        'hgrn_onorm': 1.0 + nrm(kk[20], (DEPTH, HGRN_V), 0.02),
        'q_norm': 1.0 + nrm(kk[21], (DEPTH, HEAD_DIM), 0.02),
        'k_norm': 1.0 + nrm(kk[22], (DEPTH, HEAD_DIM), 0.02),
        'w_ba': nrm(kk[23], (DEPTH, POOL_WIDTH, D_MODEL), POOL_WIDTH ** -0.5),
        'w_bb': nrm(kk[24], (DEPTH, HGRN_I_WIDTH, D_MODEL), HGRN_I_WIDTH ** -0.5),
        'w_bc': nrm(kk[25], (DEPTH, ATTN_WIDTH, D_MODEL), ATTN_WIDTH ** -0.5),
        'w_out': nrm(kk[26], (DEPTH, D_MODEL, D_MODEL), D_MODEL ** -0.5),
    }

def reference(x_prompt, x_sample, c_prompt, c_sample, cache_k, cache_v, cache_ki, page_table,
              state_pool, state_hgrn, ada_w, ada_b, norm_g, ffn_wg, ffn_wu, ffn_wd, w_in,
              pool_w, pool_scale, hgrn_lb, hgrn_onorm, q_norm, k_norm, w_ba, w_bb, w_bc, w_out):
    P = {'ada_w': ada_w, 'ada_b': ada_b, 'norm_g': norm_g, 'ffn_wg': ffn_wg, 'ffn_wu': ffn_wu,
         'ffn_wd': ffn_wd, 'w_in': w_in, 'pool_w': pool_w, 'pool_scale': pool_scale,
         'hgrn_lb': hgrn_lb, 'hgrn_onorm': hgrn_onorm, 'q_norm': q_norm, 'k_norm': k_norm,
         'w_ba': w_ba, 'w_bb': w_bb, 'w_bc': w_bc, 'w_out': w_out}
    b_p, seq = x_prompt.shape[0], x_prompt.shape[1]
    pool0 = jnp.zeros((DEPTH, b_p, POOL_STATE, POOL_WIDTH), x_prompt.dtype)
    hgrn0 = jnp.zeros((DEPTH, b_p, HGRN_HEADS, HGRN_K, HGRN_V), state_hgrn.dtype)
    y_prompt, k_p, v_p, ki_p, pool_p, hgrn_p = _trunk(
        x_prompt, c_prompt, pool0, hgrn0, None, 0, min(TOPK_MAX, seq // 4), P)
    l_vis = PAST_LEN + x_sample.shape[1]
    y_sample, k_s, v_s, ki_s, pool_s, hgrn_s = _trunk(
        x_sample, c_sample, state_pool, state_hgrn, (cache_k, cache_v, cache_ki, page_table),
        PAST_LEN, min(TOPK_MAX, l_vis // 4), P)
    return (y_prompt, y_sample, k_p, v_p, ki_p, pool_p, hgrn_p, k_s, v_s, ki_s, pool_s, hgrn_s)


_drawn_inputs = setup_inputs


def setup_inputs(seed=0):
    import zlib

    import numpy as np

    out = dict(_drawn_inputs(seed))
    spreads = {}
    factors = {'pool_scale': 6.278, 'hgrn_onorm': 7.759, 'q_norm': 24.776, 'k_norm': 10.147}
    for name, (base, spread) in spreads.items():
        noise = np.random.default_rng([zlib.crc32(name.encode()), seed]).standard_normal(out[name].shape)
        drawn = base * np.exp(spread * noise) if base else spread * noise
        out[name] = jnp.asarray(drawn.astype(out[name].dtype))
    for name, factor in factors.items():
        out[name] = (out[name] * factor).astype(out[name].dtype)
    return out
```

```python
import numpy as np
import concourse.bass as bass
from concourse import mybir
from contextlib import ExitStack

F32 = mybir.dt.float32
F32R = mybir.dt.float32r
U32 = mybir.dt.uint32
I32 = mybir.dt.int32
ACT = mybir.ActivationFunctionType
ALU = mybir.AluOpType
AX = mybir.AxisListType

P = 128
DEPTH = 2
D_MODEL = 1024
KT = D_MODEL // P
SEQ = 512
NB = 8
COLS = SEQ + NB
HALF = COLS // 2
TT = SEQ // P
D_FF = 2816
UP = (12, 10)
assert sum(UP) * P == D_FF
N_SUB = 3
POOL_WINDOWS = (2, 4, 8, 16)
POOL_G = 64
POOL_STATE = 15
HH, HK, HV = 4, 128, 64
HIW = HH * HV
NH, NKV, HD = 8, 2, 64
IDXH = 4
PAST = 256
PAGES = 2
LVIS = PAST + 1
TOP_PROMPT = 128
TOP_SAMPLE = LVIS // 4
ROPE_THETA = 10000.0
ATTN_SCALE = HD ** -0.5
IDX_SCALE = (HD * IDXH) ** -0.5
NEG_BIG = -1e30
TAKEN = -3e38
EPS = 1e-6
F_FLOOR = 1e-30
PRIMED = 1
SLOT = 2048
ROT = 15
CC = 1 + NB

SEGMENTS = []
for _f in (0, 1):
    _ffn = []
    for _h, _n in enumerate(UP):
        _ffn += [(f"up{_f}{_h}", _n, SLOT), (f"down{_f}{_h}", KT, _n * P)]
    SEGMENTS += _ffn
    if _f == 0:
        SEGMENTS += [("token", 8, SLOT), ("hgrn", 4, SLOT), ("merge", 16, SLOT), ("out", 4, SLOT)]
SLOT0, _at = {}, 0
for _name, _n, _ in SEGMENTS:
    SLOT0[_name] = _at
    _at += _n
LAYER_SLOTS = _at
USED = {name: used for name, _, used in SEGMENTS}
ADA_SLOTS = 12

MAIN0, _at = {}, 0
for _name, _n in [("up00", 4 * UP[0]), ("down00", 2 * KT), ("up01", 4 * UP[1]), ("down01", 2 * KT),
                  ("token", 24), ("hgrn", 16), ("merge", 96), ("out", 16),
                  ("up10", 4 * UP[0]), ("down10", 2 * KT), ("up11", 4 * UP[1]), ("down11", 2 * KT)]:
    assert _at % 4 == 0
    MAIN0[_name] = _at
    _at += _n
LAYER_MAIN = _at


def slot_end(stage, s):
    if stage == "merge":
        return 24 * (s // 4) + (4, 8, 12, 24)[s % 4]
    return (s + 1) * {"do": 2, "to": 3}.get(stage[:2], 4)


LEVELS = (0, 1, 2, 4, 8, 16, 32, 64)


INDEX_USES = IDXH * TT
PAIRS = HH * (len(LEVELS) + 1)
Y_HEADS = 4 + 3 + TT
STORES = 8
X_TILES = 5 * KT


def x_updates(sub):
    return X_TILES * (sub // N_SUB) + (0, 2 * KT, 3 * KT)[sub % N_SUB]


def side_order():
    keys = []
    for l in range(DEPTH):
        keys += [(l, "norm", 0, h) for h in (0, 1)] + [(l, "norm", 1, h) for h in (0, 1)]
        keys += [(l, "pooled", c) for c in (0, 1, 2)]
        keys += [(l, "ya", c, h) for c in (0, 1) for h in (0, 1)]
        keys += [(l, "rotT", t, part) for t in range(TT + 1) for part in (0, 1)]
        for hd in range(HH):
            keys += [(l, "level", hd, lv) for lv in LEVELS]
            keys += [(l, "kbT", hd), (l, "delta", hd), (l, "o", hd)]
        keys += [(l, "i_bcast", j) for j in range(4)] + [(l, "o_sample",)]
        keys += [(l, "ybT", c) for c in (0, 1, 2)]
        keys += [(l, "index", 0, h) for h in range(IDXH)]
        for t in range(TT):
            if t + 1 < TT:
                keys += [(l, "index", t + 1, h) for h in range(IDXH)]
            for kind, h in attention_order():
                keys.append((l, kind, t, h))
            keys.append((l, "ycT", t))
        keys += [(l, "kT_page", j) for j in range(4)] + [(l, "kiT_page", j) for j in range(2)]
        keys += [(l, "s_index",), (l, "s_wsel",), (l, "s_score",), (l, "s_logits",)]
        keys += [(l, "s_probT",), (l, "s_o",), (l, "s_oT",)]
        keys += [(l, "norm", 2, h) for h in (0, 1)]
    return keys


def attention_order():
    order = []
    for h in range(NH + 2):
        if h < NH:
            order.append(("logits", h))
        if 1 <= h <= NH:
            order.append(("probT", h - 1))
        if h >= 3 and h % 2 == 1:
            order.append(("pv", (h - 3) // 2))
    return order


SIDE = {key: n for n, key in enumerate(side_order())}


def constants():
    c = {}
    c["ident"] = np.eye(P, dtype=np.float32)
    s = np.arange(P)[:, None]
    t = np.arange(P)[None, :]
    levels = [(s == t)]
    for h in LEVELS[1:]:
        levels.append((s // (2 * h) == t // (2 * h)) & (s // h % 2 == 0) & (t // h % 2 == 1))
    c["levels"] = np.stack([m.astype(np.float32) for m in levels], 1)
    c["causal"] = np.concatenate([np.zeros((P, 3 * P)), np.where(t <= s, 0.0, NEG_BIG)], 1).astype(np.float32)
    win = np.zeros((P, 3, 4, P), np.float32)
    for g, w in enumerate(POOL_WINDOWS):
        inside = (s <= t) & (s > t - w)
        win[:, 0, g] = inside / np.float32(w) - (s == t)
        win[:, 1, g] = inside / np.minimum(t + 1, w).astype(np.float32) - (s == t)
        win[:, 2, g] = (s - P > t - w) / np.float32(w)
    c["windows"] = win
    past = np.zeros((NB, POOL_STATE, 4, NB), np.float32)
    own = np.zeros((NB, 4, NB), np.float32)
    for g, w in enumerate(POOL_WINDOWS):
        for b in range(NB):
            past[b, POOL_STATE - (w - 1):, g, b] = 1.0 / w
            own[b, g, b] = 1.0 / w - 1.0
    c["windows_past"] = past.reshape(NB * POOL_STATE, 4, NB)
    c["windows_own"] = own
    half = HD // 2
    inv = np.power(np.float32(ROPE_THETA), -np.arange(half, dtype=np.float32) / np.float32(half)).astype(np.float32)
    pos = np.concatenate([np.arange(SEQ), np.full(P, PAST)]).astype(np.float32)
    ang = (pos[:, None] * inv[None, :]).astype(np.float32)
    cos, sin = np.cos(ang), np.sin(ang)
    rope = np.stack([np.concatenate([cos, cos], 1), np.concatenate([-sin, sin], 1)], 1)
    c["rope"] = rope.reshape(TT + 1, P, 2, HD).transpose(1, 0, 2, 3).astype(np.float32)
    row = np.zeros((NB, NB, P), np.float32)
    row[np.arange(NB), np.arange(NB)] = 1.0
    c["row_select"] = row
    col = np.zeros((P, 2 * NB - 1), np.float32)
    col[:, NB - 1] = 1.0
    c["col_select"] = col
    c["spread_idx"] = np.repeat(np.eye(NB, dtype=np.float32), IDXH, 1)
    c["spread_heads"] = np.repeat(np.eye(NB, dtype=np.float32), NH, 1)
    c["gather_heads"] = np.ascontiguousarray(c["spread_heads"].T)
    return {k: np.ascontiguousarray(v, dtype=np.float32) for k, v in c.items()}


def build(nc, d):
    ctx = ExitStack()
    with ctx:
        cursor = [16512]

        def sb(name, shape, dt=F32, at=None):
            size = 4 * int(np.prod(shape[1:]))
            if at is None:
                at = cursor[0]
                cursor[0] += -(-size // 32) * 32
            assert at + size <= 229368, (name, at + size)
            return nc.alloc_sbuf_tensor_at(name, list(shape), dt, offset=at)

        x = sb("x", [P, KT, COLS])
        h_hi = sb("h_hi", [P, KT, SEQ + P], F32R)
        h_lo = sb("h_lo", [P, KT, SEQ + P], F32R)
        raw = [sb(f"raw{j}", [P, SLOT]) for j in range(2)]
        w_hi = [sb(f"w_hi{j}", [P, SLOT], F32R) for j in range(2)]
        w_lo = [sb(f"w_lo{j}", [P, SLOT], F32R) for j in range(2)]
        ada_w = [sb(f"ada_w{j}", [P, 2, KT, P]) for j in range(2)]
        mod = [sb(f"mod{j}", [P, 24, CC]) for j in range(2)]
        ada_b = sb("ada_b", [P, DEPTH * N_SUB, 24])
        norm_g = sb("norm_g", [P, DEPTH * N_SUB, KT])
        cond = sb("cond", [P, KT, CC])
        ident = sb("ident", [P, P])
        ones = sb("ones", [P, P])
        lb = sb("lb", [P, DEPTH, HH])
        lb_rest = sb("lb_rest", [P, DEPTH, HH])
        lb_tmp = sb("lb_tmp", [P, 4, HH])
        onorm = sb("onorm", [P, DEPTH, HV])
        pool_scale = sb("pool_scale", [P, DEPTH, 2])
        col_select = sb("col_select", [P, 2 * NB - 1])
        spread_idx = sb("spread_idx", [NB, NB, IDXH])
        spread_heads = sb("spread_heads", [NB, NB * NH])
        gather_heads = sb("gather_heads", [NB * NH, NB])
        page_ids = sb("page_ids", [1, NB * PAGES], I32)
        x_tmp = sb("x_tmp", [P, NB])
        base = cursor[0]

        def area(name, shape, at, dt=F32):
            return sb(name, shape, dt, base + at)

        mid_hi = area("mid_hi", [P, UP[0], COLS], 0, F32R)
        mid_lo = area("mid_lo", [P, UP[0], COLS], 24960, F32R)
        silu_g = area("silu_g", [P, 2, HALF], 49920)
        prod = area("prod", [P, 2, HALF], 52000)
        sq = area("sq", [P, KT, COLS], 0)
        scaled = area("scaled", [P, KT, SEQ], 16640)
        ms = area("ms", [P, COLS], 33024)
        root = area("root", [P, COLS], 35104)
        newton = area("newton", [P, COLS], 37184)
        rstd = area("rstd", [P, COLS], 39264)
        h_s = area("h_s", [P, KT, NB], 41344)
        yab_hi = area("yab_hi", [P, 4, COLS], 0, F32R)
        yab_lo = area("yab_lo", [P, 4, COLS], 8320, F32R)
        yc_hi = area("yc_hi", [P, 4, COLS], 16640, F32R)
        yc_lo = area("yc_lo", [P, 4, COLS], 24960, F32R)
        gamma = area("gamma", [P, ROT, HD], 4160)
        rope = area("rope", [P, TT + 1, 2, HD], 12480)
        rot = area("rot", [P, TT + 1, ROT, HD], 16640)
        vals = area("vals", [P, TT + 1, NKV * HD], 35840)
        wi = area("wi", [P, TT + 1, IDXH], 38400)
        rotT = area("rotT", [P, 8, COLS], 38528)
        h_i = area("h_i", [P, TT + 1, HIW], 55168)
        h_g = area("h_g", [P, TT + 1, HIW], 60288)
        pool_u = area("pool_u", [P, TT + 1, 256], 65408)
        windows = area("windows", [P, 3, 4, P], 70528)
        pooled = area("pooled", [P, 2, COLS], 76672)
        pool_past = area("pool_past", [NB * POOL_STATE, 256], 80832)
        pool_w = area("pool_w", [P, 2, P], 81856)
        windows_past = area("windows_past", [NB * POOL_STATE, 4, NB], 82880)
        windows_own = area("windows_own", [NB, 4, NB], 83008)
        rot_a = area("rot_a", [P, ROT, HD], 65408)
        rot_b = area("rot_b", [P, ROT, HD], 69248)
        rot_ms = area("rot_ms", [P, 4, TT + 1, ROT], 83200)
        hq = area("hq", [P, COLS], 16640)
        hf = area("hf", [P, COLS], 18720)
        hk = area("hk", [P, COLS], 20800)
        pre = area("pre", [P, SEQ], 22880)
        suf = area("suf", [P, SEQ], 24928)
        att = area("att", [P, TT, P], 26976)
        kbT = area("kbT", [P, TT, P], 29024)
        chain = area("chain", [P, TT, HV], 31072)
        qm = [area(f"qm{j}", [P, SEQ], 65408 + 2048 * j) for j in range(2)]
        km = [area(f"km{j}", [P, SEQ], 69504 + 2048 * j) for j in range(2)]
        h_o = area("h_o", [P, TT + 1, HH, HV], 73600)
        levels = area("levels", [P, len(LEVELS), P], 78720)
        f_s = area("f_s", [P, HH, NB], 82816)
        k_s = area("k_s", [P, HH, NB], 82944)
        q_s = area("q_s", [P, HH, NB], 83072)
        state_p = area("state_p", [P, HH, HV], 83200)
        state_in = area("state_in", [P, NB, HH, HV], 16640)
        state_s = area("state_s", [P, NB, HH, HV], 24832)
        state_q = area("state_q", [P, NB, HH, HV], 65408)
        row_select = area("row_select", [NB, NB, P], 78720)
        o_sq = area("o_sq", [P, TT + 1, HH, HV], 65408)
        o_ms = area("o_ms", [P, 4, TT + 1, HH], 82816)
        rel = [area(f"rel{j}", [P, SEQ], 55168 + 2048 * j) for j in range(2)]
        score = area("score", [P, SEQ], 59264)
        work = area("work", [P, SEQ], 61312)
        mask = [area(f"mask{j}", [P, SEQ], 63360 + 2048 * j) for j in range(2)]
        probs = [area(f"probs{j}", [P, SEQ], 67456 + 2048 * j) for j in range(2)]
        probT = [area(f"probT{j}", [P, TT, P], 71552 + 2048 * j) for j in range(4)]
        o_tok = area("o_tok", [P, NH, HD], 79744)
        causal = area("causal", [P, SEQ], 81792)
        top8 = area("top8", [P, 8], 83840)
        row_max = area("row_max", [P, NH], 83872)
        neg_max = area("neg_max", [P, NH], 83904)
        row_sum = area("row_sum", [P, NH], 83936)
        row_inv = area("row_inv", [P, NH], 83968)
        k_page = area("k_page", [P, NB, PAGES, P], 38528)
        v_page = area("v_page", [P, NB, PAGES, P], 46720)
        ki_page = area("ki_page", [P, NB, PAGES, HD], 55168)
        kT_s = area("kT_s", [P, NB, LVIS], 59264)
        kiT_s = area("kiT_s", [HD, NB, LVIS], 67488)
        q_blk = area("q_blk", [P, NB, NB, NKV, 4], 75712)
        qi_blk = area("qi_blk", [HD, NB, NB, IDXH], 77760)
        prob_s = area("prob_s", [NB * NH, LVIS], 78784)
        rel_s = area("rel_s", [NB * IDXH, LVIS], 78784)
        score_s = area("score_s", [NB, LVIS], 79840)
        work_s = area("work_s", [NB, LVIS], 80896)
        mask_s = area("mask_s", [NB, LVIS], 81952)
        probT_blk = area("probT_blk", [P, PAGES, NB, NB * NH], 79840)
        rotT_s = area("rotT_s", [P, 8, NB], 83936)
        top8_s = area("top8_s", [NB, 8], 84192)
        st_s = area("st_s", [NB * NH, 4], 84224)
        wi_exp = area("wi_exp", [NB, NB, IDXH], 83008)
        wi_sel = area("wi_sel", [NB * IDXH, NB], 84256)
        own_diag = area("own_diag", [NB * NH, NB * NH], 75712)
        own_prob = area("own_prob", [NB, NB * NH], 75968)
        o_s = area("o_s", [NB * NH, P], 76224)
        mrg_hi = area("mrg_hi", [P, KT, COLS], 33280, F32R)
        mrg_lo = area("mrg_lo", [P, KT, COLS], 49920, F32R)
        gate_s = area("gate_s", [P, 6, COLS], 66560)
        part = area("part", [P, 3, HALF], 79040)

        bank = [ctx.enter_context(nc.psum_tensor(f"bank{b}", [P, 512], F32)) for b in range(8)]
        ada_bank = bank[7]

        def sem(name):
            return ctx.enter_context(nc.semaphore(name))

        const_loaded = sem("const_loaded")
        x_loaded = sem("x_loaded")
        w_loaded = [sem(f"w_loaded{j}") for j in range(2)]
        head_split = [sem(f"head_split{j}") for j in range(2)]
        w_split = [sem(f"w_split{j}") for j in range(2)]
        ada_loaded = [sem(f"ada_loaded{j}") for j in range(2)]
        ada_used = [sem(f"ada_used{j}") for j in range(2)]
        ada_taken = sem("ada_taken")
        slots_seen = sem("slots_seen")
        main_full = sem("main_full")
        main_taken = [sem(f"main_taken{b}") for b in range(4)]
        side_full = sem("side_full")
        side_taken = [sem(f"side_taken{b}") for b in range(3)]
        setup_done = sem("setup_done")
        cond_ready = sem("cond_ready")
        lb_exp = sem("lb_exp")
        x_updated = sem("x_updated")
        squared = sem("squared")
        root_ready = sem("root_ready")
        ms_ready = sem("ms_ready")
        scaled_ready = sem("scaled_ready")
        h_hi_ready = sem("h_hi_ready")
        h_lo_ready = sem("h_lo_ready")
        mid_hi_ready = sem("mid_hi_ready")
        mid_lo_ready = sem("mid_lo_ready")
        pool_loaded = sem("pool_loaded")
        rope_loaded = sem("rope_loaded")
        rotated = sem("rotated")
        stored = sem("stored")
        y_hi_ready = sem("y_hi_ready")
        levels_loaded = sem("levels_loaded")
        pair_ready = sem("pair_ready")
        chain_ready = sem("chain_ready")
        state_loaded = sem("state_loaded")
        state_ready = sem("state_ready")
        state_q_ready = sem("state_q_ready")
        yb_ready = sem("yb_ready")
        index_used = sem("index_used")
        causal_loaded = sem("causal_loaded")
        neg_max_ready = sem("neg_max_ready")
        probs_ready = sem("probs_ready")
        o_tok_ready = sem("o_tok_ready")
        rotT_copied = sem("rotT_copied")
        pages_loaded = sem("pages_loaded")
        q_blk_ready = sem("q_blk_ready")
        wi_exp_ready = sem("wi_exp_ready")
        mask_s_ready = sem("mask_s_ready")
        s_neg_ready = sem("s_neg_ready")
        s_probs_ready = sem("s_probs_ready")
        own_diag_ready = sem("own_diag_ready")
        blk_ready = sem("blk_ready")
        mrg_ready = sem("mrg_ready")
        mrg_hi_ready = sem("mrg_hi_ready")
        mrg_lo_ready = sem("mrg_lo_ready")
        vector_step = sem("vector_step")
        scalar_step = sem("scalar_step")
        table_ids = sem("table_ids")

        primed = main_taken + w_split + ada_used + [ada_taken, mrg_ready]

        def main_unit(l, stage, n=0):
            return LAYER_MAIN * l + MAIN0[stage] + n

        def side_unit(*key):
            n = SIDE[key]
            return n, n % 3, n // 3

        def wait_main(eng, unit):
            eng.wait_ge(main_full, unit + 1)

        def wait_side(eng, *key):
            n, b, _ = side_unit(*key)
            eng.wait_ge(side_full, n + 1)
            return bank[4 + b], side_taken[b]

        def wait_side_taken(eng, *key):
            n, b, use = side_unit(*key)
            eng.wait_ge(side_taken[b], use + 1)

        def main_use(l, stage, r=0):
            return (LAYER_MAIN * l + MAIN0[stage]) // 4 + r

        def slot_use(l, stage, r=0):
            return (LAYER_SLOTS * l + SLOT0[stage]) // 2 + r

        class Chain:

            def __init__(self, eng, semaphore):
                self.eng, self.sem, self.n, self.extra = eng, semaphore, 0, 0

            def link(self, ins):
                ins.then_inc(self.sem, 1)
                self.n += 1
                self.eng.wait_ge(self.sem, self.n + self.extra)

            def loop(self, i, per, count):
                self.extra = i * per
                self.per, self.count, self.start = per, count, self.n

            def end(self):
                assert self.n - self.start == self.per, (self.n - self.start, self.per)
                self.n = self.start + self.per * self.count
                self.extra = 0

        def half(hf):
            return slice(hf * HALF, (hf + 1) * HALF)

        def newton_rsqrt(chain_, mean, rt, tmp, out):
            v = nc.vector
            chain_.link(v.reciprocal(rt, rt))
            chain_.link(v.tensor_tensor(tmp, rt, rt, ALU.mult))
            chain_.link(v.scalar_tensor_tensor(out=tmp, in0=tmp, scalar=-0.5, in1=mean, op0=ALU.mult, op1=ALU.mult))
            chain_.link(v.scalar_tensor_tensor(out=out, in0=tmp, scalar=1.5, in1=rt, op0=ALU.add, op1=ALU.mult))

        block = ctx.enter_context(nc.Block())

        @block.sync
        def _(sp):
            sp.dma_start(cond[:], d["cond"]).then_inc(const_loaded, 16)
            for k in range(2):
                sp.dma_start(x[:, 4 * k:4 * k + 4, :], d["x"][:, 4 * k:4 * k + 4, :]).then_inc(x_loaded, 16)
            for name, tile in (("ada_b", ada_b), ("norm_g", norm_g), ("ident", ident), ("hgrn_lb", lb),
                               ("pool_scale", pool_scale), ("col_select", col_select),
                               ("spread_idx", spread_idx), ("spread_heads", spread_heads),
                               ("gather_heads", gather_heads), ("page_table", page_ids)):
                src = d[name]
                if name == "spread_idx":
                    src = src.rearrange("b (c h) -> b c h", h=IDXH)
                sp.dma_start(tile[:], src).then_inc(const_loaded, 16)
            sp.dma_start(onorm[:], d["hgrn_onorm"].partition_broadcast(P)).then_inc(const_loaded, 16)

            def load_ada(sub, r, j):
                use = sub * (ADA_SLOTS // 2) + r
                sp.wait_ge(ada_used[j], use + PRIMED)
                sp.dma_start(ada_w[j][:].rearrange("p a k n -> p (a k n)"),
                             d["ada"][bass.ds(sub * ADA_SLOTS + 2 * r + j, 1)].rearrange("o p n -> p (o n)"))\
                  .then_inc(ada_loaded[j], 16)

            def load_w(l, stage, r, j):
                use = slot_use(l, stage, r)
                sp.wait_ge(w_split[j], use + PRIMED)
                n = USED[stage]
                sp.dma_start(raw[j][:, 0:n],
                             d["w"][bass.ds(l * LAYER_SLOTS + SLOT0[stage] + 2 * r + j, 1), :, 0:n]
                             .rearrange("o p n -> p (o n)")).then_inc(w_loaded[j], 16)

            with sp.Fori(0, ADA_SLOTS // 2) as r:
                for j in range(2):
                    load_ada(0, r, j)
            for l in range(DEPTH):
                for stage, slots, _ in SEGMENTS:
                    ada = None
                    if stage == "up00":
                        ada = N_SUB * l + 1
                    elif stage == "up10" and l + 1 < DEPTH:
                        ada = N_SUB * (l + 1)
                    if stage == "merge":
                        with sp.Fori(0, ADA_SLOTS // 2) as r:
                            for j in range(2):
                                load_ada(N_SUB * l + 2, r, j)
                    with sp.Fori(0, slots // 2) as r:
                        for j in range(2):
                            load_w(l, stage, r, j)
                            if ada is not None:
                                load_ada(ada, r, j)
            sp.wait_ge(x_updated, x_updates(DEPTH * N_SUB))
            for k in range(2):
                sp.dma_start(d["y"][:, 4 * k:4 * k + 4, :], x[:, 4 * k:4 * k + 4, :]).then_inc(stored, 16)
            sp.wait_ge(stored, 16 * (2 + DEPTH * STORES))

        @block.gpsimd
        def _(pool):
            for semaphore in primed:
                pool.sem_inc(semaphore, PRIMED)
            pool.memset(ones[:], 1.0).then_inc(setup_done, 1)
            pool.memset(h_hi[:, :, COLS:].bitcast(F32), 0.0).then_inc(setup_done, 1)
            pool.memset(h_lo[:, :, COLS:].bitcast(F32), 0.0).then_inc(setup_done, 1)

            def split(j, use, n, filled):
                pool.wait_ge(w_loaded[j], 16 * use + 16)
                if filled is not None:
                    pool.wait_ge(main_full, filled)
                pool.sem_inc(slots_seen, 1)
                pool.tensor_copy(w_hi[j][:, 0:n], raw[j][:, 0:n]).then_inc(head_split[j], 1)
                pool.wait_ge(head_split[j], use + 1)
                pool.tensor_tensor(w_lo[j][:, 0:n], raw[j][:, 0:n], w_hi[j][:, 0:n].bitcast(F32),
                                   ALU.subtract).then_inc(w_split[j], 1)

            before = [None, None]
            for l in range(DEPTH):
                for stage, slots, n in SEGMENTS:
                    first = LAYER_MAIN * l + MAIN0[stage]
                    body = 4 if stage == "merge" else 2
                    for s in range(body):
                        split(s % 2, slot_use(l, stage, s // 2), n, before[s] if s < 2 else first + slot_end(stage, s - 2))
                    per = slot_end(stage, body - 1)
                    with pool.Fori(1, slots // body) as r:
                        for s in range(body):
                            split(s % 2, slot_use(l, stage, r * (body // 2) + s // 2), n,
                                  first + per * r + slot_end(stage, s - 2))
                    before = [first + slot_end(stage, slots - 2), first + slot_end(stage, slots - 1)]

        @block.scalar
        def _(act):
            steps = Chain(act, scalar_step)
            s = nc.scalar
            load_sp = act.dma_start

            act.wait_ge(const_loaded, 16 * 12)
            s.activation(cond[:], cond[:], ACT.Silu).then_inc(cond_ready, 1)
            act.wait_ge(lb_exp, 1)
            s.activation(lb_tmp[:, 0:2, :], lb_tmp[:, 0:2, :], ACT.Exp).then_inc(lb_exp, 1)

            def ffn_up(l, stage, count0, tiles):
                with act.Fori(0, tiles // 2) as r:
                    for j in range(2):
                        for hf in range(2):
                            use = main_use(l, stage, 2 * r + j)
                            wait_main(act, main_unit(l, stage, 8 * r + 4 * j + 2 * hf))
                            act.wait_ge(main_taken[2 * hf + 1], use + PRIMED)
                            s.activation(silu_g[:, hf, :], bank[2 * hf][:, 0:HALF], ACT.Silu)\
                             .then_inc(main_taken[2 * hf], 1)
                            act.wait_ge(main_taken[2 * hf + 1], use + 1 + PRIMED)
                            s.copy(mid_hi[:, bass.ds(2 * r + j, 1), half(hf)].rearrange("p o n -> p (o n)"),
                                   prod[:, hf, :]).then_inc(mid_hi_ready, 1)

            def norm(sub):
                l, j3 = divmod(sub, N_SUB)
                md = mod[sub % 2]
                if sub == 0:
                    act.wait_ge(x_loaded, 32)
                else:
                    act.wait_ge(x_updated, x_updates(sub))
                for k in range(KT):
                    s.activation(sq[:, k, :], x[:, k, :], ACT.Square).then_inc(squared, 1)
                wait_side_taken(act, l, "norm", j3, 0)
                wait_side_taken(act, l, "norm", j3, 1)
                s.activation(root[:], ms[:], ACT.Sqrt).then_inc(root_ready, 1)
                roots[0] += 1
                if j3 == 1:
                    mixer_loads(l)
                act.wait_ge(scaled_ready, 9 * sub + 1)
                s.copy(h_hi[:, :, SEQ:COLS], h_s[:]).then_inc(h_hi_ready, 1)
                for k in range(KT):
                    act.wait_ge(scaled_ready, 9 * sub + 2 + k)
                    s.activation(h_hi[:, k, 0:SEQ], scaled[:, k, :], ACT.Identity,
                                 bias=md[:, k, 0:1]).then_inc(h_hi_ready, 1)

            roots = [0]

            def mixer_loads(l):
                for dst, src in ((windows[:], d["windows"]), (pool_past[:], d["state_pool"][l]),
                                 (pool_w[:], d["pool_w"][l]), (windows_past[:], d["windows_past"]),
                                 (windows_own[:], d["windows_own"])):
                    load_sp(dst, src).then_inc(pool_loaded, 16)
                load_sp(gamma[:], d["gamma"][l].partition_broadcast(P)).then_inc(rope_loaded, 16)
                load_sp(rope[:], d["rope"]).then_inc(rope_loaded, 16)

            def token_major(l):
                heads = {3: slice(0, 8, 2), 4: slice(1, 8, 2), 6: slice(10, 14)}
                for slot in range(8):
                    for u in range(3):
                        n = 3 * slot + u
                        unit = main_unit(l, "token", n)
                        wait_main(act, unit)
                        tl = slice(2 * u, 2 * u + 2) if u < 2 else slice(TT, TT + 1)
                        nt = 2 if u < 2 else 1
                        src = bank[unit % 4][:, 0:256 * nt].rearrange("p (t n) -> p t n", t=nt)
                        done = main_taken[unit % 4]
                        if slot == 0:
                            s.copy(pool_u[:, tl, :], src).then_inc(done, 1)
                        elif slot == 1:
                            s.copy(h_i[:, tl, :], src).then_inc(done, 1)
                        elif slot == 2:
                            s.activation(h_g[:, tl, :], src, ACT.Silu).then_inc(done, 1)
                        elif slot in heads:
                            s.copy(rot[:, tl, heads[slot], :], src.rearrange("p t (h n) -> p t h n", n=HD)).then_inc(done, 1)
                        elif slot == 5:
                            s.copy(rot[:, tl, 8:10, :].rearrange("p t h n -> p t (h n)"), src[:, :, 0:P])
                            s.copy(vals[:, tl, :], src[:, :, P:2 * P]).then_inc(done, 1)
                        else:
                            s.copy(rot[:, tl, 14, :], src[:, :, 0:HD])
                            s.copy(wi[:, tl, :], src[:, :, HD:HD + IDXH]).then_inc(done, 1)

            def last_token_unit(eng, l, n=23):
                unit = main_unit(l, "token", n)
                eng.wait_ge(main_taken[unit % 4], unit // 4 + 1 + PRIMED)

            def pool_branch(l):
                last_token_unit(act, l, 2)
                act.dma_start(d["pool_p"][l], pool_u[P - POOL_STATE:P, TT - 1, :]).then_inc(stored, 16)
                act.dma_start(d["pool_s"][l, :, POOL_STATE - 1, :], pool_u[0:NB, TT, :]).then_inc(stored, 16)
                act.dma_start(d["pool_s"][l, :, 0:POOL_STATE - 1, :],
                              d["state_pool"][l].rearrange("(b j) c -> b j c", j=POOL_STATE)[:, 1:, :])\
                   .then_inc(stored, 16)
                for c in range(2):
                    src, done = wait_side(act, l, "pooled", c)
                    s.copy(pooled[:, c, 0:SEQ], src[:, :]).then_inc(done, 1)
                src, done = wait_side(act, l, "pooled", 2)
                s.copy(pooled[:, :, SEQ:COLS], src[:, 0:2 * NB].rearrange("p (c n) -> p c n", c=2)).then_inc(done, 1)
                for c in range(2):
                    for hf in range(2):
                        src, _ = wait_side(act, l, "ya", c, hf)
                        s.activation(yab_hi[:, c, half(hf)], src[:, 0:HALF], ACT.Copy,
                                     scale=pool_scale[:, l, c:c + 1]).then_inc(y_hi_ready, 1)

            def rotary(l):
                act.wait_ge(ms_ready, 2 * l + 1)
                s.activation(rot_ms[:, 1], rot_ms[:, 0], ACT.Sqrt).then_inc(root_ready, 1)
                act.wait_ge(rotated, 5 * (l + 1))
                act.dma_start(d["k_out"][l], rot[:, :, 8:10, :].rearrange("p t h n -> p t (h n)")).then_inc(stored, 16)
                act.dma_start(d["ki_out"][l], rot[:, :, 14, :]).then_inc(stored, 16)
                act.dma_start(d["v_out"][l], vals[:]).then_inc(stored, 16)
                for t in range(TT + 1):
                    n = P if t < TT else NB
                    for part_ in range(2):
                        src, done = wait_side(act, l, "rotT", t, part_)
                        s.copy(rotT[:, 4 * part_:4 * part_ + 4, t * P:t * P + n],
                               src[:, 0:4 * n].rearrange("p (g n) -> p g n", g=4)).then_inc(done, 1)
                act.wait_ge(stored, 16 * (STORES * l + 6))
                load_sp(levels[:], d["levels"]).then_inc(levels_loaded, 16)

            def hgrn(l):
                for hd in range(HH):
                    use = main_use(l, "hgrn", hd)
                    if hd > 0:
                        wait_side_taken(act, l, "delta", hd - 1)
                        wait_side_taken(act, l, "level", hd - 1, LEVELS[-1])
                    for hf in range(2):
                        wait_main(act, main_unit(l, "hgrn", 4 * hd + hf))
                        s.copy(hq[:, half(hf)], bank[hf][:, 0:HALF]).then_inc(main_taken[hf], 1)
                    for hf in range(2):
                        wait_main(act, main_unit(l, "hgrn", 4 * hd + 2 + hf))
                        s.activation(hf_t[:, half(hf)], bank[2 + hf][:, 0:HALF], ACT.Sigmoid)\
                         .then_inc(main_taken[2 + hf], 1)
                    src, done = wait_side(act, l, "kbT", hd)
                    s.copy(kbT[:], src[:, :].rearrange("p (c n) -> p c n", c=TT)).then_inc(done, 1)
                    src, done = wait_side(act, l, "o", hd)
                    s.copy(h_o[:, 0:TT, hd, :], src[:, 0:TT * HV].rearrange("p (c n) -> p c n", c=TT)).then_inc(done, 1)
                act.wait_ge(chain_ready, HH * (l + 1))
                act.dma_start(d["hgrn_p"][l], state_p[:]).then_inc(stored, 16)
                load_sp(row_select[:], d["row_select"]).then_inc(state_loaded, 16)
                load_sp(state_in[:].rearrange("p b h v -> p (b h v)"), d["state_hgrn"][l]).then_inc(state_loaded, 16)
                src, done = wait_side(act, l, "o_sample")
                s.copy(h_o[0:NB, TT, :, :].rearrange("p h v -> p (h v)"), src[0:NB, 0:HIW]).then_inc(done, 1)
                act.wait_ge(state_ready, l + 1)
                act.dma_start(d["hgrn_s"][l], state_s[:].rearrange("p b h v -> p (b h v)")).then_inc(stored, 16)
                act.wait_ge(ms_ready, 2 * l + 2)
                s.activation(o_ms[:, 1], o_ms[:, 0], ACT.Sqrt).then_inc(root_ready, 1)
                for c in range(3):
                    src, _ = wait_side(act, l, "ybT", c)
                    if c < 2:
                        s.copy(yab_hi[:, 2 + c, 0:SEQ], src[:, :]).then_inc(y_hi_ready, 1)
                    else:
                        s.copy(yab_hi[:, 2:4, SEQ:COLS], src[:, 0:2 * NB].rearrange("p (c n) -> p c n", c=2))\
                         .then_inc(y_hi_ready, 1)

            def prompt_index(l, t):
                nk = (t + 1) * P
                for h in range(IDXH):
                    src, done = wait_side(act, l, "index", t, h)
                    uses = INDEX_USES * l + IDXH * t + h
                    if uses >= 2:
                        act.wait_ge(index_used, uses - 1)
                    s.activation(rel[h % 2][:, 0:nk], src[:, 0:nk], ACT.Relu, scale=IDX_SCALE).then_inc(done, 1)

            def prompt_attention(l, t):
                nk = (t + 1) * P
                for kind, h in attention_order():
                    if kind == "logits":
                        act.wait_ge(neg_max_ready, NH * (TT * l + t) + h + 1)
                        s.activation(probs[h % 2][:, 0:nk], probs[h % 2][:, 0:nk], ACT.Exp, scale=ATTN_SCALE,
                                     bias=neg_max[:, h:h + 1], accum_out=row_sum[:, h:h + 1]).then_inc(probs_ready, 1)
                    elif kind == "probT":
                        src, done = wait_side(act, l, "probT", t, h)
                        s.copy(probT[h % 4][:, 0:t + 1, :],
                               src[:, 0:nk].rearrange("p (b n) -> p b n", b=t + 1)).then_inc(done, 1)
                src, _ = wait_side(act, l, "ycT", t)
                s.copy(yc_hi[:, :, t * P:(t + 1) * P], src[:, :].rearrange("p (c n) -> p c n", c=4)).then_inc(y_hi_ready, 1)

            def sample_attention(l, page_regs):
                act.wait_ge(rotT_copied, l + 1)
                for b in range(NB):
                    for pg in range(PAGES):
                        page = page_regs[PAGES * b + pg]
                        for dst, src in ((k_page[:, b, pg, :], d["cache_k"]), (v_page[:, b, pg, :], d["cache_v"]),
                                         (ki_page[:, b, pg, :], d["cache_ki"])):
                            load_sp(dst, src[l, bass.ds(page, 1)].rearrange("o p n -> p (o n)"))\
                                .then_inc(pages_loaded, 16)
                for j in range(4):
                    src, done = wait_side(act, l, "kT_page", j)
                    s.copy(kT_s[:, 2 * j:2 * j + 2, 0:PAST], src[:, :].rearrange("p (b n) -> p b n", b=2)).then_inc(done, 1)
                for j in range(2):
                    src, done = wait_side(act, l, "kiT_page", j)
                    for pg in range(PAGES):
                        last = s.copy(kiT_s[:, 4 * j:4 * j + 4, pg * P:(pg + 1) * P],
                                      src[pg * HD:(pg + 1) * HD, :].rearrange("p (b n) -> p b n", b=4))
                    last.then_inc(done, 1)
                src, done = wait_side(act, l, "s_index")
                s.activation(rel_s[:], src[0:NB * IDXH, 0:LVIS], ACT.Relu, scale=IDX_SCALE).then_inc(done, 1)
                src, done = wait_side(act, l, "s_wsel")
                s.copy(wi_sel[:], src[0:NB * IDXH, 0:NB]).then_inc(done, 1)
                act.wait_ge(s_neg_ready, l + 1)
                s.activation(prob_s[:], prob_s[:], ACT.Exp, scale=ATTN_SCALE, bias=st_s[:, 1:2],
                             accum_out=st_s[:, 2:3]).then_inc(s_probs_ready, 1)

            def merge(l):
                with act.Fori(0, 4) as r:
                    for g in range(12):
                        tile, hf = divmod(g, 2)
                        use = main_use(l, "merge", 6 * r + g // 4)
                        wait_main(act, main_unit(l, "merge", 24 * r + g))
                        if g == 0:
                            act.wait_ge(mrg_ready, 16 * l + 4 * r + PRIMED)
                        s.activation(gate_s[:, tile, half(hf)], bank[g % 4][:, 0:HALF], ACT.Sigmoid)\
                         .then_inc(main_taken[g % 4], 1)
                    for n in range(2):
                        for hf in range(2):
                            act.wait_ge(mrg_ready, 16 * l + 4 * r + 2 * n + hf + 1 + PRIMED)
                            s.copy(mrg_hi[:, bass.ds(2 * r + n, 1), half(hf)].rearrange("p o n -> p (o n)"),
                                   part[:, 2, :]).then_inc(mrg_hi_ready, 1)

            hf_t = hf
            page_regs = None
            for l in range(DEPTH):
                norm(N_SUB * l)
                ffn_up(l, "up00", 0, UP[0])
                ffn_up(l, "up01", 0, UP[1])
                norm(N_SUB * l + 1)
                token_major(l)
                pool_branch(l)
                rotary(l)
                hgrn(l)
                wait_side_taken(act, l, "ybT", 2)
                act.wait_ge(stored, 16 * STORES * (l + 1))
                load_sp(causal[:], d["causal"]).then_inc(causal_loaded, 16)
                prompt_index(l, 0)
                for t in range(TT):
                    if t + 1 < TT:
                        prompt_index(l, t + 1)
                    prompt_attention(l, t)
                if page_regs is None:
                    page_regs = [act.value_load(page_ids[0:1, n:n + 1], min_val=0, max_val=d["cache_k"].shape[1] - 1)
                                 for n in range(NB * PAGES)]
                sample_attention(l, page_regs)
                merge(l)
                norm(N_SUB * l + 2)
                ffn_up(l, "up10", 0, UP[0])
                ffn_up(l, "up11", 0, UP[1])

        @block.vector
        def _(dve):
            v = nc.vector
            steps = Chain(dve, vector_step)
            link = steps.link

            def bc(ap, shape):
                return ap.to_broadcast(shape)

            dve.wait_ge(const_loaded, 16 * 12)
            link(v.tensor_tensor(lb_tmp[:, 2], lb[:, 0], lb[:, 1], ALU.max))
            link(v.tensor_tensor(lb_tmp[:, 0], lb[:, 0], lb_tmp[:, 2], ALU.subtract))
            v.tensor_tensor(lb_tmp[:, 1], lb[:, 1], lb_tmp[:, 2], ALU.subtract).then_inc(lb_exp, 1)
            dve.wait_ge(lb_exp, 2)
            link(v.tensor_tensor(lb_tmp[:, 2], lb_tmp[:, 0], lb_tmp[:, 1], ALU.add))
            link(v.reciprocal(lb_tmp[:, 3], lb_tmp[:, 2]))
            link(v.tensor_tensor(lb_tmp[:, 0], lb_tmp[:, 0], lb_tmp[:, 3], ALU.mult))
            link(v.tensor_tensor(lb_tmp[:, 1], lb_tmp[:, 1], lb_tmp[:, 3], ALU.mult))
            link(v.tensor_tensor(lb_tmp[:, 1], lb_tmp[:, 0], lb_tmp[:, 1], ALU.add))
            link(v.tensor_tensor(lb[:, 0], lb_tmp[:, 0], lb_tmp[:, 0], ALU.subtract))
            link(v.tensor_tensor(lb[:, 1], lb_tmp[:, 1], lb_tmp[:, 0], ALU.subtract))
            link(v.tensor_scalar(lb_rest[:], lb[:], -1.0, 1.0, ALU.mult, ALU.add))

            def take_ada(sub, r, j):
                dve.wait_ge(ada_used[j], sub * (ADA_SLOTS // 2) + r + 1 + PRIMED)
                at = 4 * r + 2 * j
                v.tensor_tensor(mod[sub % 2][:, bass.ds(at, 2), :],
                                ada_bank[:, 0:2 * CC].rearrange("p (a c) -> p a c", a=2),
                                bc(ada_b[:, sub, bass.ds(at, 2)].unsqueeze(2), [P, 2, CC]),
                                ALU.add).then_inc(ada_taken, 1)

            def norm(sub):
                l, j3 = divmod(sub, N_SUB)
                md = mod[sub % 2]
                dve.wait_ge(ada_taken, ADA_SLOTS * (sub + 1) + PRIMED)
                link(v.scalar_tensor_tensor(out=md[:, 8:16, :], in0=md[:, 8:16, :], scalar=1.0,
                                            in1=bc(norm_g[:, sub, :].unsqueeze(2), [P, KT, CC]),
                                            op0=ALU.add, op1=ALU.mult))
                if j3 != 1:
                    link(v.tensor_scalar(md[:, 16:24, :], md[:, 16:24, :], 0.5, None, ALU.mult))
                for hf in range(2):
                    src, done = wait_side(dve, l, "norm", j3, hf)
                    v.tensor_scalar(ms[:, half(hf)], src[:, 0:HALF], 1.0 / D_MODEL, EPS, ALU.mult, ALU.add)\
                     .then_inc(done, 1)
                dve.wait_ge(root_ready, 5 * l + (1, 2, 5)[j3])
                newton_rsqrt(steps, ms[:], root[:], newton[:], rstd[:])
                link(v.tensor_tensor(h_s[:], x[:, :, SEQ:COLS], md[:, 8:16, 1:CC], ALU.mult))
                link(v.tensor_tensor(h_s[:], h_s[:], bc(rstd[:, SEQ:COLS].unsqueeze(1), [P, KT, NB]), ALU.mult))
                v.tensor_tensor(h_s[:], h_s[:], md[:, 0:8, 1:CC], ALU.add).then_inc(scaled_ready, 1)
                for k in range(KT + 1):
                    if k < KT:
                        v.scalar_tensor_tensor(out=scaled[:, k, :], in0=x[:, k, 0:SEQ], scalar=md[:, 8 + k, 0:1],
                                               in1=rstd[:, 0:SEQ], op0=ALU.mult, op1=ALU.mult)\
                         .then_inc(scaled_ready, 1)
                    if k == 0:
                        dve.wait_ge(h_hi_ready, 9 * sub + 1)
                        dve.wait_ge(scaled_ready, 9 * sub + 1)
                        v.tensor_tensor(h_lo[:, :, SEQ:COLS], h_s[:], h_hi[:, :, SEQ:COLS].bitcast(F32),
                                        ALU.subtract).then_inc(h_lo_ready, 1)
                    else:
                        dve.wait_ge(h_hi_ready, 9 * sub + 1 + k)
                        v.scalar_tensor_tensor(out=h_lo[:, k - 1, 0:SEQ], in0=scaled[:, k - 1, :],
                                               scalar=md[:, k - 1, 0:1], in1=h_hi[:, k - 1, 0:SEQ].bitcast(F32),
                                               op0=ALU.add, op1=ALU.subtract).then_inc(h_lo_ready, 1)

            def ffn_up(l, stage, ada, tiles, count0):
                with dve.Fori(0, tiles // 2) as r:
                    for j in range(2):
                        for hf in range(2):
                            use = main_use(l, stage, 2 * r + j)
                            n = count0 + 4 * r + 2 * j + hf
                            wait_main(dve, main_unit(l, stage, 8 * r + 4 * j + 2 * hf + 1))
                            dve.wait_ge(main_taken[2 * hf], use + 1 + PRIMED)
                            v.tensor_tensor(prod[:, hf, :], silu_g[:, hf, :], bank[2 * hf + 1][:, 0:HALF],
                                            ALU.mult).then_inc(main_taken[2 * hf + 1], 1)
                            dve.wait_ge(main_taken[2 * hf + 1], use + 1 + PRIMED)
                            dve.wait_ge(mid_hi_ready, n + 1)
                            at = bass.ds(2 * r + j, 1)
                            v.tensor_tensor(mid_lo[:, at, half(hf)].rearrange("p o n -> p (o n)"), prod[:, hf, :],
                                            mid_hi[:, at, half(hf)].rearrange("p o n -> p (o n)").bitcast(F32),
                                            ALU.subtract).then_inc(mid_lo_ready, 1)
                        if ada is not None:
                            take_ada(ada, r, j)

            def residual(l, stage, sub, per_slot, slots):
                md = mod[sub % 2]
                tiles = per_slot * 2
                x0 = x_updates(sub) + (KT if stage in ("down01", "down11") else 0)
                links = tiles
                with dve.Fori(0, slots // 2) as r:
                    steps.loop(r, links, slots // 2)
                    for n in range(tiles):
                        at = r * tiles + n
                        for hf in range(2):
                            b = (2 * n + hf) % 4
                            wait_main(dve, main_unit(l, stage, 2 * tiles * r + 2 * n + hf))
                            if hf == 0:
                                cols = slice(0, HALF)
                            else:
                                cols = slice(HALF, SEQ)
                                link(v.tensor_tensor(x_tmp[:], bank[b][:, SEQ - HALF:HALF],
                                                     md[:, bass.ds(at + 16, 1), 1:CC].rearrange("p o c -> p (o c)"),
                                                     ALU.mult))
                            xs = x[:, bass.ds(at, 1), cols].rearrange("p o n -> p (o n)")
                            v.scalar_tensor_tensor(out=xs, in0=bank[b][:, 0:cols.stop - cols.start],
                                                   scalar=md[:, bass.ds(at + 16, 1), 0:1].rearrange("p o c -> p (o c)"),
                                                   in1=xs, op0=ALU.mult, op1=ALU.add).then_inc(main_taken[b], 1)
                        xs = x[:, bass.ds(at, 1), SEQ:COLS].rearrange("p o n -> p (o n)")
                        v.tensor_tensor(xs, xs, x_tmp[:], ALU.add).then_inc(x_updated, 1)
                        dve.wait_ge(x_updated, x0 + at + 1)
                    steps.end()

            def rotary(l):
                unit = main_unit(l, "token", 23)
                dve.wait_ge(main_taken[unit % 4], unit // 4 + 1 + PRIMED)
                dve.wait_ge(rope_loaded, 32 * (l + 1))
                for c in range(2):
                    for hf in range(2):
                        wait_side_taken(dve, l, "ya", c, hf)
                dve.wait_ge(stored, 16 * (STORES * l + 3))
                for t in range(TT + 1):
                    buf = (rot_a, rot_b)[t % 2]
                    link(v.tensor_tensor(buf[:], rot[:, t], rot[:, t], ALU.mult))
                    link(v.reduce_sum(rot_ms[:, 0, t, :], buf[:], axis=AX.X))
                v.tensor_scalar(rot_ms[:, 0], rot_ms[:, 0], 1.0 / HD, EPS, ALU.mult, ALU.add).then_inc(ms_ready, 1)
                dve.wait_ge(root_ready, 5 * l + 3)
                dve.wait_ge(ms_ready, 2 * l + 1)
                newton_rsqrt(steps, rot_ms[:, 0], rot_ms[:, 1], rot_ms[:, 2], rot_ms[:, 3])
                link(v.memset(rot_ms[:, 3, :, 10:14], 1.0))
                hw = HD // 2
                for t in range(TT + 1):
                    link(v.tensor_tensor(rot_a[:], rot[:, t], bc(rot_ms[:, 3, t, :].unsqueeze(2), [P, ROT, HD]), ALU.mult))
                    link(v.tensor_tensor(rot_a[:], rot_a[:], gamma[:], ALU.mult))
                    v.tensor_tensor(rot_b[:, :, 0:hw], rot_a[:, :, hw:HD],
                                    bc(rope[:, t, 1, 0:hw].unsqueeze(1), [P, ROT, hw]), ALU.mult)
                    v.tensor_tensor(rot_b[:, :, hw:HD], rot_a[:, :, 0:hw],
                                    bc(rope[:, t, 1, hw:HD].unsqueeze(1), [P, ROT, hw]), ALU.mult)
                    link(v.tensor_tensor(rot[:, t], rot_a[:], bc(rope[:, t, 0, :].unsqueeze(1), [P, ROT, HD]), ALU.mult))
                    v.tensor_tensor(rot[:, t], rot[:, t], rot_b[:], ALU.add).then_inc(rotated, 1)
                    dve.wait_ge(rotated, 5 * l + t + 1)

            def ya_tails(l):
                for c in range(2):
                    for hf in range(2):
                        src, done = wait_side(dve, l, "ya", c, hf)
                        dve.wait_ge(y_hi_ready, Y_HEADS * l + 2 * c + hf + 1)
                        v.scalar_tensor_tensor(out=yab_lo[:, c, half(hf)], in0=src[:, 0:HALF],
                                               scalar=pool_scale[:, l, c:c + 1],
                                               in1=yab_hi[:, c, half(hf)].bitcast(F32),
                                               op0=ALU.mult, op1=ALU.subtract).then_inc(done, 1)

            def hgrn(l):
                wait_side_taken(dve, l, "rotT", TT, 1)
                dve.wait_ge(levels_loaded, 16 * (l + 1))
                link(v.memset(h_o[:, TT], 0.0))
                pairs = PAIRS * l
                for hd in range(HH):
                    dve.wait_ge(main_taken[1], main_use(l, "hgrn", hd) + 1 + PRIMED)
                    dve.wait_ge(main_taken[3], main_use(l, "hgrn", hd) + 1 + PRIMED)
                    if hd > 0:
                        dve.wait_ge(side_full, SIDE[(l, "o", hd - 1)] + 1)
                    link(v.tensor_scalar(hf[:], hf[:], lb_rest[:, l, hd:hd + 1], lb[:, l, hd:hd + 1], ALU.mult, ALU.add))
                    v.tensor_scalar(hk[:], hf[:], -1.0, 1.0, ALU.mult, ALU.add).then_inc(pair_ready, 1)
                    pairs += 1
                    link(v.tensor_scalar(pre[:], hf[:, 0:SEQ], F_FLOOR, None, ALU.max))
                    dve.wait_ge(pair_ready, pairs)
                    link(v.tensor_scalar(f_s[:, hd, :], hf[:, SEQ:COLS], F_FLOOR, None, ALU.max))
                    link(v.tensor_copy(k_s[:, hd, :], hk[:, SEQ:COLS]))
                    link(v.tensor_copy(q_s[:, hd, :], hq[:, SEQ:COLS]))
                    link(v.memset(suf[:], 1.0))
                    for n, h in enumerate(LEVELS[1:] + (P,)):
                        if n >= 2:
                            dve.wait_ge(side_full, SIDE[(l, "level", hd, LEVELS[n - 1])] + 1)
                        v.tensor_tensor(qm[n % 2][:], hq[:, 0:SEQ], pre[:], ALU.mult)
                        v.tensor_tensor(km[n % 2][:], hk[:, 0:SEQ], suf[:], ALU.mult).then_inc(pair_ready, 1)
                        pairs += 1
                        if h < P:
                            pv = pre[:].rearrange("p (m a h) -> p m a h", a=2, h=h)
                            sv = suf[:].rearrange("p (m a h) -> p m a h", a=2, h=h)
                            m = SEQ // (2 * h)
                            dve.wait_ge(pair_ready, pairs)
                            link(v.tensor_tensor(sv[:, :, 0, :], sv[:, :, 0, :], bc(pv[:, :, 1, h - 1:h], [P, m, h]), ALU.mult))
                            link(v.tensor_tensor(pv[:, :, 1, :], pv[:, :, 1, :], bc(pv[:, :, 0, h - 1:h], [P, m, h]), ALU.mult))
                        src, done = wait_side(dve, l, "level", hd, LEVELS[n])
                        sv = src[:, :].rearrange("p (c n) -> p c n", c=TT)
                        mk = bc(levels[:, n, :].unsqueeze(1), [P, TT, P])
                        if n == 0:
                            v.tensor_tensor(att[:], sv, mk, ALU.mult).then_inc(done, 1)
                        else:
                            wait_side_taken(dve, l, "level", hd, LEVELS[n - 1])
                            v.copy_predicated(att[:], mk.bitcast(U32), sv).then_inc(done, 1)
                    src, done = wait_side(dve, l, "delta", hd)
                    dl = src[:, 0:TT * HV].rearrange("p (c n) -> p c n", c=TT)
                    link(v.tensor_copy(chain[:, 0], dl[:, 0]))
                    for c in range(1, TT):
                        last = v.scalar_tensor_tensor(out=chain[:, c], in0=chain[:, c - 1],
                                                      scalar=pre[:, (c + 1) * P - 1:(c + 1) * P], in1=dl[:, c],
                                                      op0=ALU.mult, op1=ALU.add)
                        if c < TT - 1:
                            link(last)
                    last.then_inc(done, 1)
                    wait_side_taken(dve, l, "delta", hd)
                    v.tensor_copy(state_p[:, hd], chain[:, TT - 1]).then_inc(chain_ready, 1)

                dve.wait_ge(state_loaded, 32 * (l + 1))
                dve.wait_ge(side_full, SIDE[(l, "o", HH - 1)] + 1)

                def over_v(tile, b0, nb):
                    return bc(tile[:, :, b0:b0 + nb].rearrange("p h b -> p b h").unsqueeze(3), [P, nb, HH, HV])

                for j in range(4):
                    bs = slice(2 * j, 2 * j + 2)
                    link(v.tensor_tensor(state_s[:, bs], state_in[:, bs], over_v(f_s, 2 * j, 2), ALU.mult))
                    src, done = wait_side(dve, l, "i_bcast", j)
                    v.tensor_tensor(state_in[:, bs], src[:, :].rearrange("p (b h v) -> p b h v", b=2, h=HH),
                                    over_v(k_s, 2 * j, 2), ALU.mult).then_inc(done, 1)
                    wait_side_taken(dve, l, "i_bcast", j)
                    last = v.tensor_tensor(state_s[:, bs], state_s[:, bs], state_in[:, bs], ALU.add)
                    if j < 3:
                        link(last)
                last.then_inc(state_ready, 1)
                dve.wait_ge(state_ready, l + 1)
                for j in range(4):
                    bs = slice(2 * j, 2 * j + 2)
                    last = v.tensor_tensor(state_q[:, bs], state_s[:, bs], over_v(q_s, 2 * j, 2), ALU.mult)
                last.then_inc(state_q_ready, 1)
                wait_side_taken(dve, l, "o_sample")
                wait_side_taken(dve, l, "o", HH - 1)
                link(v.tensor_tensor(o_sq[:], h_o[:], h_o[:], ALU.mult))
                link(v.reduce_sum(o_ms[:, 0], o_sq[:], axis=AX.X))
                v.tensor_scalar(o_ms[:, 0], o_ms[:, 0], 1.0 / HV, EPS, ALU.mult, ALU.add).then_inc(ms_ready, 1)
                dve.wait_ge(ms_ready, 2 * l + 2)
                dve.wait_ge(root_ready, 5 * l + 4)
                newton_rsqrt(steps, o_ms[:, 0], o_ms[:, 1], o_ms[:, 2], o_ms[:, 3])
                ov = h_o[:].rearrange("p t h v -> p (t h) v")
                link(v.tensor_tensor(ov, ov, bc(o_ms[:, 3].rearrange("p t h -> p (t h)").unsqueeze(2),
                                               [P, (TT + 1) * HH, HV]), ALU.mult))
                link(v.tensor_tensor(ov, ov, bc(onorm[:, l, :].unsqueeze(1), [P, (TT + 1) * HH, HV]), ALU.mult))
                v.tensor_tensor(h_o[:].rearrange("p t h v -> p t (h v)"), h_o[:].rearrange("p t h v -> p t (h v)"),
                                h_g[:], ALU.mult).then_inc(yb_ready, 1)
                for c in range(3):
                    src, done = wait_side(dve, l, "ybT", c)
                    dve.wait_ge(y_hi_ready, Y_HEADS * l + 4 + c + 1)
                    if c < 2:
                        v.tensor_tensor(yab_lo[:, 2 + c, 0:SEQ], src[:, :], yab_hi[:, 2 + c, 0:SEQ].bitcast(F32),
                                        ALU.subtract).then_inc(done, 1)
                    else:
                        v.tensor_tensor(yab_lo[:, 2:4, SEQ:COLS], src[:, 0:2 * NB].rearrange("p (c n) -> p c n", c=2),
                                        yab_hi[:, 2:4, SEQ:COLS].bitcast(F32), ALU.subtract).then_inc(done, 1)

            def prompt_index(l, t):
                nk = (t + 1) * P
                for h in range(IDXH):
                    wait_side_taken(dve, l, "index", t, h)
                    v.scalar_tensor_tensor(out=score[:, 0:nk], in0=rel[h % 2][:, 0:nk], scalar=wi[:, t, h:h + 1],
                                           in1=causal[:, SEQ - nk:SEQ] if h == 0 else score[:, 0:nk],
                                           op0=ALU.mult, op1=ALU.add).then_inc(index_used, 1)
                    dve.wait_ge(index_used, INDEX_USES * l + 4 * t + h + 1)

            def top_round(t, n):
                nk = (t + 1) * P
                src = score if n == 0 else work
                link(v.max(top8[:], src[:, 0:nk]))
                link(v.match_replace(out=work[:, 0:nk], in_to_replace=top8[:], in_values=src[:, 0:nk], imm_value=TAKEN))

            def make_mask(t):
                nk = (t + 1) * P
                if t == 0:
                    link(v.tensor_copy(mask[0][:, 0:nk], causal[:, SEQ - nk:SEQ]))
                else:
                    link(v.tensor_scalar(mask[t % 2][:, 0:nk], work[:, 0:nk], TAKEN, NEG_BIG, ALU.not_equal, ALU.mult))

            def prompt_attention(l, t):
                nk = (t + 1) * P
                rounds = list(range(TOP_PROMPT // 8)) if t + 1 < TT else []
                heads = NH * (TT * l + t)
                for kind, h in attention_order():
                    if kind == "logits":
                        src, done = wait_side(dve, l, "logits", t, h)
                        if h >= 2:
                            dve.wait_ge(side_full, SIDE[(l, "probT", t, h - 2)] + 1)
                        v.tensor_tensor_reduce(out=probs[h % 2][:, 0:nk], in0=src[:, 0:nk], in1=mask[t % 2][:, 0:nk],
                                               scale=1.0, scalar=TAKEN, op0=ALU.add, op1=ALU.max,
                                               accum_out=row_max[:, h:h + 1]).then_inc(done, 1)
                        wait_side_taken(dve, l, "logits", t, h)
                        v.tensor_scalar(neg_max[:, h:h + 1], row_max[:, h:h + 1], -ATTN_SCALE, None, ALU.mult)\
                         .then_inc(neg_max_ready, 1)
                        for _ in range(2):
                            if rounds:
                                top_round(t + 1, rounds.pop(0))
                    elif kind == "pv":
                        src, done = wait_side(dve, l, "pv", t, h)
                        dve.wait_ge(probs_ready, heads + 2 * h + 2)
                        link(v.reciprocal(row_inv[:, 2 * h:2 * h + 2], row_sum[:, 2 * h:2 * h + 2]))
                        v.tensor_tensor(o_tok[:, 2 * h:2 * h + 2, :], src[:, 0:2 * HD].rearrange("p (a n) -> p a n", a=2),
                                        bc(row_inv[:, 2 * h:2 * h + 2].unsqueeze(2), [P, 2, HD]), ALU.mult)\
                         .then_inc(done, 1)
                src, done = wait_side(dve, l, "ycT", t)
                dve.wait_ge(y_hi_ready, Y_HEADS * l + 7 + t + 1)
                v.tensor_tensor(yc_lo[:, :, t * P:(t + 1) * P], src[:, :].rearrange("p (c n) -> p c n", c=4),
                                yc_hi[:, :, t * P:(t + 1) * P].bitcast(F32), ALU.subtract).then_inc(done, 1)
                if t + 1 < TT:
                    make_mask(t + 1)
                for n in range(3 * t, 3 * t + 3):
                    take_ada(N_SUB * l + 2, n // 2, n % 2)

            def sample_attention(l):
                v.tensor_copy(rotT_s[:], rotT[:, :, SEQ:COLS]).then_inc(rotT_copied, 1)
                dve.wait_ge(rotT_copied, l + 1)
                v.memset(q_blk[:], 0.0)
                link(v.memset(qi_blk[:], 0.0))
                qd = q_blk[:].rearrange("p c b n g -> p (c b) n g")
                for n in range(NKV):
                    ps = slice(n * HD, (n + 1) * HD)
                    v.tensor_copy(qd[ps, 0:NB * NB:NB + 1, n, :], rotT_s[ps, 0:4, :].rearrange("p g b -> p b g"))
                qi = qi_blk[:].rearrange("p c b h -> p (c b) h")
                for par in range(2):
                    last = v.tensor_copy(qi[:, 0:NB * NB:NB + 1, par:IDXH:2],
                                         rotT_s[par * HD:(par + 1) * HD, 5:7, :].rearrange("p g b -> p b g"))
                v.tensor_copy(kT_s[:, :, PAST], rotT_s[:, 4, :])
                v.tensor_copy(kiT_s[:, :, PAST], rotT_s[0:HD, 7, :]).then_inc(q_blk_ready, 1)
                v.tensor_tensor(wi_exp[:], spread_idx[:], bc(wi[0:NB, TT, :].unsqueeze(1), [NB, NB, IDXH]),
                                ALU.mult).then_inc(wi_exp_ready, 1)
                src, done = wait_side(dve, l, "s_score")
                v.tensor_copy(score_s[:], src[0:NB, 0:LVIS]).then_inc(done, 1)
                wait_side_taken(dve, l, "s_score")
                for n in range(TOP_SAMPLE // 8):
                    cur = score_s if n == 0 else work_s
                    link(v.max(top8_s[:], cur[:]))
                    link(v.match_replace(out=work_s[:], in_to_replace=top8_s[:], in_values=cur[:], imm_value=TAKEN))
                v.tensor_scalar(mask_s[:], work_s[:], TAKEN, NEG_BIG, ALU.not_equal, ALU.mult).then_inc(mask_s_ready, 1)
                src, done = wait_side(dve, l, "s_logits")
                v.tensor_copy(prob_s[:], src[0:NB * NH, 0:LVIS]).then_inc(done, 1)
                wait_side_taken(dve, l, "s_logits")
                link(v.reduce_max(st_s[:, 0:1], prob_s[:], axis=AX.X))
                v.tensor_scalar(st_s[:, 1:2], st_s[:, 0:1], -ATTN_SCALE, None, ALU.mult).then_inc(s_neg_ready, 1)
                link(v.memset(probT_blk[:], 0.0))
                dve.wait_ge(s_probs_ready, l + 1)
                link(v.reciprocal(st_s[:, 3:4], st_s[:, 2:3]))
                v.tensor_scalar(own_diag[:], ident[0:NB * NH, 0:NB * NH], prob_s[:, PAST:LVIS], None, ALU.mult)\
                 .then_inc(own_diag_ready, 1)
                src, done = wait_side(dve, l, "s_probT")
                for pg in range(PAGES):
                    dst = probT_blk[:, pg].rearrange("p c (b h) -> p (c b) h", h=NH)
                    v.tensor_copy(dst[:, 0:NB * NB:NB + 1, :],
                                  src[:, pg * NB * NH:(pg + 1) * NB * NH].rearrange("p (b h) -> p b h", h=NH))
                v.tensor_copy(own_prob[:], src[0:NB, 2 * NB * NH:3 * NB * NH]).then_inc(done, 1)
                src, done = wait_side(dve, l, "s_o")
                v.tensor_scalar(o_s[:], src[0:NB * NH, 0:P], st_s[:, 3:4], None, ALU.mult).then_inc(done, 1)
                src, done = wait_side(dve, l, "s_oT")
                sv = src[:, 0:NB * NH].rearrange("p (b n g) -> p b n g", n=NKV, g=4)
                for n in range(NKV):
                    for par in range(2):
                        dst = slice(par * HD, (par + 1) * HD)
                        frm = sv[n * HD:(n + 1) * HD, :, n, par:4:2].rearrange("p b g -> p g b")
                        link(v.tensor_copy(yc_hi[dst, 2 * n:2 * n + 2, SEQ:COLS], frm))
                for n in range(NKV):
                    for par in range(2):
                        dst = slice(par * HD, (par + 1) * HD)
                        frm = sv[n * HD:(n + 1) * HD, :, n, par:4:2].rearrange("p b g -> p g b")
                        last = v.tensor_tensor(yc_lo[dst, 2 * n:2 * n + 2, SEQ:COLS], frm,
                                               yc_hi[dst, 2 * n:2 * n + 2, SEQ:COLS].bitcast(F32), ALU.subtract)
                last.then_inc(done, 1)

            def merge(l):
                with dve.Fori(0, 4) as r:
                    steps.loop(r, 4, 4)
                    for n in range(2):
                        for hf in range(2):
                            for b in range(3):
                                g = 12 + 6 * n + 3 * hf + b
                                wait_main(dve, main_unit(l, "merge", 24 * r + g))
                                if b == 0:
                                    dve.wait_ge(main_taken[3], main_use(l, "merge", 6 * r + 3) + PRIMED)
                                last = v.tensor_tensor(part[:, b, :], gate_s[:, 3 * n + b, half(hf)],
                                                       bank[g % 4][:, 0:HALF], ALU.mult)
                                last.then_inc(main_taken[g % 4], 1)
                                dve.wait_ge(main_taken[g % 4], main_use(l, "merge", 6 * r + g // 4) + 1 + PRIMED)
                            link(v.tensor_tensor(part[:, 0, :], part[:, 0, :], part[:, 1, :], ALU.add))
                            v.tensor_tensor(part[:, 2, :], part[:, 0, :], part[:, 2, :], ALU.add).then_inc(mrg_ready, 1)
                            dve.wait_ge(mrg_ready, 16 * l + 4 * r + 2 * n + hf + 1 + PRIMED)
                            dve.wait_ge(mrg_hi_ready, 16 * l + 4 * r + 2 * n + hf + 1)
                            at = bass.ds(2 * r + n, 1)
                            v.tensor_tensor(mrg_lo[:, at, half(hf)].rearrange("p o n -> p (o n)"), part[:, 2, :],
                                            mrg_hi[:, at, half(hf)].rearrange("p o n -> p (o n)").bitcast(F32),
                                            ALU.subtract).then_inc(mrg_lo_ready, 1)
                    steps.end()

            with dve.Fori(0, ADA_SLOTS // 2) as r:
                for j in range(2):
                    take_ada(0, r, j)
            mids = 0
            for l in range(DEPTH):
                for f in range(2):
                    sub = N_SUB * l + 2 * f
                    norm(sub)
                    following = sub + 1 if sub + 1 < DEPTH * N_SUB else None
                    ffn_up(l, f"up{f}0", following, UP[0], mids)
                    mids += 2 * UP[0]
                    residual(l, f"down{f}0", sub, 1, KT)
                    ffn_up(l, f"up{f}1", None, UP[1], mids)
                    mids += 2 * UP[1]
                    residual(l, f"down{f}1", sub, 1, KT)
                    if f == 0:
                        norm(sub + 1)
                        ya_tails(l)
                        rotary(l)
                        hgrn(l)
                        dve.wait_ge(causal_loaded, 16 * (l + 1))
                        prompt_index(l, 0)
                        make_mask(0)
                        for t in range(TT):
                            if t + 1 < TT:
                                prompt_index(l, t + 1)
                            prompt_attention(l, t)
                        sample_attention(l)
                        merge(l)
                        residual(l, "out", sub + 1, 2, 4)

        @block.tensor
        def _(pe):
            mm = nc.tensor.matmul
            order = [0]

            def open_side(*key):
                n, b, use = side_unit(*key)
                assert n == order[0], (key, n, order[0])
                order[0] += 1
                if use > 0:
                    pe.wait_ge(side_taken[b], use)
                return bank[4 + b]

            def product(out, blocks, ws, xs):
                (wh, wl), (xh, xl) = ws, xs
                for n, (wb, xb) in enumerate(blocks):
                    mm(out, wh(wb), xh(xb), start=(n == 0), stop=False)
                    mm(out, wl(wb), xh(xb), start=False, stop=False)
                    last = mm(out, wh(wb), xl(xb), start=False, stop=(n == len(blocks) - 1))
                return last

            def weights(j):
                def blk(tile):
                    return lambda n: tile[:, n * P:(n + 1) * P]
                return blk(w_hi[j]), blk(w_lo[j])

            def moving(hi, lo, hf):
                return (lambda k: hi[:, k, half(hf)]), (lambda k: lo[:, k, half(hf)])

            def wait_slot(l, stage, r, j):
                pe.wait_ge(w_split[j], slot_use(l, stage, r) + 1 + PRIMED)

            def take_main(b, use):
                pe.wait_ge(main_taken[b], use + PRIMED)

            def ada(sub, r, j):
                n = sub * (ADA_SLOTS // 2) + r
                pe.wait_ge(ada_loaded[j], 16 * n + 16)
                pe.wait_ge(ada_taken, 2 * n + j + PRIMED)
                for a in range(2):
                    for k in range(KT):
                        last = mm(ada_bank[:, a * CC:(a + 1) * CC], ada_w[j][:, a, k, :], cond[:, k, :],
                                  start=(k == 0), stop=(k == KT - 1))
                last.then_inc(ada_used[j], 1)

            def norm(sub):
                l, j3 = divmod(sub, N_SUB)
                outs = [open_side(l, "norm", j3, hf) for hf in range(2)]
                for k in range(KT):
                    pe.wait_ge(squared, KT * sub + k + 1)
                    for hf in range(2):
                        last = mm(outs[hf][:, 0:HALF], ones[:], sq[:, k, half(hf)], start=(k == 0), stop=(k == KT - 1))
                        if k == KT - 1:
                            last.then_inc(side_full, 1)
                pe.wait_ge(h_lo_ready, 9 * (sub + 1))

            def ffn_up(l, stage, sub_ada, tiles):
                with pe.Fori(0, tiles // 2) as r:
                    for j in range(2):
                        wait_slot(l, stage, r, j)
                        use = main_use(l, stage, 2 * r + j)
                        for hf in range(2):
                            for which in range(2):
                                take_main(2 * hf + which, use)
                                product(bank[2 * hf + which][:, 0:HALF], [(which * KT + k, k) for k in range(KT)],
                                        (lambda n: weights(j)[0](n), lambda n: weights(j)[1](n)),
                                        moving(h_hi, h_lo, hf)).then_inc(main_full, 1)
                        if sub_ada is not None:
                            ada(sub_ada, r, j)

            def down(l, stage, tiles, mids):
                pe.wait_ge(mid_lo_ready, mids)
                with pe.Fori(0, KT // 2) as r:
                    for j in range(2):
                        wait_slot(l, stage, r, j)
                        use = main_use(l, stage, r)
                        for hf in range(2):
                            take_main(2 * j + hf, use)
                            product(bank[2 * j + hf][:, 0:HALF], [(k, k) for k in range(tiles)], weights(j),
                                    moving(mid_hi, mid_lo, hf)).then_inc(main_full, 1)

            def token_major(l):
                for slot in range(8):
                    j, r = slot % 2, slot // 2
                    wait_slot(l, "token", r, j)
                    width = 256 if slot < 7 else HD + IDXH
                    for u in range(3):
                        unit = main_unit(l, "token", 3 * slot + u)
                        take_main(unit % 4, unit // 4)
                        for i, t in enumerate((2 * u, 2 * u + 1) if u < 2 else (TT,)):
                            out = bank[unit % 4][:, 256 * i:256 * i + width]
                            for k in range(KT):
                                cols = slice(t * P, (t + 1) * P)
                                wcols = slice(k * 256, k * 256 + width)
                                mm(out, h_hi[:, k, cols], w_hi[j][:, wcols], start=(k == 0), stop=False)
                                mm(out, h_lo[:, k, cols], w_hi[j][:, wcols], start=False, stop=False)
                                last = mm(out, h_hi[:, k, cols], w_lo[j][:, wcols], start=False, stop=(k == KT - 1))
                        last.then_inc(main_full, 1)

            def token_tile_wait(l, n):
                unit = main_unit(l, "token", n)
                pe.wait_ge(main_taken[unit % 4], unit // 4 + 1 + PRIMED)

            def pool_branch(l):
                pe.wait_ge(pool_loaded, 80 * (l + 1))
                token_tile_wait(l, 2)
                for c in range(2):
                    out = open_side(l, "pooled", c)
                    for g in (2 * c, 2 * c + 1):
                        rows = slice((g % 2) * 64, (g % 2) * 64 + 64)
                        ch = slice(g * POOL_G, (g + 1) * POOL_G)
                        for t in range(TT):
                            o = out[rows, t * P:(t + 1) * P]
                            last = mm(o, pool_u[:, t, ch], windows[:, 1 if t == 0 else 0, g, :], start=True, stop=(t == 0))
                            if t > 0:
                                last = mm(o, pool_u[:, t - 1, ch], windows[:, 2, g, :], start=False, stop=True)
                    last.then_inc(side_full, 1)
                out = open_side(l, "pooled", 2)
                for g in range(4):
                    rows = slice((g % 2) * 64, (g % 2) * 64 + 64)
                    ch = slice(g * POOL_G, (g + 1) * POOL_G)
                    o = out[rows, (g // 2) * NB:(g // 2 + 1) * NB]
                    mm(o, pool_past[:, ch], windows_past[:, g, :], start=True, stop=False)
                    last = mm(o, pool_u[0:NB, TT, ch], windows_own[:, g, :], start=False, stop=True)
                last.then_inc(side_full, 1)
                for c in range(2):
                    wait_side_taken(pe, l, "pooled", c)
                wait_side_taken(pe, l, "pooled", 2)
                for c in range(2):
                    for hf in range(2):
                        out = open_side(l, "ya", c, hf)
                        mm(out[:, 0:HALF], pool_w[:, c, :], pooled[:, c, half(hf)], start=True, stop=True)\
                            .then_inc(side_full, 1)

            def rotary(l):
                for t in range(TT + 1):
                    n = P if t < TT else NB
                    pe.wait_ge(rotated, 5 * l + t + 1)
                    rt = rot[0:n, t]
                    for part_ in range(2):
                        out = open_side(l, "rotT", t, part_)
                        for i in range(4 if part_ == 0 else 3):
                            row = 8 * part_ + 2 * i
                            last = nc.tensor.transpose(out[:, i * n:(i + 1) * n],
                                                       rt[:, row:row + 2, :].rearrange("p a e -> p (a e)"), ident[0:n, 0:n])
                        if part_ == 1:
                            for a in range(2):
                                last = mm(out[a * HD:(a + 1) * HD, 3 * n:4 * n], rt[:, ROT - 1, :], ident[0:n, 0:n],
                                          start=True, stop=True)
                        last.then_inc(side_full, 1)

            def hgrn(l):
                pairs = PAIRS * l
                for hd in range(HH):
                    j, r = hd % 2, hd // 2
                    wait_slot(l, "hgrn", r, j)
                    for which in range(2):
                        for hf in range(2):
                            b = 2 * which + hf
                            take_main(b, main_use(l, "hgrn", hd))
                            product(bank[b][:, 0:HALF], [(which * KT + k, k) for k in range(KT)], weights(j),
                                    moving(h_hi, h_lo, hf)).then_inc(main_full, 1)
                    for n, h in enumerate(LEVELS):
                        out = open_side(l, "level", hd, h)
                        pairs += 1
                        pe.wait_ge(pair_ready, pairs)
                        for c in range(TT):
                            cs = slice(c * P, (c + 1) * P)
                            kt, qt = (hk, hq) if n == 0 else (km[(n - 1) % 2], qm[(n - 1) % 2])
                            last = mm(out[:, cs], kt[:, cs], qt[:, cs], start=True, stop=True)
                        last.then_inc(side_full, 1)
                    pairs += 1
                    fin = len(LEVELS[1:]) % 2
                    pe.wait_ge(pair_ready, pairs)
                    out = open_side(l, "kbT", hd)
                    for c in range(TT):
                        cs = slice(c * P, (c + 1) * P)
                        last = nc.tensor.transpose(out[:, cs], km[fin][:, cs], ident[:])
                    last.then_inc(side_full, 1)
                    vs = slice(hd * HV, (hd + 1) * HV)
                    out = open_side(l, "delta", hd)
                    wait_side_taken(pe, l, "kbT", hd)
                    for c in range(TT):
                        last = mm(out[:, c * HV:(c + 1) * HV], kbT[:, c, :], h_i[:, c, vs], start=True, stop=True)
                    last.then_inc(side_full, 1)
                    out = open_side(l, "o", hd)
                    wait_side_taken(pe, l, "delta", hd)
                    wait_side_taken(pe, l, "level", hd, LEVELS[-1])
                    for c in range(TT):
                        o = out[:, c * HV:(c + 1) * HV]
                        last = mm(o, att[:, c, :], h_i[:, c, vs], start=True, stop=(c == 0))
                        if c > 0:
                            last = mm(o, qm[fin][:, c * P:(c + 1) * P], chain[:, c - 1, :], start=False, stop=True)
                    last.then_inc(side_full, 1)
                pe.wait_ge(state_loaded, 32 * (l + 1))
                for j in range(4):
                    out = open_side(l, "i_bcast", j)
                    for i in range(2):
                        last = mm(out[:, i * HIW:(i + 1) * HIW], row_select[:, 2 * j + i, :], h_i[0:NB, TT, :],
                                  start=True, stop=True)
                    last.then_inc(side_full, 1)
                out = open_side(l, "o_sample")
                pe.wait_ge(state_q_ready, l + 1)
                for b in range(NB):
                    last = mm(out[0:NB, 0:HIW], col_select[:, NB - 1 - b:2 * NB - 1 - b],
                              state_q[:, b].rearrange("p h v -> p (h v)"), start=(b == 0), stop=(b == NB - 1))
                last.then_inc(side_full, 1)
                pe.wait_ge(yb_ready, l + 1)
                for c in range(2):
                    out = open_side(l, "ybT", c)
                    for t in range(TT):
                        src = h_o[:, t].rearrange("p h v -> p (h v)")
                        last = nc.tensor.transpose(out[:, t * P:(t + 1) * P], src[:, c * P:(c + 1) * P], ident[:])
                    last.then_inc(side_full, 1)
                out = open_side(l, "ybT", 2)
                for c in range(2):
                    src = h_o[0:NB, TT].rearrange("p h v -> p (h v)")
                    last = nc.tensor.transpose(out[:, c * NB:(c + 1) * NB], src[:, c * P:(c + 1) * P], ident[0:NB, 0:NB])
                last.then_inc(side_full, 1)

            def prompt_index(l, t):
                nk = (t + 1) * P
                for h in range(IDXH):
                    out = open_side(l, "index", t, h)
                    rows = slice((h % 2) * HD, (h % 2 + 1) * HD)
                    mm(out[:, 0:nk], rotT[rows, 5 + h // 2, t * P:(t + 1) * P], rotT[rows, 7, 0:nk],
                       start=True, stop=True).then_inc(side_full, 1)

            def prompt_attention(l, t):
                nk = (t + 1) * P
                for kind, h in attention_order():
                    out = open_side(l, kind, t, h)
                    if kind == "logits":
                        n, g = divmod(h, 4)
                        rows = slice(n * HD, (n + 1) * HD)
                        last = mm(out[:, 0:nk], rotT[rows, g, t * P:(t + 1) * P], rotT[rows, 4, 0:nk], start=True, stop=True)
                    elif kind == "probT":
                        pe.wait_ge(probs_ready, NH * (TT * l + t) + h + 1)
                        for kb in range(t + 1):
                            ks = slice(kb * P, (kb + 1) * P)
                            last = nc.tensor.transpose(out[:, ks], probs[h % 2][:, ks], ident[:])
                    else:
                        wait_side_taken(pe, l, "probT", t, 2 * h)
                        wait_side_taken(pe, l, "probT", t, 2 * h + 1)
                        for i in range(2):
                            head = 2 * h + i
                            n = head // 4
                            for kb in range(t + 1):
                                last = mm(out[:, i * HD:(i + 1) * HD], probT[head % 4][:, kb, :],
                                          vals[:, kb, n * HD:(n + 1) * HD], start=(kb == 0), stop=(kb == t))
                    last.then_inc(side_full, 1)
                out = open_side(l, "ycT", t)
                wait_side_taken(pe, l, "pv", t, NH // 2 - 1)
                for c in range(4):
                    last = nc.tensor.transpose(out[:, c * P:(c + 1) * P],
                                               o_tok[:, 2 * c:2 * c + 2, :].rearrange("p a n -> p (a n)"), ident[:])
                last.then_inc(side_full, 1)
                for n in range(3 * t, 3 * t + 3):
                    ada(N_SUB * l + 2, n // 2, n % 2)

            def sample_attention(l):
                pe.wait_ge(pages_loaded, 16 * 3 * NB * PAGES * (l + 1))
                for j in range(4):
                    out = open_side(l, "kT_page", j)
                    for i in range(4):
                        b, pg = 2 * j + i // 2, i % 2
                        last = nc.tensor.transpose(out[:, i * P:(i + 1) * P], k_page[:, b, pg, :], ident[:])
                    last.then_inc(side_full, 1)
                for j in range(2):
                    out = open_side(l, "kiT_page", j)
                    for i in range(4):
                        last = nc.tensor.transpose(out[:, i * P:(i + 1) * P],
                                                   ki_page[:, 4 * j + i].rearrange("p a n -> p (a n)"), ident[:])
                    last.then_inc(side_full, 1)
                out = open_side(l, "s_index")
                pe.wait_ge(q_blk_ready, l + 1)
                wait_side_taken(pe, l, "kiT_page", 1)
                for b in range(NB):
                    last = mm(out[0:NB * IDXH, 0:LVIS], qi_blk[:, b].rearrange("p b h -> p (b h)"), kiT_s[:, b, :],
                              start=(b == 0), stop=(b == NB - 1))
                last.then_inc(side_full, 1)
                out = open_side(l, "s_wsel")
                pe.wait_ge(wi_exp_ready, l + 1)
                nc.tensor.transpose(out[0:NB * IDXH, 0:NB], wi_exp[:].rearrange("p b h -> p (b h)"), ident[0:NB, 0:NB])\
                    .then_inc(side_full, 1)
                out = open_side(l, "s_score")
                wait_side_taken(pe, l, "s_index")
                wait_side_taken(pe, l, "s_wsel")
                mm(out[0:NB, 0:LVIS], wi_sel[:], rel_s[:], start=True, stop=True).then_inc(side_full, 1)
                out = open_side(l, "s_logits")
                wait_side_taken(pe, l, "kT_page", 3)
                for b in range(NB):
                    mm(out[0:NB * NH, 0:LVIS], q_blk[:, b].rearrange("p b n g -> p (b n g)"), kT_s[:, b, :],
                       start=(b == 0), stop=False)
                pe.wait_ge(mask_s_ready, l + 1)
                mm(out[0:NB * NH, 0:LVIS], spread_heads[:], mask_s[:], start=False, stop=True).then_inc(side_full, 1)
                out = open_side(l, "s_probT")
                pe.wait_ge(s_probs_ready, l + 1)
                for pg in range(PAGES):
                    nc.tensor.transpose(out[:, pg * NB * NH:(pg + 1) * NB * NH], prob_s[:, pg * P:(pg + 1) * P],
                                        ident[0:NB * NH, 0:NB * NH])
                pe.wait_ge(own_diag_ready, l + 1)
                mm(out[0:NB, 2 * NB * NH:3 * NB * NH], gather_heads[:], own_diag[:], start=True, stop=True)\
                    .then_inc(side_full, 1)
                out = open_side(l, "s_o")
                wait_side_taken(pe, l, "s_probT")
                for b in range(NB):
                    for pg in range(PAGES):
                        mm(out[0:NB * NH, 0:P], probT_blk[:, pg, b, :], v_page[:, b, pg, :],
                           start=(b == 0 and pg == 0), stop=False)
                mm(out[0:NB * NH, 0:P], own_prob[:], vals[0:NB, TT, :], start=False, stop=True).then_inc(side_full, 1)
                out = open_side(l, "s_oT")
                wait_side_taken(pe, l, "s_o")
                nc.tensor.transpose(out[:, 0:NB * NH], o_s[:], ident[0:NB * NH, 0:NB * NH]).then_inc(side_full, 1)

            def merge(l):
                wait_side_taken(pe, l, "s_oT")
                with pe.Fori(0, 4) as r:
                    for slot in range(3):
                        j = slot % 2
                        wait_slot(l, "merge", 2 * r + slot // 2, j)
                        for a in range(2):
                            for hf in range(2):
                                b = 2 * a + hf
                                take_main(b, main_use(l, "merge", 6 * r + slot))
                                product(bank[b][:, 0:HALF], [(a * KT + k, k) for k in range(KT)], weights(j),
                                        moving(h_hi, h_lo, hf)).then_inc(main_full, 1)
                    wait_slot(l, "merge", 2 * r + 1, 1)
                    for n in range(2):
                        for hf in range(2):
                            for br, (first, count) in enumerate(((0, 2), (2, 2), (4, 4))):
                                g = 12 + 6 * n + 3 * hf + br
                                take_main(g % 4, main_use(l, "merge", 6 * r + g // 4))
                                hi, lo, off = (yab_hi, yab_lo, 0) if br < 2 else (yc_hi, yc_lo, 4)
                                product(bank[g % 4][:, 0:HALF],
                                        [(n * KT + first + k, first + k - off) for k in range(count)],
                                        weights(1), moving(hi, lo, hf)).then_inc(main_full, 1)
                pe.wait_ge(mrg_lo_ready, 16 * (l + 1))
                with pe.Fori(0, 2) as r:
                    for j in range(2):
                        wait_slot(l, "out", r, j)
                        for a in range(2):
                            for hf in range(2):
                                b = 2 * a + hf
                                take_main(b, main_use(l, "out", 2 * r + j))
                                product(bank[b][:, 0:HALF], [(a * KT + k, k) for k in range(KT)], weights(j),
                                        moving(mrg_hi, mrg_lo, hf)).then_inc(main_full, 1)

            pe.wait_ge(const_loaded, 16 * 12)
            pe.wait_ge(cond_ready, 1)
            pe.wait_ge(setup_done, 3)
            with pe.Fori(0, ADA_SLOTS // 2) as r:
                for j in range(2):
                    ada(0, r, j)
            mids = 0
            for l in range(DEPTH):
                for f in range(2):
                    sub = N_SUB * l + 2 * f
                    following = sub + 1 if sub + 1 < DEPTH * N_SUB else None
                    norm(sub)
                    for p_ in range(2):
                        ffn_up(l, f"up{f}{p_}", following if p_ == 0 else None, UP[p_])
                        mids += 2 * UP[p_]
                        down(l, f"down{f}{p_}", UP[p_], mids)
                    if f == 0:
                        norm(sub + 1)
                        token_major(l)
                        pool_branch(l)
                        rotary(l)
                        hgrn(l)
                        prompt_index(l, 0)
                        for t in range(TT):
                            if t + 1 < TT:
                                prompt_index(l, t + 1)
                            prompt_attention(l, t)
                        sample_attention(l)
                        merge(l)


def kernel(**inputs):
    import concourse.bacc as bacc
    from concourse.bass_utils import run_bass_kernel_spmd

    a = {k: np.asarray(v) for k, v in inputs.items()}

    def blocks(w):
        k, n = w.shape
        return w.reshape(k // P, P, n // P, P).transpose(1, 2, 0, 3)

    def per_slot(w, tiles):
        p, n, k, _ = w.shape
        return w.reshape(p, n // tiles, tiles * k * P).transpose(1, 0, 2)

    w = np.zeros((DEPTH * LAYER_SLOTS, P, SLOT), np.float32)
    for l in range(DEPTH):
        at = LAYER_SLOTS * l
        w_in = a["w_in"][l]
        cuts = np.cumsum((256, 512, 512, 256, 256, 512, 128, 128, 256, 64, 4))
        u, hq, hf, hi, hg, aq, ak, av, iq, ik, iw, gl = np.split(w_in, cuts, axis=1)
        for f in (0, 1):
            g_b, u_b = blocks(a["ffn_wg"][l, f]), blocks(a["ffn_wu"][l, f])
            down = blocks(a["ffn_wd"][l, f])
            first = 0
            for p_, tiles in enumerate(UP):
                s0 = at + SLOT0[f"up{f}{p_}"]
                both = np.stack([g_b[:, first:first + tiles], u_b[:, first:first + tiles]], 2)
                w[s0:s0 + tiles] = both.reshape(P, tiles, SLOT).transpose(1, 0, 2)
                s0 = at + SLOT0[f"down{f}{p_}"]
                w[s0:s0 + KT, :, 0:tiles * P] = per_slot(down[:, :, first:first + tiles], 1)
                first += tiles
        token = [u, hi, hg, aq[:, 0:256], aq[:, 256:512], np.concatenate([ak, av], 1), iq,
                 np.concatenate([ik, iw, np.zeros((D_MODEL, 256 - 68), np.float32)], 1)]
        s0 = at + SLOT0["token"]
        for n, t in enumerate(token):
            w[s0 + n] = t.reshape(KT, P, 256).transpose(1, 0, 2).reshape(P, SLOT)
        s0 = at + SLOT0["hgrn"]
        w[s0:s0 + HH] = np.stack([blocks(hq), blocks(hf)], 2).reshape(P, HH, SLOT).transpose(1, 0, 2)
        gates = blocks(gl).reshape(P, N_SUB, KT, KT, P).transpose(0, 2, 1, 3, 4)
        gates = gates.reshape(P, 12, SLOT)
        branches = np.concatenate([blocks(a["w_ba"][l]), blocks(a["w_bb"][l]), blocks(a["w_bc"][l])], 2)
        branches = branches.reshape(P, 4, SLOT)
        s0 = at + SLOT0["merge"]
        for r in range(4):
            for q in range(3):
                w[s0 + 4 * r + q] = gates[:, 3 * r + q]
            w[s0 + 4 * r + 3] = branches[:, r]
        s0 = at + SLOT0["out"]
        w[s0:s0 + 4] = per_slot(blocks(a["w_out"][l]), 2)

    ada = np.concatenate([per_slot(blocks(a["ada_w"][l]), 2) for l in range(DEPTH)])
    tokens = np.concatenate([a["x_prompt"][0], a["x_sample"][:, 0]])
    pool_w = np.zeros((DEPTH, P, 2, P), np.float32)
    for g in range(4):
        half = slice((g % 2) * POOL_G, (g % 2 + 1) * POOL_G)
        pool_w[:, half, g // 2, half] = a["pool_w"][:, g]
    gamma = np.ones((DEPTH, ROT, HD), np.float32)
    gamma[:, 0:8] = a["q_norm"][:, None]
    gamma[:, 8:10] = a["k_norm"][:, None]
    n_phys = a["cache_k"].shape[1]
    arrays = {
        "w": w,
        "ada": ada,
        "x": tokens.T.reshape(KT, P, COLS).transpose(1, 0, 2),
        "cond": np.concatenate([a["c_prompt"], a["c_sample"]]).T.reshape(KT, P, CC).transpose(1, 0, 2),
        "ada_b": a["ada_b"].reshape(DEPTH * N_SUB, 24, P).transpose(2, 0, 1),
        "norm_g": a["norm_g"].reshape(DEPTH * N_SUB, KT, P).transpose(2, 0, 1),
        "hgrn_lb": a["hgrn_lb"].reshape(DEPTH, HH, P).transpose(2, 0, 1),
        "hgrn_onorm": a["hgrn_onorm"],
        "pool_scale": a["pool_scale"].reshape(DEPTH, 2, P).transpose(2, 0, 1),
        "pool_w": pool_w,
        "gamma": gamma,
        "page_table": a["page_table"].reshape(1, NB * PAGES),
        "cache_k": a["cache_k"].reshape(DEPTH, n_phys, P, P),
        "cache_v": a["cache_v"].reshape(DEPTH, n_phys, P, P),
        "cache_ki": a["cache_ki"],
        "state_pool": a["state_pool"].reshape(DEPTH, NB * POOL_STATE, 256),
        "state_hgrn": a["state_hgrn"].transpose(0, 3, 1, 2, 4).reshape(DEPTH, P, NB * HIW),
    }
    arrays.update(constants())
    arrays = {k: np.ascontiguousarray(v) for k, v in arrays.items()}
    outputs = {
        "y": (P, KT, COLS),
        "k_out": (DEPTH, P, TT + 1, NKV * HD),
        "v_out": (DEPTH, P, TT + 1, NKV * HD),
        "ki_out": (DEPTH, P, TT + 1, HD),
        "pool_p": (DEPTH, POOL_STATE, 256),
        "pool_s": (DEPTH, NB, POOL_STATE, 256),
        "hgrn_p": (DEPTH, P, HH, HV),
        "hgrn_s": (DEPTH, P, NB * HIW),
    }
    nc = bacc.Bacc("TRN2", target_bir_lowering=False, num_devices=1)
    d = {}
    for k, v in arrays.items():
        d[k] = nc.dram_tensor(f"in_{k}", v.shape, mybir.dt.from_np(v.dtype), kind="ExternalInput").ap()
    for k, shape in outputs.items():
        d[k] = nc.dram_tensor(f"out_{k}", shape, F32, kind="ExternalOutput").ap()
    build(nc, d)
    res = run_bass_kernel_spmd(nc, [{f"in_{k}": v for k, v in arrays.items()}], core_ids=[0])
    o = {k: np.asarray(res.results[0][f"out_{k}"]) for k in outputs}

    y = o["y"].transpose(2, 1, 0).reshape(COLS, D_MODEL)

    def tokens_of(t):
        n = t.shape[-1]
        return (t[:, :, 0:TT].transpose(0, 2, 1, 3).reshape(DEPTH, 1, SEQ, n),
                t[:, 0:NB, TT].reshape(DEPTH, NB, 1, n))

    k_p, k_s = tokens_of(o["k_out"])
    v_p, v_s = tokens_of(o["v_out"])
    ki_p, ki_s = tokens_of(o["ki_out"])
    heads = (NKV, HD)
    hgrn_s = o["hgrn_s"].reshape(DEPTH, P, NB, HH, HV).transpose(0, 2, 3, 1, 4)
    c = np.ascontiguousarray
    return (c(y[0:SEQ][None]), c(y[SEQ:][:, None]),
            c(k_p.reshape(DEPTH, 1, SEQ, *heads)), c(v_p.reshape(DEPTH, 1, SEQ, *heads)), c(ki_p),
            c(o["pool_p"][:, None]), c(o["hgrn_p"].transpose(0, 2, 1, 3)[:, None]),
            c(k_s.reshape(DEPTH, NB, 1, *heads)), c(v_s.reshape(DEPTH, NB, 1, *heads)), c(ki_s),
            c(o["pool_s"]), c(hgrn_s))
```

```python
import numpy as np
import concourse.bass as bass
from concourse import mybir
from contextlib import ExitStack

F32 = mybir.dt.float32
F32R = mybir.dt.float32r
U32 = mybir.dt.uint32
I32 = mybir.dt.int32
ACT = mybir.ActivationFunctionType
ALU = mybir.AluOpType
AX = mybir.AxisListType

P = 128
DEPTH = 2
D_MODEL = 1024
KT = D_MODEL // P
SEQ = 512
NB = 8
COLS = SEQ + NB
HALF = COLS // 2
TT = SEQ // P
D_FF = 2816
UP = (12, 10)
assert sum(UP) * P == D_FF
N_SUB = 3
POOL_WINDOWS = (2, 4, 8, 16)
POOL_G = 64
POOL_STATE = 15
HH, HK, HV = 4, 128, 64
HIW = HH * HV
NH, NKV, HD = 8, 2, 64
IDXH = 4
PAST = 256
PAGES = 2
LVIS = PAST + 1
TOP_PROMPT = 128
TOP_SAMPLE = LVIS // 4
ROPE_THETA = 10000.0
ATTN_SCALE = HD ** -0.5
IDX_SCALE = (HD * IDXH) ** -0.5
NEG_BIG = -1e30
TAKEN = -3e38
EPS = 1e-6
F_FLOOR = 1e-30
PRIMED = 1
SLOT = 2048
ROT = 15
CC = 1 + NB

SEGMENTS = []
for _f in (0, 1):
    _ffn = []
    for _h, _n in enumerate(UP):
        _ffn += [(f"up{_f}{_h}", _n, SLOT), (f"down{_f}{_h}", KT, _n * P)]
    SEGMENTS += _ffn
    if _f == 0:
        SEGMENTS += [("token", 8, SLOT), ("hgrn", 4, SLOT), ("merge", 16, SLOT), ("out", 4, SLOT)]
SLOT0, _at = {}, 0
for _name, _n, _ in SEGMENTS:
    SLOT0[_name] = _at
    _at += _n
LAYER_SLOTS = _at
USED = {name: used for name, _, used in SEGMENTS}
SLOTS = {name: n for name, n, _ in SEGMENTS}
ADA_CHUNKS = 4
ADA_N = 384
ADA_SLOTS = 2 * KT
ADA_Q = ADA_N // P

MAIN0, _at = {}, 0
for _name, _n in [("up00", 4 * UP[0]), ("down00", 2 * KT), ("up01", 4 * UP[1]), ("down01", 2 * KT),
                  ("token", 24), ("hgrn", 16), ("merge", 96), ("out", 16),
                  ("up10", 4 * UP[0]), ("down10", 2 * KT), ("up11", 4 * UP[1]), ("down11", 2 * KT)]:
    assert _at % 4 == 0
    MAIN0[_name] = _at
    _at += _n
LAYER_MAIN = _at


def slot_end(stage, s):
    if stage == "merge":
        return 24 * (s // 4) + (4, 8, 12, 24)[s % 4]
    return (s + 1) * {"do": 2, "to": 3}.get(stage[:2], 4)


LEVELS = (0, 1, 2, 4, 8, 16, 32, 64)


INDEX_USES = IDXH * TT
PAIRS = HH * (len(LEVELS) + 1)
Y_HEADS = 4 + 3 + TT
STORES = 8
X_TILES = 5 * KT
SQUARES = 2 * KT - 1


def x_updates(sub):
    return X_TILES * (sub // N_SUB) + (0, 2 * KT, 3 * KT)[sub % N_SUB]


def mixer_adas(l):
    return [sub for sub in (N_SUB * l + 2, N_SUB * l + 3) if sub < DEPTH * N_SUB]


def side_order():
    keys = []
    for l in range(DEPTH):
        keys += [(l, "norm", 0, h) for h in (0, 1)] + [(l, "norm", 1, h) for h in (0, 1)]
        keys += [(l, "pooled", c) for c in (0, 1, 2)]
        keys += [(l, "ya", c, h) for c in (0, 1) for h in (0, 1)]
        keys += [(l, "rotT", t, part) for t in range(TT + 1) for part in (0, 1)]
        for hd in range(HH):
            keys.append((l, "level", hd, LEVELS[0]))
            if hd > 0:
                keys.append((l, "o", hd - 1))
            keys += [(l, "level", hd, lv) for lv in LEVELS[1:]]
            keys += [(l, "kbT", hd), (l, "delta", hd)]
        keys.append((l, "o", HH - 1))
        keys += [(l, "i_bcast", j) for j in range(4)] + [(l, "o_sample",)]
        keys += [(l, "ybT", c) for c in (0, 1, 2)]
        keys += [(l, "index", 0, h) for h in range(IDXH)]
        for t in range(TT):
            if t + 1 < TT:
                keys += [(l, "index", t + 1, h) for h in range(IDXH)]
            for kind, h in attention_order():
                keys.append((l, kind, t, h))
            keys.append((l, "ycT", t))
        keys += [(l, "kiT_page", j) for j in range(2)] + [(l, "s_index",), (l, "s_wsel",), (l, "s_score",)]
        keys += [(l, "kT_page", j) for j in range(4)] + [(l, "s_logits",)]
        keys += [(l, "s_probT",), (l, "s_o",), (l, "s_oT",)]
        keys += [(l, "norm", 2, h) for h in (0, 1)]
    return keys


def attention_order():
    order = []
    for h in range(NH + 2):
        if h < NH:
            order.append(("logits", h))
        if 1 <= h <= NH:
            order.append(("probT", h - 1))
        if h >= 3 and h % 2 == 1:
            order.append(("pv", (h - 3) // 2))
    return order


SIDE = {key: n for n, key in enumerate(side_order())}


def constants():
    c = {}
    c["ident"] = np.eye(P, dtype=np.float32)
    s = np.arange(P)[:, None]
    t = np.arange(P)[None, :]
    levels = [(s == t)]
    for h in LEVELS[1:]:
        levels.append((s // (2 * h) == t // (2 * h)) & (s // h % 2 == 0) & (t // h % 2 == 1))
    c["levels"] = np.stack([m.astype(np.float32) for m in levels], 1)
    c["causal"] = np.concatenate([np.zeros((P, 3 * P)), np.where(t <= s, 0.0, NEG_BIG)], 1).astype(np.float32)
    win = np.zeros((P, 3, 4, P), np.float32)
    for g, w in enumerate(POOL_WINDOWS):
        inside = (s <= t) & (s > t - w)
        win[:, 0, g] = inside / np.float32(w) - (s == t)
        win[:, 1, g] = inside / np.minimum(t + 1, w).astype(np.float32) - (s == t)
        win[:, 2, g] = (s - P > t - w) / np.float32(w)
    c["windows"] = win
    past = np.zeros((NB, POOL_STATE, 4, NB), np.float32)
    own = np.zeros((NB, 4, NB), np.float32)
    for g, w in enumerate(POOL_WINDOWS):
        for b in range(NB):
            past[b, POOL_STATE - (w - 1):, g, b] = 1.0 / w
            own[b, g, b] = 1.0 / w - 1.0
    c["windows_past"] = past.reshape(NB * POOL_STATE, 4, NB)
    c["windows_own"] = own
    half = HD // 2
    inv = np.power(np.float32(ROPE_THETA), -np.arange(half, dtype=np.float32) / np.float32(half)).astype(np.float32)
    pos = np.concatenate([np.arange(SEQ), np.full(P, PAST)]).astype(np.float32)
    ang = (pos[:, None] * inv[None, :]).astype(np.float32)
    cos, sin = np.cos(ang), np.sin(ang)
    rope = np.stack([np.concatenate([cos, cos], 1), np.concatenate([-sin, sin], 1)], 1)
    c["rope"] = rope.reshape(TT + 1, P, 2, HD).transpose(1, 0, 2, 3).astype(np.float32)
    row = np.zeros((NB, NB, P), np.float32)
    row[np.arange(NB), np.arange(NB)] = 1.0
    c["row_select"] = row
    col = np.zeros((P, 2 * NB - 1), np.float32)
    col[:, NB - 1] = 1.0
    c["col_select"] = col
    sel = np.zeros((ADA_CHUNKS, 32, ADA_CHUNKS, CC), np.float32)
    for j in range(ADA_CHUNKS):
        sel[j, np.arange(CC), j, np.arange(CC)] = 1.0
    c["ada_select"] = sel.reshape(P, ADA_CHUNKS, CC)
    c["spread_idx"] = np.repeat(np.eye(NB, dtype=np.float32), IDXH, 1)
    c["spread_heads"] = np.repeat(np.eye(NB, dtype=np.float32), NH, 1)
    c["gather_heads"] = np.ascontiguousarray(c["spread_heads"].T)
    return {k: np.ascontiguousarray(v, dtype=np.float32) for k, v in c.items()}


def build(nc, d):
    ctx = ExitStack()
    with ctx:
        cursor = [16512]

        def sb(name, shape, dt=F32, at=None):
            size = 4 * int(np.prod(shape[1:]))
            if at is None:
                at = cursor[0]
                cursor[0] += -(-size // 32) * 32
            assert at + size <= 229368, (name, at + size)
            return nc.alloc_sbuf_tensor_at(name, list(shape), dt, offset=at)

        x = sb("x", [P, KT, COLS])
        h_hi = sb("h_hi", [P, KT, SEQ + P], F32R)
        h_lo = sb("h_lo", [P, KT, SEQ + P], F32R)
        raw = [sb(f"raw{j}", [P, SLOT]) for j in range(2)]
        w_hi = [sb(f"w_hi{j}", [P, SLOT], F32R) for j in range(2)]
        w_lo = [sb(f"w_lo{j}", [P, SLOT], F32R) for j in range(2)]
        ada_w = [sb(f"ada_w{j}", [P, ADA_CHUNKS, ADA_N]) for j in range(2)]
        ada_row = sb("ada_row", [P, ADA_N])
        mod = [sb(f"mod{j}", [P, 24, CC]) for j in range(N_SUB)]
        ada_select = sb("ada_select", [P, ADA_CHUNKS, CC])
        ada_b = sb("ada_b", [P, DEPTH * N_SUB, 24])
        norm_g = sb("norm_g", [P, DEPTH * N_SUB, KT])
        cond = sb("cond", [P, KT, CC])
        ident = sb("ident", [P, P])
        ones = sb("ones", [P, P])
        lb = sb("lb", [P, DEPTH, HH])
        lb_rest = sb("lb_rest", [P, DEPTH, HH])
        lb_tmp = sb("lb_tmp", [P, 4, HH])
        onorm = sb("onorm", [P, DEPTH, HV])
        pool_scale = sb("pool_scale", [P, DEPTH, 2])
        col_select = sb("col_select", [P, 2 * NB - 1])
        spread_idx = sb("spread_idx", [NB, NB, IDXH])
        spread_heads = sb("spread_heads", [NB, NB * NH])
        gather_heads = sb("gather_heads", [NB * NH, NB])
        page_ids = sb("page_ids", [1, NB * PAGES], I32)
        x_tmp = sb("x_tmp", [P, NB])
        base = cursor[0]

        def area(name, shape, at, dt=F32):
            return sb(name, shape, dt, base + at)

        mid_hi = area("mid_hi", [P, UP[0], COLS], 0, F32R)
        mid_lo = area("mid_lo", [P, UP[0], COLS], 24960, F32R)
        silu_g = area("silu_g", [P, 2, HALF], 49920)
        prod = area("prod", [P, 2, HALF], 52000)
        sq = area("sq", [P, COLS], 66560)
        sq_sum = area("sq_sum", [P, COLS], 68640)
        scaled = area("scaled", [P, KT, SEQ], 16640)
        ms = area("ms", [P, COLS], 33024)
        root = area("root", [P, COLS], 35104)
        newton = area("newton", [P, COLS], 37184)
        rstd = area("rstd", [P, COLS], 39264)
        h_s = area("h_s", [P, KT, NB], 41344)
        yab_hi = area("yab_hi", [P, 4, COLS], 0, F32R)
        yab_lo = area("yab_lo", [P, 4, COLS], 8320, F32R)
        yc_hi = area("yc_hi", [P, 4, COLS], 16640, F32R)
        yc_lo = area("yc_lo", [P, 4, COLS], 24960, F32R)
        gamma = area("gamma", [P, ROT, HD], 4160)
        rope = area("rope", [P, TT + 1, 2, HD], 12480)
        rot = area("rot", [P, TT + 1, ROT, HD], 16640)
        vals = area("vals", [P, TT + 1, NKV * HD], 35840)
        wi = area("wi", [P, TT + 1, IDXH], 38400)
        rotT = area("rotT", [P, 8, COLS], 38528)
        h_i = area("h_i", [P, TT + 1, HIW], 55168)
        h_g = area("h_g", [P, TT + 1, HIW], 60288)
        pool_u = area("pool_u", [P, TT + 1, 256], 65408)
        windows = area("windows", [P, 3, 4, P], 70528)
        pooled = area("pooled", [P, 2, COLS], 76672)
        pool_past = area("pool_past", [NB * POOL_STATE, 256], 80832)
        pool_w = area("pool_w", [P, 2, P], 81856)
        windows_past = area("windows_past", [NB * POOL_STATE, 4, NB], 82880)
        windows_own = area("windows_own", [NB, 4, NB], 83008)
        rot_a = area("rot_a", [P, ROT, HD], 65408)
        rot_b = area("rot_b", [P, ROT, HD], 69248)
        rot_ms = area("rot_ms", [P, 4, TT + 1, ROT], 83200)
        hq = [area(f"hq{j}", [P, COLS], (16640, 33536)[j]) for j in range(2)]
        hf = area("hf", [P, COLS], 18720)
        hk = area("hk", [P, COLS], 20800)
        pre = area("pre", [P, SEQ], 22880)
        suf = area("suf", [P, SEQ], 24928)
        att = area("att", [P, TT, P], 26976)
        kbT = area("kbT", [P, TT, P], 29024)
        chain = area("chain", [P, TT, HV], 31072)
        qm = [area(f"qm{j}", [P, SEQ], 65408 + 2048 * j) for j in range(2)]
        km = [area(f"km{j}", [P, SEQ], 69504 + 2048 * j) for j in range(2)]
        h_o = area("h_o", [P, TT + 1, HH, HV], 73600)
        levels = area("levels", [P, len(LEVELS), P], 78720)
        f_s = area("f_s", [P, HH, NB], 82816)
        k_s = area("k_s", [P, HH, NB], 82944)
        q_s = area("q_s", [P, HH, NB], 83072)
        decay = area("decay", [P, TT], 84224)
        state_p = area("state_p", [P, HH, HV], 83200)
        state_in = area("state_in", [P, NB, HH, HV], 16640)
        state_s = area("state_s", [P, NB, HH, HV], 24832)
        state_q = area("state_q", [P, NB, HH, HV], 65408)
        row_select = area("row_select", [NB, NB, P], 78720)
        o_sq = area("o_sq", [P, TT + 1, HH, HV], 65408)
        o_ms = area("o_ms", [P, 4, TT + 1, HH], 82816)
        rel = [area(f"rel{j}", [P, SEQ], 55168 + 2048 * j) for j in range(2)]
        score = area("score", [P, SEQ], 59264)
        work = area("work", [P, SEQ], 61312)
        mask = [area(f"mask{j}", [P, SEQ], 63360 + 2048 * j) for j in range(2)]
        probs = [area(f"probs{j}", [P, SEQ], 67456 + 2048 * j) for j in range(2)]
        probT = [area(f"probT{j}", [P, TT, P], 71552 + 2048 * j) for j in range(4)]
        o_tok = area("o_tok", [P, NH, HD], 79744)
        causal = area("causal", [P, SEQ], 81792)
        top8 = area("top8", [P, 8], 83840)
        row_max = area("row_max", [P, NH], 83872)
        neg_max = area("neg_max", [P, NH], 83904)
        row_sum = area("row_sum", [P, NH], 83936)
        row_inv = area("row_inv", [P, NH], 83968)
        k_page = area("k_page", [P, NB, PAGES, P], 38528)
        v_page = area("v_page", [P, NB, PAGES, P], 46720)
        ki_page = area("ki_page", [P, NB, PAGES, HD], 55168)
        kT_s = area("kT_s", [P, NB, LVIS], 59264)
        kiT_s = area("kiT_s", [HD, NB, LVIS], 67488)
        q_blk = area("q_blk", [P, NB, NB, NKV, 4], 75712)
        qi_blk = area("qi_blk", [HD, NB, NB, IDXH], 77760)
        prob_s = area("prob_s", [NB * NH, LVIS], 78784)
        rel_s = area("rel_s", [NB * IDXH, LVIS], 78784)
        score_s = area("score_s", [NB, LVIS], 79840)
        work_s = area("work_s", [NB, LVIS], 80896)
        mask_s = area("mask_s", [NB, LVIS], 81952)
        probT_blk = area("probT_blk", [P, PAGES, NB, NB * NH], 79840)
        rotT_s = area("rotT_s", [P, 8, NB], 33280)
        top8_s = area("top8_s", [NB, 8], 84192)
        st_s = area("st_s", [NB * NH, 4], 84224)
        wi_exp = area("wi_exp", [NB, NB, IDXH], 83008)
        wi_sel = area("wi_sel", [NB * IDXH, NB], 84256)
        own_diag = area("own_diag", [NB * NH, NB * NH], 75712)
        own_prob = area("own_prob", [NB, NB * NH], 75968)
        o_s = area("o_s", [NB * NH, P], 76224)
        mrg_hi = area("mrg_hi", [P, KT, COLS], 33280, F32R)
        mrg_lo = area("mrg_lo", [P, KT, COLS], 49920, F32R)
        gate_s = area("gate_s", [P, 6, COLS], 66560)
        part = area("part", [P, 3, HALF], 79040)

        bank = [ctx.enter_context(nc.psum_tensor(f"bank{b}", [P, 512], F32)) for b in range(8)]
        ada_bank = bank[7]

        def sem(name):
            return ctx.enter_context(nc.semaphore(name))

        const_loaded = sem("const_loaded")
        x_loaded = sem("x_loaded")
        w_loaded = [sem(f"w_loaded{j}") for j in range(2)]
        head_split = [sem(f"head_split{j}") for j in range(2)]
        w_split = [sem(f"w_split{j}") for j in range(2)]
        ada_loaded = [sem(f"ada_loaded{j}") for j in range(2)]
        ada_used = [sem(f"ada_used{j}") for j in range(2)]
        ada_taken0 = sem("ada_taken0")
        ada_row_ready = sem("ada_row_ready")
        ada_turned = sem("ada_turned")
        ada_taken = sem("ada_taken")
        main_full = sem("main_full")
        main_taken = [sem(f"main_taken{b}") for b in range(4)]
        side_full = sem("side_full")
        side_taken = [sem(f"side_taken{b}") for b in range(3)]
        setup_done = sem("setup_done")
        cond_ready = sem("cond_ready")
        lb_exp = sem("lb_exp")
        x_updated = sem("x_updated")
        squared = sem("squared")
        root_ready = sem("root_ready")
        ms_ready = sem("ms_ready")
        scaled_ready = sem("scaled_ready")
        h_hi_ready = sem("h_hi_ready")
        h_lo_ready = sem("h_lo_ready")
        mid_hi_ready = sem("mid_hi_ready")
        mid_lo_ready = sem("mid_lo_ready")
        pool_loaded = sem("pool_loaded")
        rope_loaded = sem("rope_loaded")
        rotated = sem("rotated")
        stored = sem("stored")
        y_hi_ready = sem("y_hi_ready")
        levels_loaded = sem("levels_loaded")
        pair_ready = sem("pair_ready")
        hf_used = sem("hf_used")
        chain_ready = sem("chain_ready")
        state_loaded = sem("state_loaded")
        state_ready = sem("state_ready")
        state_q_ready = sem("state_q_ready")
        yb_ready = sem("yb_ready")
        index_used = sem("index_used")
        causal_loaded = sem("causal_loaded")
        neg_max_ready = sem("neg_max_ready")
        probs_ready = sem("probs_ready")
        o_tok_ready = sem("o_tok_ready")
        rotT_copied = sem("rotT_copied")
        ki_loaded = sem("ki_loaded")
        k_loaded = sem("k_loaded")
        v_loaded = sem("v_loaded")
        q_blk_ready = sem("q_blk_ready")
        wi_exp_ready = sem("wi_exp_ready")
        mask_s_ready = sem("mask_s_ready")
        s_neg_ready = sem("s_neg_ready")
        s_probs_ready = sem("s_probs_ready")
        own_diag_ready = sem("own_diag_ready")
        blk_ready = sem("blk_ready")
        mrg_ready = sem("mrg_ready")
        mrg_hi_ready = sem("mrg_hi_ready")
        mrg_lo_ready = sem("mrg_lo_ready")
        vector_step = sem("vector_step")
        scalar_step = sem("scalar_step")
        table_ids = sem("table_ids")

        primed = main_taken + w_split + ada_used + [mrg_ready]

        def main_unit(l, stage, n=0):
            return LAYER_MAIN * l + MAIN0[stage] + n

        def side_unit(*key):
            n = SIDE[key]
            return n, n % 3, n // 3

        def wait_main(eng, unit):
            eng.wait_ge(main_full, unit + 1)

        def wait_side(eng, *key):
            n, b, _ = side_unit(*key)
            eng.wait_ge(side_full, n + 1)
            return bank[4 + b], side_taken[b]

        def wait_side_taken(eng, *key):
            n, b, use = side_unit(*key)
            eng.wait_ge(side_taken[b], use + 1)

        def main_use(l, stage, r=0):
            return (LAYER_MAIN * l + MAIN0[stage]) // 4 + r

        def slot_use(l, stage, r=0):
            return (LAYER_SLOTS * l + SLOT0[stage]) // 2 + r

        class Chain:

            def __init__(self, eng, semaphore):
                self.eng, self.sem, self.n, self.extra = eng, semaphore, 0, 0

            def link(self, ins):
                ins.then_inc(self.sem, 1)
                self.n += 1
                self.eng.wait_ge(self.sem, self.n + self.extra)

            def loop(self, i, per, count):
                self.extra = i * per
                self.per, self.count, self.start = per, count, self.n

            def end(self):
                assert self.n - self.start == self.per, (self.n - self.start, self.per)
                self.n = self.start + self.per * self.count
                self.extra = 0

        def half(hf):
            return slice(hf * HALF, (hf + 1) * HALF)

        def newton_rsqrt(chain_, mean, rt, tmp, out):
            v = nc.vector
            chain_.link(v.reciprocal(rt, rt))
            chain_.link(v.tensor_tensor(tmp, rt, rt, ALU.mult))
            chain_.link(v.scalar_tensor_tensor(out=tmp, in0=tmp, scalar=-0.5, in1=mean, op0=ALU.mult, op1=ALU.mult))
            chain_.link(v.scalar_tensor_tensor(out=out, in0=tmp, scalar=1.5, in1=rt, op0=ALU.add, op1=ALU.mult))

        block = ctx.enter_context(nc.Block())

        @block.sync
        def _(sp):
            sp.dma_start(cond[:], d["cond"]).then_inc(const_loaded, 16)
            for k in range(2):
                sp.dma_start(x[:, 4 * k:4 * k + 4, :], d["x"][:, 4 * k:4 * k + 4, :]).then_inc(x_loaded, 16)
            for name, tile in (("ada_b", ada_b), ("norm_g", norm_g), ("ident", ident), ("hgrn_lb", lb),
                               ("pool_scale", pool_scale), ("col_select", col_select),
                               ("spread_idx", spread_idx), ("spread_heads", spread_heads),
                               ("gather_heads", gather_heads), ("page_table", page_ids),
                               ("ada_select", ada_select)):
                src = d[name]
                if name == "spread_idx":
                    src = src.rearrange("b (c h) -> b c h", h=IDXH)
                sp.dma_start(tile[:], src).then_inc(const_loaded, 16)
            sp.dma_start(onorm[:], d["hgrn_onorm"].partition_broadcast(P)).then_inc(const_loaded, 16)

            def load_ada(sub, r, j):
                use = sub * (ADA_SLOTS // 2) + r
                sp.wait_ge(ada_used[j], use + PRIMED)
                sp.dma_start(ada_w[j][:].rearrange("p a n -> p (a n)"),
                             d["ada"][bass.ds(sub * ADA_SLOTS + 2 * r + j, 1)].rearrange("o p n -> p (o n)"))\
                  .then_inc(ada_loaded[j], 16)

            def load_w(l, stage, r, j):
                use = slot_use(l, stage, r)
                sp.wait_ge(w_split[j], use + PRIMED)
                n = USED[stage]
                sp.dma_start(raw[j][:, 0:n],
                             d["w"][bass.ds(l * LAYER_SLOTS + SLOT0[stage] + 2 * r + j, 1), :, 0:n]
                             .rearrange("o p n -> p (o n)")).then_inc(w_loaded[j], 16)

            with sp.Fori(0, ADA_SLOTS // 2) as r:
                for j in range(2):
                    load_ada(0, r, j)

            sp.wait_ge(const_loaded, 16 * 13)
            pages = [sp.value_load(page_ids[0:1, n:n + 1], min_val=0, max_val=d["cache_k"].shape[1] - 1)
                     for n in range(NB * PAGES)]

            def load_pages(l, dst, src, loaded):
                for n, page in enumerate(pages):
                    sp.dma_start(dst[:, n // PAGES, n % PAGES, :],
                                 src[l, bass.ds(page, 1)].rearrange("o p n -> p (o n)")).then_inc(loaded, 16)

            for l in range(DEPTH):
                for stage, slots, _ in SEGMENTS:
                    ada = {"down00": 0, "down01": ADA_SLOTS // 4}.get(stage)
                    early = 0
                    if stage == "merge":
                        early = 1
                        for j in range(2):
                            load_w(l, stage, 0, j)
                        for sub in mixer_adas(l):
                            with sp.Fori(0, ADA_SLOTS // 2) as r:
                                for j in range(2):
                                    load_ada(sub, r, j)
                            if sub == N_SUB * l + 2:
                                sp.wait_ge(index_used, INDEX_USES * (l + 1))
                                load_pages(l, ki_page, d["cache_ki"], ki_loaded)
                        sp.wait_ge(rotT_copied, l + 1)
                        sp.wait_ge(side_full, SIDE[(l, "logits", TT - 1, NH - 1)] + 1)
                        load_pages(l, k_page, d["cache_k"], k_loaded)
                        load_pages(l, v_page, d["cache_v"], v_loaded)
                    with sp.Fori(early, slots // 2) as r:
                        for j in range(2):
                            load_w(l, stage, r, j)
                            if ada is not None:
                                load_ada(N_SUB * l + 1, ada + r, j)
            sp.wait_ge(x_updated, x_updates(DEPTH * N_SUB))
            for k in range(2):
                sp.dma_start(d["y"][:, 4 * k:4 * k + 4, :], x[:, 4 * k:4 * k + 4, :]).then_inc(stored, 16)
            sp.wait_ge(stored, 16 * (2 + DEPTH * STORES))

        @block.gpsimd
        def _(pool):
            for semaphore in primed:
                pool.sem_inc(semaphore, PRIMED)
            pool.memset(ones[:], 1.0).then_inc(setup_done, 1)
            pool.memset(h_hi[:, :, COLS:].bitcast(F32), 0.0).then_inc(setup_done, 1)
            pool.memset(h_lo[:, :, COLS:].bitcast(F32), 0.0).then_inc(setup_done, 1)

            def split(l, stage, r, j):
                n = USED[stage]
                pool.wait_ge(head_split[j], slot_use(l, stage, r) + 1)
                pool.tensor_tensor(w_lo[j][:, 0:n], raw[j][:, 0:n], w_hi[j][:, 0:n].bitcast(F32),
                                   ALU.subtract).then_inc(w_split[j], 1)

            def square(sub, k):
                before = SQUARES * sub + 2 * k - 1
                if sub == 0:
                    if k == 0:
                        pool.wait_ge(x_loaded, 32)
                else:
                    pool.wait_ge(x_updated, x_updates(sub) - KT + k + 1)
                if k == 0:
                    pool.tensor_tensor(sq_sum[:], x[:, 0, :], x[:, 0, :], ALU.mult).then_inc(squared, 1)
                else:
                    pool.wait_ge(squared, before)
                    pool.tensor_tensor(sq[:], x[:, k, :], x[:, k, :], ALU.mult).then_inc(squared, 1)
                    pool.wait_ge(squared, before + 1)
                    pool.tensor_tensor(sq_sum[:], sq_sum[:], sq[:], ALU.add).then_inc(squared, 1)

            for k in range(KT):
                square(0, k)
            for l in range(DEPTH):
                for stage, slots, _ in SEGMENTS:
                    sub = N_SUB * l + {"down01": 1, "out": 2, "down11": 3}.get(stage, 0)
                    if sub == N_SUB * l or sub == N_SUB * DEPTH:
                        with pool.Fori(0, slots // 2) as r:
                            for j in range(2):
                                split(l, stage, r, j)
                        continue
                    per = KT // slots
                    for slot in range(slots + 2):
                        if slot < slots:
                            split(l, stage, slot // 2, slot % 2)
                        for k in range(per * (slot - 2), per * (slot - 1)):
                            if k >= 0:
                                square(sub, k)

        @block.scalar
        def _(act):
            steps = Chain(act, scalar_step)
            s = nc.scalar
            load_sp = act.dma_start

            act.wait_ge(const_loaded, 16 * 13)
            s.activation(cond[:], cond[:], ACT.Silu).then_inc(cond_ready, 1)
            act.wait_ge(lb_exp, 1)
            s.activation(lb_tmp[:, 0:2, :], lb_tmp[:, 0:2, :], ACT.Exp).then_inc(lb_exp, 1)

            def head(l, stage, r, j, filled):
                act.wait_ge(w_loaded[j], 16 * (slot_use(l, stage, r) + 1))
                if filled is not None:
                    act.wait_ge(main_full, filled)
                n = USED[stage]
                s.copy(w_hi[j][:, 0:n], raw[j][:, 0:n]).then_inc(head_split[j], 1)

            stages = [(l, name, n) for l in range(DEPTH) for name, n, _ in SEGMENTS]

            def head_after(l, stage, slot):
                filled = LAYER_MAIN * l + MAIN0[stage] + slot_end(stage, slot)
                at = [i for i, (l_, name, _) in enumerate(stages) if (l_, name) == (l, stage)][0]
                ahead = slot + 2
                if ahead >= stages[at][2]:
                    ahead -= stages[at][2]
                    at += 1
                if at < len(stages):
                    head(stages[at][0], stages[at][1], ahead // 2, ahead % 2, filled)

            def down(l, stage):
                first = LAYER_MAIN * l + MAIN0[stage]
                per = slot_end(stage, 0)
                with act.Fori(0, SLOTS[stage] // 2 - 1) as r:
                    for j in range(2):
                        head(l, stage, r + 1, j, first + per * (2 * r + j + 1))
                for slot in (SLOTS[stage] - 2, SLOTS[stage] - 1):
                    head_after(l, stage, slot)

            def ffn_up(l, stage, tiles):
                first = LAYER_MAIN * l + MAIN0[stage]

                def turn(r, last):
                    for j in range(2):
                        for hf in range(2):
                            use = main_use(l, stage, 2 * r + j)
                            wait_main(act, main_unit(l, stage, 8 * r + 4 * j + 2 * hf))
                            act.wait_ge(main_taken[2 * hf + 1], use + PRIMED)
                            s.activation(silu_g[:, hf, :], bank[2 * hf][:, 0:HALF], ACT.Silu)\
                             .then_inc(main_taken[2 * hf], 1)
                            act.wait_ge(main_taken[2 * hf + 1], use + 1 + PRIMED)
                            s.copy(mid_hi[:, bass.ds(2 * r + j, 1), half(hf)].rearrange("p o n -> p (o n)"),
                                   prod[:, hf, :]).then_inc(mid_hi_ready, 1)
                        if last:
                            head_after(l, stage, 2 * r + j)
                        else:
                            head(l, stage, r + 1, j, first + 4 * (2 * r + j + 1))

                with act.Fori(0, tiles // 2 - 1) as r:
                    turn(r, False)
                turn(tiles // 2 - 1, True)

            def norm(sub):
                l, j3 = divmod(sub, N_SUB)
                md = mod[sub % N_SUB]
                wait_side_taken(act, l, "norm", j3, 0)
                wait_side_taken(act, l, "norm", j3, 1)
                s.activation(root[:], ms[:], ACT.Sqrt).then_inc(root_ready, 1)
                roots[0] += 1
                if j3 == 1:
                    mixer_loads(l)
                act.wait_ge(scaled_ready, 9 * sub + 1)
                s.copy(h_hi[:, :, SEQ:COLS], h_s[:]).then_inc(h_hi_ready, 1)
                for k in range(KT):
                    act.wait_ge(scaled_ready, 9 * sub + 2 + k)
                    s.activation(h_hi[:, k, 0:SEQ], scaled[:, k, :], ACT.Identity,
                                 bias=md[:, k, 0:1]).then_inc(h_hi_ready, 1)

            roots = [0]

            def mixer_loads(l):
                for dst, src in ((windows[:], d["windows"]), (pool_past[:], d["state_pool"][l]),
                                 (pool_w[:], d["pool_w"][l]), (windows_past[:], d["windows_past"]),
                                 (windows_own[:], d["windows_own"])):
                    load_sp(dst, src).then_inc(pool_loaded, 16)
                load_sp(gamma[:], d["gamma"][l].partition_broadcast(P)).then_inc(rope_loaded, 16)
                load_sp(rope[:], d["rope"]).then_inc(rope_loaded, 16)

            def token_major(l):
                heads = {3: slice(0, 8, 2), 4: slice(1, 8, 2), 6: slice(10, 14)}
                for slot in range(8):
                    for u in range(3):
                        n = 3 * slot + u
                        unit = main_unit(l, "token", n)
                        wait_main(act, unit)
                        tl = slice(2 * u, 2 * u + 2) if u < 2 else slice(TT, TT + 1)
                        nt = 2 if u < 2 else 1
                        src = bank[unit % 4][:, 0:256 * nt].rearrange("p (t n) -> p t n", t=nt)
                        done = main_taken[unit % 4]
                        if slot == 0:
                            s.copy(pool_u[:, tl, :], src).then_inc(done, 1)
                        elif slot == 1:
                            s.copy(h_i[:, tl, :], src).then_inc(done, 1)
                        elif slot == 2:
                            s.activation(h_g[:, tl, :], src, ACT.Silu).then_inc(done, 1)
                        elif slot in heads:
                            s.copy(rot[:, tl, heads[slot], :], src.rearrange("p t (h n) -> p t h n", n=HD)).then_inc(done, 1)
                        elif slot == 5:
                            s.copy(rot[:, tl, 8:10, :].rearrange("p t h n -> p t (h n)"), src[:, :, 0:P])
                            s.copy(vals[:, tl, :], src[:, :, P:2 * P]).then_inc(done, 1)
                        else:
                            s.copy(rot[:, tl, 14, :], src[:, :, 0:HD])
                            s.copy(wi[:, tl, :], src[:, :, HD:HD + IDXH]).then_inc(done, 1)
                    head_after(l, "token", slot)

            def last_token_unit(eng, l, n=23):
                unit = main_unit(l, "token", n)
                eng.wait_ge(main_taken[unit % 4], unit // 4 + 1 + PRIMED)

            def pool_branch(l):
                last_token_unit(act, l, 2)
                act.dma_start(d["pool_p"][l], pool_u[P - POOL_STATE:P, TT - 1, :]).then_inc(stored, 16)
                act.dma_start(d["pool_s"][l, :, POOL_STATE - 1, :], pool_u[0:NB, TT, :]).then_inc(stored, 16)
                act.dma_start(d["pool_s"][l, :, 0:POOL_STATE - 1, :],
                              d["state_pool"][l].rearrange("(b j) c -> b j c", j=POOL_STATE)[:, 1:, :])\
                   .then_inc(stored, 16)
                for c in range(2):
                    src, done = wait_side(act, l, "pooled", c)
                    s.copy(pooled[:, c, 0:SEQ], src[:, :]).then_inc(done, 1)
                src, done = wait_side(act, l, "pooled", 2)
                s.copy(pooled[:, :, SEQ:COLS], src[:, 0:2 * NB].rearrange("p (c n) -> p c n", c=2)).then_inc(done, 1)
                for c in range(2):
                    for hf in range(2):
                        src, _ = wait_side(act, l, "ya", c, hf)
                        s.activation(yab_hi[:, c, half(hf)], src[:, 0:HALF], ACT.Copy,
                                     scale=pool_scale[:, l, c:c + 1]).then_inc(y_hi_ready, 1)

            def rotary(l):
                act.wait_ge(ms_ready, 2 * l + 1)
                s.activation(rot_ms[:, 1], rot_ms[:, 0], ACT.Sqrt).then_inc(root_ready, 1)
                act.wait_ge(rotated, 5 * (l + 1))
                act.dma_start(d["k_out"][l], rot[:, :, 8:10, :].rearrange("p t h n -> p t (h n)")).then_inc(stored, 16)
                act.dma_start(d["ki_out"][l], rot[:, :, 14, :]).then_inc(stored, 16)
                act.dma_start(d["v_out"][l], vals[:]).then_inc(stored, 16)
                for t in range(TT + 1):
                    n = P if t < TT else NB
                    for part_ in range(2):
                        src, done = wait_side(act, l, "rotT", t, part_)
                        s.copy(rotT[:, 4 * part_:4 * part_ + 4, t * P:t * P + n],
                               src[:, 0:4 * n].rearrange("p (g n) -> p g n", g=4)).then_inc(done, 1)
                act.wait_ge(stored, 16 * (STORES * l + 6))
                load_sp(levels[:], d["levels"]).then_inc(levels_loaded, 16)

            def hgrn(l):
                def projections(hd):
                    for hf in range(2):
                        wait_main(act, main_unit(l, "hgrn", 4 * hd + hf))
                        s.copy(hq[hd % 2][:, half(hf)], bank[hf][:, 0:HALF]).then_inc(main_taken[hf], 1)
                    if hd > 0:
                        act.wait_ge(hf_used, HH * l + hd)
                    for hf in range(2):
                        wait_main(act, main_unit(l, "hgrn", 4 * hd + 2 + hf))
                        s.activation(hf_t[:, half(hf)], bank[2 + hf][:, 0:HALF], ACT.Sigmoid)\
                         .then_inc(main_taken[2 + hf], 1)
                    head_after(l, "hgrn", hd)

                def outputs(hd):
                    src, done = wait_side(act, l, "o", hd)
                    s.copy(h_o[:, 0:TT, hd, :], src[:, 0:TT * HV].rearrange("p (c n) -> p c n", c=TT)).then_inc(done, 1)

                projections(0)
                for hd in range(HH):
                    if hd > 0:
                        outputs(hd - 1)
                    if hd + 1 < HH:
                        projections(hd + 1)
                    src, done = wait_side(act, l, "kbT", hd)
                    s.copy(kbT[:], src[:, :].rearrange("p (c n) -> p c n", c=TT)).then_inc(done, 1)
                outputs(HH - 1)
                act.wait_ge(chain_ready, HH * (l + 1))
                act.dma_start(d["hgrn_p"][l], state_p[:]).then_inc(stored, 16)
                load_sp(row_select[:], d["row_select"]).then_inc(state_loaded, 16)
                load_sp(state_in[:].rearrange("p b h v -> p (b h v)"), d["state_hgrn"][l]).then_inc(state_loaded, 16)
                src, done = wait_side(act, l, "o_sample")
                s.copy(h_o[0:NB, TT, :, :].rearrange("p h v -> p (h v)"), src[0:NB, 0:HIW]).then_inc(done, 1)
                act.wait_ge(state_ready, l + 1)
                act.dma_start(d["hgrn_s"][l], state_s[:].rearrange("p b h v -> p (b h v)")).then_inc(stored, 16)
                act.wait_ge(ms_ready, 2 * l + 2)
                s.activation(o_ms[:, 1], o_ms[:, 0], ACT.Sqrt).then_inc(root_ready, 1)
                for c in range(3):
                    src, _ = wait_side(act, l, "ybT", c)
                    if c < 2:
                        s.copy(yab_hi[:, 2 + c, 0:SEQ], src[:, :]).then_inc(y_hi_ready, 1)
                    else:
                        s.copy(yab_hi[:, 2:4, SEQ:COLS], src[:, 0:2 * NB].rearrange("p (c n) -> p c n", c=2))\
                         .then_inc(y_hi_ready, 1)

            def prompt_index(l, t):
                nk = (t + 1) * P
                for h in range(IDXH):
                    src, done = wait_side(act, l, "index", t, h)
                    uses = INDEX_USES * l + IDXH * t + h
                    if uses >= 2:
                        act.wait_ge(index_used, uses - 1)
                    s.activation(rel[h % 2][:, 0:nk], src[:, 0:nk], ACT.Relu, scale=IDX_SCALE).then_inc(done, 1)

            def prompt_attention(l, t):
                nk = (t + 1) * P
                for kind, h in attention_order():
                    if kind == "logits":
                        act.wait_ge(neg_max_ready, NH * (TT * l + t) + h + 1)
                        s.activation(probs[h % 2][:, 0:nk], probs[h % 2][:, 0:nk], ACT.Exp, scale=ATTN_SCALE,
                                     bias=neg_max[:, h:h + 1], accum_out=row_sum[:, h:h + 1]).then_inc(probs_ready, 1)
                    elif kind == "probT":
                        src, done = wait_side(act, l, "probT", t, h)
                        s.copy(probT[h % 4][:, 0:t + 1, :],
                               src[:, 0:nk].rearrange("p (b n) -> p b n", b=t + 1)).then_inc(done, 1)
                src, _ = wait_side(act, l, "ycT", t)
                s.copy(yc_hi[:, :, t * P:(t + 1) * P], src[:, :].rearrange("p (c n) -> p c n", c=4)).then_inc(y_hi_ready, 1)

            def sample_attention(l):
                wait_side_taken(act, l, "ycT", TT - 1)
                for j in range(2):
                    src, done = wait_side(act, l, "kiT_page", j)
                    for pg in range(PAGES):
                        last = s.copy(kiT_s[:, 4 * j:4 * j + 4, pg * P:(pg + 1) * P],
                                      src[pg * HD:(pg + 1) * HD, :].rearrange("p (b n) -> p b n", b=4))
                    last.then_inc(done, 1)
                src, done = wait_side(act, l, "s_index")
                s.activation(rel_s[:], src[0:NB * IDXH, 0:LVIS], ACT.Relu, scale=IDX_SCALE).then_inc(done, 1)
                src, done = wait_side(act, l, "s_wsel")
                s.copy(wi_sel[:], src[0:NB * IDXH, 0:NB]).then_inc(done, 1)
                for j in range(4):
                    src, done = wait_side(act, l, "kT_page", j)
                    s.copy(kT_s[:, 2 * j:2 * j + 2, 0:PAST], src[:, :].rearrange("p (b n) -> p b n", b=2)).then_inc(done, 1)
                act.wait_ge(s_neg_ready, l + 1)
                s.activation(prob_s[:], prob_s[:], ACT.Exp, scale=ATTN_SCALE, bias=st_s[:, 1:2],
                             accum_out=st_s[:, 2:3]).then_inc(s_probs_ready, 1)

            def merge(l):
                first = LAYER_MAIN * l + MAIN0["merge"]

                def turn(r, last):
                    def next_head(slot):
                        if last:
                            head_after(l, "merge", 4 * r + slot)
                        else:
                            ahead = slot + 2
                            head(l, "merge", 2 * r + ahead // 2, ahead % 2, first + 24 * r + slot_end("merge", slot))

                    for g in range(12):
                        tile, hf = divmod(g, 2)
                        wait_main(act, main_unit(l, "merge", 24 * r + g))
                        if g == 0:
                            act.wait_ge(mrg_ready, 16 * l + 4 * r + PRIMED)
                        s.activation(gate_s[:, tile, half(hf)], bank[g % 4][:, 0:HALF], ACT.Sigmoid)\
                         .then_inc(main_taken[g % 4], 1)
                        if g % 4 == 3:
                            next_head(g // 4)
                    for n in range(2):
                        for hf in range(2):
                            act.wait_ge(mrg_ready, 16 * l + 4 * r + 2 * n + hf + 1 + PRIMED)
                            s.copy(mrg_hi[:, bass.ds(2 * r + n, 1), half(hf)].rearrange("p o n -> p (o n)"),
                                   part[:, 2, :]).then_inc(mrg_hi_ready, 1)
                    next_head(3)

                with act.Fori(0, 3) as r:
                    turn(r, False)
                turn(3, True)

            hf_t = hf
            for j in range(2):
                head(0, "up00", 0, j, None)
            for l in range(DEPTH):
                norm(N_SUB * l)
                for p_ in range(2):
                    ffn_up(l, f"up0{p_}", UP[p_])
                    down(l, f"down0{p_}")
                norm(N_SUB * l + 1)
                token_major(l)
                pool_branch(l)
                rotary(l)
                hgrn(l)
                wait_side_taken(act, l, "ybT", 2)
                act.wait_ge(stored, 16 * STORES * (l + 1))
                load_sp(causal[:], d["causal"]).then_inc(causal_loaded, 16)
                prompt_index(l, 0)
                for t in range(TT):
                    if t + 1 < TT:
                        prompt_index(l, t + 1)
                    prompt_attention(l, t)
                sample_attention(l)
                merge(l)
                down(l, "out")
                norm(N_SUB * l + 2)
                for p_ in range(2):
                    ffn_up(l, f"up1{p_}", UP[p_])
                    down(l, f"down1{p_}")

        @block.vector
        def _(dve):
            v = nc.vector
            steps = Chain(dve, vector_step)
            link = steps.link

            def bc(ap, shape):
                return ap.to_broadcast(shape)

            dve.wait_ge(const_loaded, 16 * 13)
            link(v.tensor_tensor(lb_tmp[:, 2], lb[:, 0], lb[:, 1], ALU.max))
            link(v.tensor_tensor(lb_tmp[:, 0], lb[:, 0], lb_tmp[:, 2], ALU.subtract))
            v.tensor_tensor(lb_tmp[:, 1], lb[:, 1], lb_tmp[:, 2], ALU.subtract).then_inc(lb_exp, 1)
            dve.wait_ge(lb_exp, 2)
            link(v.tensor_tensor(lb_tmp[:, 2], lb_tmp[:, 0], lb_tmp[:, 1], ALU.add))
            link(v.reciprocal(lb_tmp[:, 3], lb_tmp[:, 2]))
            link(v.tensor_tensor(lb_tmp[:, 0], lb_tmp[:, 0], lb_tmp[:, 3], ALU.mult))
            link(v.tensor_tensor(lb_tmp[:, 1], lb_tmp[:, 1], lb_tmp[:, 3], ALU.mult))
            link(v.tensor_tensor(lb_tmp[:, 1], lb_tmp[:, 0], lb_tmp[:, 1], ALU.add))
            link(v.tensor_tensor(lb[:, 0], lb_tmp[:, 0], lb_tmp[:, 0], ALU.subtract))
            link(v.tensor_tensor(lb[:, 1], lb_tmp[:, 1], lb_tmp[:, 0], ALU.subtract))
            link(v.tensor_scalar(lb_rest[:], lb[:], -1.0, 1.0, ALU.mult, ALU.add))

            def ada_rows(sub, hh):
                dve.wait_ge(ada_used[1], (ADA_SLOTS * sub + KT * (hh + 1)) // 2 + PRIMED)
                v.tensor_copy(ada_row[:], ada_bank[:, 0:ADA_N]).then_inc(ada_row_ready, 1)

            def ada_take(sub, hh):
                dve.wait_ge(ada_turned, 2 * sub + hh + 1)
                src = ada_bank[:, ADA_N:ADA_N + ADA_Q * ADA_CHUNKS * CC]
                tiles = "p (a h q) -> p h q a"
                v.tensor_tensor(mod[sub % N_SUB][:].rearrange("p (a h q) c -> p h q a c", h=2, q=ADA_Q)[:, hh],
                                src.rearrange("p (q a c) -> p q a c", q=ADA_Q, a=ADA_CHUNKS),
                                bc(ada_b[:, sub, :].rearrange(tiles, h=2, q=ADA_Q)[:, hh].unsqueeze(3),
                                   [P, ADA_Q, ADA_CHUNKS, CC]), ALU.add).then_inc(ada_taken, 1)

            def norm(sub):
                l, j3 = divmod(sub, N_SUB)
                md = mod[sub % N_SUB]
                dve.wait_ge(ada_taken, 2 * (sub + 1))
                link(v.scalar_tensor_tensor(out=md[:, 8:16, :], in0=md[:, 8:16, :], scalar=1.0,
                                            in1=bc(norm_g[:, sub, :].unsqueeze(2), [P, KT, CC]),
                                            op0=ALU.add, op1=ALU.mult))
                if j3 != 1:
                    link(v.tensor_scalar(md[:, 16:24, :], md[:, 16:24, :], 0.5, None, ALU.mult))
                for hf in range(2):
                    src, done = wait_side(dve, l, "norm", j3, hf)
                    v.tensor_scalar(ms[:, half(hf)], src[:, 0:HALF], 1.0 / D_MODEL, EPS, ALU.mult, ALU.add)\
                     .then_inc(done, 1)
                dve.wait_ge(root_ready, 5 * l + (1, 2, 5)[j3])
                newton_rsqrt(steps, ms[:], root[:], newton[:], rstd[:])
                link(v.tensor_tensor(h_s[:], x[:, :, SEQ:COLS], md[:, 8:16, 1:CC], ALU.mult))
                link(v.tensor_tensor(h_s[:], h_s[:], bc(rstd[:, SEQ:COLS].unsqueeze(1), [P, KT, NB]), ALU.mult))
                v.tensor_tensor(h_s[:], h_s[:], md[:, 0:8, 1:CC], ALU.add).then_inc(scaled_ready, 1)
                for k in range(KT + 1):
                    if k < KT:
                        v.scalar_tensor_tensor(out=scaled[:, k, :], in0=x[:, k, 0:SEQ], scalar=md[:, 8 + k, 0:1],
                                               in1=rstd[:, 0:SEQ], op0=ALU.mult, op1=ALU.mult)\
                         .then_inc(scaled_ready, 1)
                    if k == 0:
                        dve.wait_ge(h_hi_ready, 9 * sub + 1)
                        dve.wait_ge(scaled_ready, 9 * sub + 1)
                        v.tensor_tensor(h_lo[:, :, SEQ:COLS], h_s[:], h_hi[:, :, SEQ:COLS].bitcast(F32),
                                        ALU.subtract).then_inc(h_lo_ready, 1)
                    else:
                        dve.wait_ge(h_hi_ready, 9 * sub + 1 + k)
                        v.scalar_tensor_tensor(out=h_lo[:, k - 1, 0:SEQ], in0=scaled[:, k - 1, :],
                                               scalar=md[:, k - 1, 0:1], in1=h_hi[:, k - 1, 0:SEQ].bitcast(F32),
                                               op0=ALU.add, op1=ALU.subtract).then_inc(h_lo_ready, 1)

            def ffn_up(l, stage, tiles, count0):
                with dve.Fori(0, tiles // 2) as r:
                    for j in range(2):
                        for hf in range(2):
                            use = main_use(l, stage, 2 * r + j)
                            n = count0 + 4 * r + 2 * j + hf
                            wait_main(dve, main_unit(l, stage, 8 * r + 4 * j + 2 * hf + 1))
                            dve.wait_ge(main_taken[2 * hf], use + 1 + PRIMED)
                            v.tensor_tensor(prod[:, hf, :], silu_g[:, hf, :], bank[2 * hf + 1][:, 0:HALF],
                                            ALU.mult).then_inc(main_taken[2 * hf + 1], 1)
                            dve.wait_ge(main_taken[2 * hf + 1], use + 1 + PRIMED)
                            dve.wait_ge(mid_hi_ready, n + 1)
                            at = bass.ds(2 * r + j, 1)
                            v.tensor_tensor(mid_lo[:, at, half(hf)].rearrange("p o n -> p (o n)"), prod[:, hf, :],
                                            mid_hi[:, at, half(hf)].rearrange("p o n -> p (o n)").bitcast(F32),
                                            ALU.subtract).then_inc(mid_lo_ready, 1)

            def residual(l, stage, sub, per_slot, slots):
                md = mod[sub % N_SUB]
                tiles = per_slot * 2
                x0 = x_updates(sub) + (KT if stage in ("down01", "down11") else 0)
                links = tiles
                with dve.Fori(0, slots // 2) as r:
                    steps.loop(r, links, slots // 2)
                    for n in range(tiles):
                        at = r * tiles + n
                        for hf in range(2):
                            b = (2 * n + hf) % 4
                            wait_main(dve, main_unit(l, stage, 2 * tiles * r + 2 * n + hf))
                            if hf == 0:
                                cols = slice(0, HALF)
                            else:
                                cols = slice(HALF, SEQ)
                                link(v.tensor_tensor(x_tmp[:], bank[b][:, SEQ - HALF:HALF],
                                                     md[:, bass.ds(at + 16, 1), 1:CC].rearrange("p o c -> p (o c)"),
                                                     ALU.mult))
                            xs = x[:, bass.ds(at, 1), cols].rearrange("p o n -> p (o n)")
                            v.scalar_tensor_tensor(out=xs, in0=bank[b][:, 0:cols.stop - cols.start],
                                                   scalar=md[:, bass.ds(at + 16, 1), 0:1].rearrange("p o c -> p (o c)"),
                                                   in1=xs, op0=ALU.mult, op1=ALU.add).then_inc(main_taken[b], 1)
                        xs = x[:, bass.ds(at, 1), SEQ:COLS].rearrange("p o n -> p (o n)")
                        v.tensor_tensor(xs, xs, x_tmp[:], ALU.add).then_inc(x_updated, 1)
                        dve.wait_ge(x_updated, x0 + at + 1)
                    steps.end()

            def rotary(l):
                unit = main_unit(l, "token", 23)
                dve.wait_ge(main_taken[unit % 4], unit // 4 + 1 + PRIMED)
                dve.wait_ge(rope_loaded, 32 * (l + 1))
                for c in range(2):
                    for hf in range(2):
                        wait_side_taken(dve, l, "ya", c, hf)
                dve.wait_ge(stored, 16 * (STORES * l + 3))
                for t in range(TT + 1):
                    buf = (rot_a, rot_b)[t % 2]
                    link(v.tensor_tensor(buf[:], rot[:, t], rot[:, t], ALU.mult))
                    link(v.reduce_sum(rot_ms[:, 0, t, :], buf[:], axis=AX.X))
                v.tensor_scalar(rot_ms[:, 0], rot_ms[:, 0], 1.0 / HD, EPS, ALU.mult, ALU.add).then_inc(ms_ready, 1)
                dve.wait_ge(root_ready, 5 * l + 3)
                dve.wait_ge(ms_ready, 2 * l + 1)
                newton_rsqrt(steps, rot_ms[:, 0], rot_ms[:, 1], rot_ms[:, 2], rot_ms[:, 3])
                link(v.memset(rot_ms[:, 3, :, 10:14], 1.0))
                hw = HD // 2
                for t in range(TT + 1):
                    link(v.tensor_tensor(rot_a[:], rot[:, t], bc(rot_ms[:, 3, t, :].unsqueeze(2), [P, ROT, HD]), ALU.mult))
                    link(v.tensor_tensor(rot_a[:], rot_a[:], gamma[:], ALU.mult))
                    v.tensor_tensor(rot_b[:, :, 0:hw], rot_a[:, :, hw:HD],
                                    bc(rope[:, t, 1, 0:hw].unsqueeze(1), [P, ROT, hw]), ALU.mult)
                    v.tensor_tensor(rot_b[:, :, hw:HD], rot_a[:, :, 0:hw],
                                    bc(rope[:, t, 1, hw:HD].unsqueeze(1), [P, ROT, hw]), ALU.mult)
                    link(v.tensor_tensor(rot[:, t], rot_a[:], bc(rope[:, t, 0, :].unsqueeze(1), [P, ROT, HD]), ALU.mult))
                    v.tensor_tensor(rot[:, t], rot[:, t], rot_b[:], ALU.add).then_inc(rotated, 1)
                    dve.wait_ge(rotated, 5 * l + t + 1)

            def ya_tails(l):
                for c in range(2):
                    for hf in range(2):
                        src, done = wait_side(dve, l, "ya", c, hf)
                        dve.wait_ge(y_hi_ready, Y_HEADS * l + 2 * c + hf + 1)
                        v.scalar_tensor_tensor(out=yab_lo[:, c, half(hf)], in0=src[:, 0:HALF],
                                               scalar=pool_scale[:, l, c:c + 1],
                                               in1=yab_hi[:, c, half(hf)].bitcast(F32),
                                               op0=ALU.mult, op1=ALU.subtract).then_inc(done, 1)

            def hgrn(l):
                wait_side_taken(dve, l, "rotT", TT, 1)
                dve.wait_ge(levels_loaded, 16 * (l + 1))
                v.tensor_copy(rotT_s[:], rotT[:, :, SEQ:COLS]).then_inc(rotT_copied, 1)
                dve.wait_ge(rotT_copied, l + 1)
                link(v.memset(h_o[:, TT], 0.0))
                pairs = [PAIRS * l]
                mixing = LEVELS[1:] + (P,)

                def start(hd):
                    dve.wait_ge(main_taken[1], main_use(l, "hgrn", hd) + 1 + PRIMED)
                    dve.wait_ge(main_taken[3], main_use(l, "hgrn", hd) + 1 + PRIMED)
                    link(v.tensor_scalar(hf[:], hf[:], lb_rest[:, l, hd:hd + 1], lb[:, l, hd:hd + 1], ALU.mult, ALU.add))
                    v.tensor_scalar(hk[:], hf[:], -1.0, 1.0, ALU.mult, ALU.add).then_inc(pair_ready, 1)
                    pairs[0] += 1
                    v.tensor_scalar(pre[:], hf[:, 0:SEQ], F_FLOOR, None, ALU.max)
                    v.memset(suf[:], 1.0)
                    v.tensor_scalar(f_s[:, hd, :], hf[:, SEQ:COLS], F_FLOOR, None, ALU.max).then_inc(hf_used, 1)
                    dve.wait_ge(pair_ready, pairs[0])
                    v.tensor_copy(k_s[:, hd, :], hk[:, SEQ:COLS])
                    link(v.tensor_copy(q_s[:, hd, :], hq[hd % 2][:, SEQ:COLS]))

                def pair(hd, n):
                    if n == 1 and hd > 0:
                        dve.wait_ge(side_full, SIDE[(l, "kbT", hd - 1)] + 1)
                    elif n >= 2:
                        dve.wait_ge(side_full, SIDE[(l, "level", hd, LEVELS[n - 1])] + 1)
                    to = hq[hd % 2][:, 0:SEQ] if mixing[n] == P else qm[n % 2][:]
                    v.tensor_tensor(to, hq[hd % 2][:, 0:SEQ], pre[:], ALU.mult)
                    v.tensor_tensor(km[n % 2][:], hk[:, 0:SEQ], suf[:], ALU.mult).then_inc(pair_ready, 1)
                    pairs[0] += 1

                def double(h):
                    pv = pre[:].rearrange("p (m a h) -> p m a h", a=2, h=h)
                    sv = suf[:].rearrange("p (m a h) -> p m a h", a=2, h=h)
                    m = SEQ // (2 * h)
                    dve.wait_ge(pair_ready, pairs[0])
                    link(v.tensor_tensor(sv[:, :, 0, :], sv[:, :, 0, :], bc(pv[:, :, 1, h - 1:h], [P, m, h]), ALU.mult))
                    link(v.tensor_tensor(pv[:, :, 1, :], pv[:, :, 1, :], bc(pv[:, :, 0, h - 1:h], [P, m, h]), ALU.mult))

                def scores(hd, n):
                    src, done = wait_side(dve, l, "level", hd, LEVELS[n])
                    sv = src[:, :].rearrange("p (c n) -> p c n", c=TT)
                    mk = bc(levels[:, n, :].unsqueeze(1), [P, TT, P])
                    if n == 0:
                        if hd > 0:
                            dve.wait_ge(side_full, SIDE[(l, "o", hd - 1)] + 1)
                        v.tensor_tensor(att[:], sv, mk, ALU.mult).then_inc(done, 1)
                    else:
                        wait_side_taken(dve, l, "level", hd, LEVELS[n - 1])
                        v.copy_predicated(att[:], mk.bitcast(U32), sv).then_inc(done, 1)

                def finish(hd):
                    scores(hd, len(LEVELS) - 1)
                    src, done = wait_side(dve, l, "delta", hd)
                    dl = src[:, 0:TT * HV].rearrange("p (c n) -> p c n", c=TT)
                    link(v.tensor_copy(chain[:, 0], dl[:, 0]))
                    for c in range(1, TT):
                        last = v.scalar_tensor_tensor(out=chain[:, c], in0=chain[:, c - 1], scalar=decay[:, c:c + 1],
                                                      in1=dl[:, c], op0=ALU.mult, op1=ALU.add)
                        if c < TT - 1:
                            link(last)
                    last.then_inc(done, 1)
                    wait_side_taken(dve, l, "delta", hd)
                    v.tensor_copy(state_p[:, hd], chain[:, TT - 1]).then_inc(chain_ready, 1)

                for hd in range(HH):
                    start(hd)
                    if hd > 0:
                        finish(hd - 1)
                    for n, h in enumerate(mixing):
                        pair(hd, n)
                        if h < P:
                            double(h)
                        else:
                            link(v.tensor_copy(decay[:], pre[:, P - 1:SEQ:P]))
                            dve.wait_ge(pair_ready, pairs[0])
                        if n > 0:
                            scores(hd, n - 1)
                finish(HH - 1)

                dve.wait_ge(state_loaded, 32 * (l + 1))
                dve.wait_ge(side_full, SIDE[(l, "o", HH - 1)] + 1)

                def over_v(tile, b0, nb):
                    return bc(tile[:, :, b0:b0 + nb].rearrange("p h b -> p b h").unsqueeze(3), [P, nb, HH, HV])

                for j in range(4):
                    bs = slice(2 * j, 2 * j + 2)
                    link(v.tensor_tensor(state_s[:, bs], state_in[:, bs], over_v(f_s, 2 * j, 2), ALU.mult))
                    src, done = wait_side(dve, l, "i_bcast", j)
                    v.tensor_tensor(state_in[:, bs], src[:, :].rearrange("p (b h v) -> p b h v", b=2, h=HH),
                                    over_v(k_s, 2 * j, 2), ALU.mult).then_inc(done, 1)
                    wait_side_taken(dve, l, "i_bcast", j)
                    last = v.tensor_tensor(state_s[:, bs], state_s[:, bs], state_in[:, bs], ALU.add)
                    if j < 3:
                        link(last)
                last.then_inc(state_ready, 1)
                dve.wait_ge(state_ready, l + 1)
                for j in range(4):
                    bs = slice(2 * j, 2 * j + 2)
                    last = v.tensor_tensor(state_q[:, bs], state_s[:, bs], over_v(q_s, 2 * j, 2), ALU.mult)
                last.then_inc(state_q_ready, 1)
                wait_side_taken(dve, l, "o_sample")
                wait_side_taken(dve, l, "o", HH - 1)
                link(v.tensor_tensor(o_sq[:], h_o[:], h_o[:], ALU.mult))
                link(v.reduce_sum(o_ms[:, 0], o_sq[:], axis=AX.X))
                v.tensor_scalar(o_ms[:, 0], o_ms[:, 0], 1.0 / HV, EPS, ALU.mult, ALU.add).then_inc(ms_ready, 1)
                dve.wait_ge(ms_ready, 2 * l + 2)
                dve.wait_ge(root_ready, 5 * l + 4)
                newton_rsqrt(steps, o_ms[:, 0], o_ms[:, 1], o_ms[:, 2], o_ms[:, 3])
                ov = h_o[:].rearrange("p t h v -> p (t h) v")
                link(v.tensor_tensor(ov, ov, bc(o_ms[:, 3].rearrange("p t h -> p (t h)").unsqueeze(2),
                                               [P, (TT + 1) * HH, HV]), ALU.mult))
                link(v.tensor_tensor(ov, ov, bc(onorm[:, l, :].unsqueeze(1), [P, (TT + 1) * HH, HV]), ALU.mult))
                v.tensor_tensor(h_o[:].rearrange("p t h v -> p t (h v)"), h_o[:].rearrange("p t h v -> p t (h v)"),
                                h_g[:], ALU.mult).then_inc(yb_ready, 1)
                for c in range(3):
                    src, done = wait_side(dve, l, "ybT", c)
                    dve.wait_ge(y_hi_ready, Y_HEADS * l + 4 + c + 1)
                    if c < 2:
                        v.tensor_tensor(yab_lo[:, 2 + c, 0:SEQ], src[:, :], yab_hi[:, 2 + c, 0:SEQ].bitcast(F32),
                                        ALU.subtract).then_inc(done, 1)
                    else:
                        v.tensor_tensor(yab_lo[:, 2:4, SEQ:COLS], src[:, 0:2 * NB].rearrange("p (c n) -> p c n", c=2),
                                        yab_hi[:, 2:4, SEQ:COLS].bitcast(F32), ALU.subtract).then_inc(done, 1)

            def prompt_index(l, t):
                nk = (t + 1) * P
                for h in range(IDXH):
                    wait_side_taken(dve, l, "index", t, h)
                    v.scalar_tensor_tensor(out=score[:, 0:nk], in0=rel[h % 2][:, 0:nk], scalar=wi[:, t, h:h + 1],
                                           in1=causal[:, SEQ - nk:SEQ] if h == 0 else score[:, 0:nk],
                                           op0=ALU.mult, op1=ALU.add).then_inc(index_used, 1)
                    dve.wait_ge(index_used, INDEX_USES * l + 4 * t + h + 1)

            def top_round(t, n):
                nk = (t + 1) * P
                src = score if n == 0 else work
                link(v.max(top8[:], src[:, 0:nk]))
                link(v.match_replace(out=work[:, 0:nk], in_to_replace=top8[:], in_values=src[:, 0:nk], imm_value=TAKEN))

            def make_mask(t):
                nk = (t + 1) * P
                if t == 0:
                    link(v.tensor_copy(mask[0][:, 0:nk], causal[:, SEQ - nk:SEQ]))
                else:
                    link(v.tensor_scalar(mask[t % 2][:, 0:nk], work[:, 0:nk], TAKEN, NEG_BIG, ALU.not_equal, ALU.mult))

            def prompt_attention(l, t):
                nk = (t + 1) * P
                rounds = list(range(TOP_PROMPT // 8)) if t + 1 < TT else []
                heads = NH * (TT * l + t)
                for kind, h in attention_order():
                    if kind == "logits":
                        src, done = wait_side(dve, l, "logits", t, h)
                        if h >= 2:
                            dve.wait_ge(side_full, SIDE[(l, "probT", t, h - 2)] + 1)
                        v.tensor_tensor_reduce(out=probs[h % 2][:, 0:nk], in0=src[:, 0:nk], in1=mask[t % 2][:, 0:nk],
                                               scale=1.0, scalar=TAKEN, op0=ALU.add, op1=ALU.max,
                                               accum_out=row_max[:, h:h + 1]).then_inc(done, 1)
                        wait_side_taken(dve, l, "logits", t, h)
                        v.tensor_scalar(neg_max[:, h:h + 1], row_max[:, h:h + 1], -ATTN_SCALE, None, ALU.mult)\
                         .then_inc(neg_max_ready, 1)
                        for _ in range(2):
                            if rounds:
                                top_round(t + 1, rounds.pop(0))
                    elif kind == "pv":
                        src, done = wait_side(dve, l, "pv", t, h)
                        dve.wait_ge(probs_ready, heads + 2 * h + 2)
                        link(v.reciprocal(row_inv[:, 2 * h:2 * h + 2], row_sum[:, 2 * h:2 * h + 2]))
                        v.tensor_tensor(o_tok[:, 2 * h:2 * h + 2, :], src[:, 0:2 * HD].rearrange("p (a n) -> p a n", a=2),
                                        bc(row_inv[:, 2 * h:2 * h + 2].unsqueeze(2), [P, 2, HD]), ALU.mult)\
                         .then_inc(done, 1)
                src, done = wait_side(dve, l, "ycT", t)
                dve.wait_ge(y_hi_ready, Y_HEADS * l + 7 + t + 1)
                v.tensor_tensor(yc_lo[:, :, t * P:(t + 1) * P], src[:, :].rearrange("p (c n) -> p c n", c=4),
                                yc_hi[:, :, t * P:(t + 1) * P].bitcast(F32), ALU.subtract).then_inc(done, 1)
                if t + 1 < TT:
                    make_mask(t + 1)
                sub, hh = N_SUB * l + 2 + t // 2, t % 2
                if sub in mixer_adas(l):
                    ada_rows(sub, hh)
                    ada_take(sub, hh)

            def sample_attention(l):
                v.memset(q_blk[:], 0.0)
                link(v.memset(qi_blk[:], 0.0))
                qd = q_blk[:].rearrange("p c b n g -> p (c b) n g")
                for n in range(NKV):
                    ps = slice(n * HD, (n + 1) * HD)
                    v.tensor_copy(qd[ps, 0:NB * NB:NB + 1, n, :], rotT_s[ps, 0:4, :].rearrange("p g b -> p b g"))
                qi = qi_blk[:].rearrange("p c b h -> p (c b) h")
                for par in range(2):
                    last = v.tensor_copy(qi[:, 0:NB * NB:NB + 1, par:IDXH:2],
                                         rotT_s[par * HD:(par + 1) * HD, 5:7, :].rearrange("p g b -> p b g"))
                v.tensor_copy(kT_s[:, :, PAST], rotT_s[:, 4, :])
                v.tensor_copy(kiT_s[:, :, PAST], rotT_s[0:HD, 7, :]).then_inc(q_blk_ready, 1)
                v.tensor_tensor(wi_exp[:], spread_idx[:], bc(wi[0:NB, TT, :].unsqueeze(1), [NB, NB, IDXH]),
                                ALU.mult).then_inc(wi_exp_ready, 1)
                src, done = wait_side(dve, l, "s_score")
                v.tensor_copy(score_s[:], src[0:NB, 0:LVIS]).then_inc(done, 1)
                wait_side_taken(dve, l, "s_score")
                for n in range(TOP_SAMPLE // 8):
                    cur = score_s if n == 0 else work_s
                    link(v.max(top8_s[:], cur[:]))
                    link(v.match_replace(out=work_s[:], in_to_replace=top8_s[:], in_values=cur[:], imm_value=TAKEN))
                v.tensor_scalar(mask_s[:], work_s[:], TAKEN, NEG_BIG, ALU.not_equal, ALU.mult).then_inc(mask_s_ready, 1)
                src, done = wait_side(dve, l, "s_logits")
                v.tensor_copy(prob_s[:], src[0:NB * NH, 0:LVIS]).then_inc(done, 1)
                wait_side_taken(dve, l, "s_logits")
                link(v.reduce_max(st_s[:, 0:1], prob_s[:], axis=AX.X))
                v.tensor_scalar(st_s[:, 1:2], st_s[:, 0:1], -ATTN_SCALE, None, ALU.mult).then_inc(s_neg_ready, 1)
                link(v.memset(probT_blk[:], 0.0))
                dve.wait_ge(s_probs_ready, l + 1)
                link(v.reciprocal(st_s[:, 3:4], st_s[:, 2:3]))
                v.tensor_scalar(own_diag[:], ident[0:NB * NH, 0:NB * NH], prob_s[:, PAST:LVIS], None, ALU.mult)\
                 .then_inc(own_diag_ready, 1)
                src, done = wait_side(dve, l, "s_probT")
                for pg in range(PAGES):
                    dst = probT_blk[:, pg].rearrange("p c (b h) -> p (c b) h", h=NH)
                    v.tensor_copy(dst[:, 0:NB * NB:NB + 1, :],
                                  src[:, pg * NB * NH:(pg + 1) * NB * NH].rearrange("p (b h) -> p b h", h=NH))
                v.tensor_copy(own_prob[:], src[0:NB, 2 * NB * NH:3 * NB * NH]).then_inc(done, 1)
                src, done = wait_side(dve, l, "s_o")
                v.tensor_scalar(o_s[:], src[0:NB * NH, 0:P], st_s[:, 3:4], None, ALU.mult).then_inc(done, 1)
                src, done = wait_side(dve, l, "s_oT")
                sv = src[:, 0:NB * NH].rearrange("p (b n g) -> p b n g", n=NKV, g=4)
                for n in range(NKV):
                    for par in range(2):
                        dst = slice(par * HD, (par + 1) * HD)
                        frm = sv[n * HD:(n + 1) * HD, :, n, par:4:2].rearrange("p b g -> p g b")
                        link(v.tensor_copy(yc_hi[dst, 2 * n:2 * n + 2, SEQ:COLS], frm))
                for n in range(NKV):
                    for par in range(2):
                        dst = slice(par * HD, (par + 1) * HD)
                        frm = sv[n * HD:(n + 1) * HD, :, n, par:4:2].rearrange("p b g -> p g b")
                        last = v.tensor_tensor(yc_lo[dst, 2 * n:2 * n + 2, SEQ:COLS], frm,
                                               yc_hi[dst, 2 * n:2 * n + 2, SEQ:COLS].bitcast(F32), ALU.subtract)
                last.then_inc(done, 1)

            def merge(l):
                with dve.Fori(0, 4) as r:
                    steps.loop(r, 4, 4)
                    for n in range(2):
                        for hf in range(2):
                            for b in range(3):
                                g = 12 + 6 * n + 3 * hf + b
                                wait_main(dve, main_unit(l, "merge", 24 * r + g))
                                if b == 0:
                                    dve.wait_ge(main_taken[3], main_use(l, "merge", 6 * r + 3) + PRIMED)
                                last = v.tensor_tensor(part[:, b, :], gate_s[:, 3 * n + b, half(hf)],
                                                       bank[g % 4][:, 0:HALF], ALU.mult)
                                last.then_inc(main_taken[g % 4], 1)
                                dve.wait_ge(main_taken[g % 4], main_use(l, "merge", 6 * r + g // 4) + 1 + PRIMED)
                            link(v.tensor_tensor(part[:, 0, :], part[:, 0, :], part[:, 1, :], ALU.add))
                            v.tensor_tensor(part[:, 2, :], part[:, 0, :], part[:, 2, :], ALU.add).then_inc(mrg_ready, 1)
                            dve.wait_ge(mrg_ready, 16 * l + 4 * r + 2 * n + hf + 1 + PRIMED)
                            dve.wait_ge(mrg_hi_ready, 16 * l + 4 * r + 2 * n + hf + 1)
                            at = bass.ds(2 * r + n, 1)
                            v.tensor_tensor(mrg_lo[:, at, half(hf)].rearrange("p o n -> p (o n)"), part[:, 2, :],
                                            mrg_hi[:, at, half(hf)].rearrange("p o n -> p (o n)").bitcast(F32),
                                            ALU.subtract).then_inc(mrg_lo_ready, 1)
                    steps.end()

            v.memset(ada_bank[:], 0.0).then_inc(ada_taken0, 1)
            for hh in range(2):
                ada_rows(0, hh)
                ada_take(0, hh)
            mids = 0
            for l in range(DEPTH):
                for f in range(2):
                    sub = N_SUB * l + 2 * f
                    norm(sub)
                    for p_ in range(2):
                        ffn_up(l, f"up{f}{p_}", UP[p_], mids)
                        mids += 2 * UP[p_]
                        if f == 0 and p_ == 1:
                            ada_take(sub + 1, 0)
                        residual(l, f"down{f}{p_}", sub, 1, KT)
                        if f == 0:
                            ada_rows(sub + 1, p_)
                    if f == 0:
                        ada_take(sub + 1, 1)
                        norm(sub + 1)
                        ya_tails(l)
                        rotary(l)
                        hgrn(l)
                        dve.wait_ge(causal_loaded, 16 * (l + 1))
                        prompt_index(l, 0)
                        make_mask(0)
                        for t in range(TT):
                            if t + 1 < TT:
                                prompt_index(l, t + 1)
                            prompt_attention(l, t)
                        sample_attention(l)
                        merge(l)
                        residual(l, "out", sub + 1, 2, 4)

        @block.tensor
        def _(pe):
            mm = nc.tensor.matmul
            order = [0]

            def open_side(*key):
                n, b, use = side_unit(*key)
                assert n == order[0], (key, n, order[0])
                order[0] += 1
                if use > 0:
                    pe.wait_ge(side_taken[b], use)
                return bank[4 + b]

            def product(out, blocks, ws, xs):
                (wh, wl), (xh, xl) = ws, xs
                for n, (wb, xb) in enumerate(blocks):
                    mm(out, wh(wb), xh(xb), start=(n == 0), stop=False)
                    mm(out, wl(wb), xh(xb), start=False, stop=False)
                    last = mm(out, wh(wb), xl(xb), start=False, stop=(n == len(blocks) - 1))
                return last

            def weights(j):
                def blk(tile):
                    return lambda n: tile[:, n * P:(n + 1) * P]
                return blk(w_hi[j]), blk(w_lo[j])

            def moving(hi, lo, hf):
                return (lambda k: hi[:, k, half(hf)]), (lambda k: lo[:, k, half(hf)])

            def wait_slot(l, stage, r, j):
                pe.wait_ge(w_split[j], slot_use(l, stage, r) + 1 + PRIMED)

            def take_main(b, use):
                pe.wait_ge(main_taken[b], use + PRIMED)

            def ada(sub, n):
                j, k = n % 2, n % KT
                pe.wait_ge(ada_loaded[j], 16 * (ADA_SLOTS * sub // 2 + n // 2 + 1))
                if sub + n == 0:
                    pe.wait_ge(ada_taken0, 1)
                elif k == 0:
                    pe.wait_ge(ada_taken, 2 * sub + n // KT)
                for a in range(ADA_CHUNKS):
                    last = mm(ada_bank[32 * a:32 * a + CC, 0:ADA_N], cond[:, k, :], ada_w[j][:, a, :],
                              start=(k == 0), stop=(k == KT - 1))
                last.then_inc(ada_used[j], 1)

            def ada_turn(sub, hh):
                pe.wait_ge(ada_row_ready, 2 * sub + hh + 1)
                for q in range(ADA_Q):
                    at = ADA_N + q * ADA_CHUNKS * CC
                    last = mm(ada_bank[:, at:at + ADA_CHUNKS * CC], ada_row[:, q * P:(q + 1) * P],
                              ada_select[:].rearrange("p a c -> p (a c)"), start=True, stop=True)
                last.then_inc(ada_turned, 1)

            def norm(sub):
                l, j3 = divmod(sub, N_SUB)
                for hf in range(2):
                    out = open_side(l, "norm", j3, hf)
                    pe.wait_ge(squared, SQUARES * (sub + 1))
                    mm(out[:, 0:HALF], ones[:], sq_sum[:, half(hf)], start=True, stop=True).then_inc(side_full, 1)

            def wait_h(sub, k):
                pe.wait_ge(h_lo_ready, 9 * sub + k + 2)

            def split_products(outs, k, w, xs):
                for out, (wh, wl), (xh, xl) in zip(outs, w, xs):
                    mm(out, wh, xh, start=(k == 0), stop=False)
                    mm(out, wl, xh, start=False, stop=False)
                    last = mm(out, wh, xl, start=False, stop=(k == KT - 1))
                    if k == KT - 1:
                        last.then_inc(main_full, 1)

            def ffn_up(l, stage, tiles, sub=None):
                if sub is not None:
                    wait_slot(l, stage, 0, 0)
                    for b in range(4):
                        take_main(b, main_use(l, stage))
                    for k in range(KT):
                        wait_h(sub, k)
                        outs = [bank[b][:, 0:HALF] for b in range(4)]
                        w = [tuple(tile((b % 2) * KT + k) for tile in weights(0)) for b in range(4)]
                        xs = [tuple(tile(k) for tile in moving(h_hi, h_lo, b // 2)) for b in range(4)]
                        split_products(outs, k, w, xs)
                    up_slot(l, stage, 0, 1)
                with pe.Fori(0 if sub is None else 1, tiles // 2) as r:
                    for j in range(2):
                        up_slot(l, stage, r, j)

            def up_slot(l, stage, r, j):
                wait_slot(l, stage, r, j)
                use = main_use(l, stage, 2 * r + j)
                for hf in range(2):
                    for which in range(2):
                        take_main(2 * hf + which, use)
                        product(bank[2 * hf + which][:, 0:HALF], [(which * KT + k, k) for k in range(KT)],
                                (lambda n: weights(j)[0](n), lambda n: weights(j)[1](n)),
                                moving(h_hi, h_lo, hf)).then_inc(main_full, 1)

            def down(l, stage, tiles, mids, ada_sub, hh):
                pe.wait_ge(mid_lo_ready, mids)

                def slot(r, j):
                    wait_slot(l, stage, r, j)
                    for hf in range(2):
                        take_main(2 * j + hf, main_use(l, stage, r))
                        product(bank[2 * j + hf][:, 0:HALF], [(k, k) for k in range(tiles)], weights(j),
                                moving(mid_hi, mid_lo, hf)).then_inc(main_full, 1)

                if ada_sub is None:
                    with pe.Fori(0, KT // 2) as r:
                        for j in range(2):
                            slot(r, j)
                else:
                    for n in range(KT):
                        slot(n // 2, n % 2)
                        ada(ada_sub, KT * hh + n)

            def token_major(l):
                def tile(slot, u, i, k):
                    j = slot % 2
                    width = 256 if slot < 7 else HD + IDXH
                    t = 2 * u + i
                    out = bank[main_unit(l, "token", 3 * slot + u) % 4][:, 256 * i:256 * i + width]
                    cols = slice(t * P, (t + 1) * P)
                    wcols = slice(k * 256, k * 256 + width)
                    mm(out, h_hi[:, k, cols], w_hi[j][:, wcols], start=(k == 0), stop=False)
                    mm(out, h_lo[:, k, cols], w_hi[j][:, wcols], start=False, stop=False)
                    return mm(out, h_hi[:, k, cols], w_lo[j][:, wcols], start=False, stop=(k == KT - 1))

                for slot in range(8):
                    wait_slot(l, "token", slot // 2, slot % 2)
                    if slot == 0:
                        for u in range(3):
                            take_main(u, main_use(l, "token"))
                        for k in range(KT):
                            wait_h(N_SUB * l + 1, k)
                            for u in range(3 if k < KT - 1 else 2):
                                tile(0, u, 0, k)
                    for u in range(3):
                        unit = main_unit(l, "token", 3 * slot + u)
                        if slot > 0:
                            take_main(unit % 4, unit // 4)
                        for i in range(2 if u < 2 else 1):
                            first_k = 0 if slot > 0 or i > 0 else KT - (u == 2)
                            for k in range(first_k, KT):
                                last = tile(slot, u, i, k)
                        last.then_inc(main_full, 1)

            def token_tile_wait(l, n):
                unit = main_unit(l, "token", n)
                pe.wait_ge(main_taken[unit % 4], unit // 4 + 1 + PRIMED)

            def pool_branch(l):
                pe.wait_ge(pool_loaded, 80 * (l + 1))
                token_tile_wait(l, 2)
                for c in range(2):
                    out = open_side(l, "pooled", c)
                    for g in (2 * c, 2 * c + 1):
                        rows = slice((g % 2) * 64, (g % 2) * 64 + 64)
                        ch = slice(g * POOL_G, (g + 1) * POOL_G)
                        for t in range(TT):
                            o = out[rows, t * P:(t + 1) * P]
                            last = mm(o, pool_u[:, t, ch], windows[:, 1 if t == 0 else 0, g, :], start=True, stop=(t == 0))
                            if t > 0:
                                last = mm(o, pool_u[:, t - 1, ch], windows[:, 2, g, :], start=False, stop=True)
                    last.then_inc(side_full, 1)
                out = open_side(l, "pooled", 2)
                for g in range(4):
                    rows = slice((g % 2) * 64, (g % 2) * 64 + 64)
                    ch = slice(g * POOL_G, (g + 1) * POOL_G)
                    o = out[rows, (g // 2) * NB:(g // 2 + 1) * NB]
                    mm(o, pool_past[:, ch], windows_past[:, g, :], start=True, stop=False)
                    last = mm(o, pool_u[0:NB, TT, ch], windows_own[:, g, :], start=False, stop=True)
                last.then_inc(side_full, 1)
                for c in range(2):
                    wait_side_taken(pe, l, "pooled", c)
                wait_side_taken(pe, l, "pooled", 2)
                for c in range(2):
                    for hf in range(2):
                        out = open_side(l, "ya", c, hf)
                        mm(out[:, 0:HALF], pool_w[:, c, :], pooled[:, c, half(hf)], start=True, stop=True)\
                            .then_inc(side_full, 1)

            def rotary(l):
                for t in range(TT + 1):
                    n = P if t < TT else NB
                    pe.wait_ge(rotated, 5 * l + t + 1)
                    rt = rot[0:n, t]
                    for part_ in range(2):
                        out = open_side(l, "rotT", t, part_)
                        for i in range(4 if part_ == 0 else 3):
                            row = 8 * part_ + 2 * i
                            last = nc.tensor.transpose(out[:, i * n:(i + 1) * n],
                                                       rt[:, row:row + 2, :].rearrange("p a e -> p (a e)"), ident[0:n, 0:n])
                        if part_ == 1:
                            for a in range(2):
                                last = mm(out[a * HD:(a + 1) * HD, 3 * n:4 * n], rt[:, ROT - 1, :], ident[0:n, 0:n],
                                          start=True, stop=True)
                        last.then_inc(side_full, 1)

            def hgrn_projection(l, hd, b):
                which, hf = divmod(b, 2)
                wait_slot(l, "hgrn", hd // 2, hd % 2)
                take_main(b, main_use(l, "hgrn", hd))
                product(bank[b][:, 0:HALF], [(which * KT + k, k) for k in range(KT)], weights(hd % 2),
                        moving(h_hi, h_lo, hf)).then_inc(main_full, 1)

            def hgrn(l):
                pairs = PAIRS * l
                fin = len(LEVELS[1:]) % 2

                def outputs(hd):
                    vs = slice(hd * HV, (hd + 1) * HV)
                    out = open_side(l, "o", hd)
                    wait_side_taken(pe, l, "delta", hd)
                    wait_side_taken(pe, l, "level", hd, LEVELS[-1])
                    for c in range(TT):
                        o = out[:, c * HV:(c + 1) * HV]
                        last = mm(o, att[:, c, :], h_i[:, c, vs], start=True, stop=(c == 0))
                        if c > 0:
                            last = mm(o, hq[hd % 2][:, c * P:(c + 1) * P], chain[:, c - 1, :], start=False, stop=True)
                    last.then_inc(side_full, 1)

                for hd in range(HH):
                    for n, h in enumerate(LEVELS):
                        if hd + 1 < HH and 3 <= n < 7:
                            hgrn_projection(l, hd + 1, n - 3)
                        out = open_side(l, "level", hd, h)
                        pairs += 1
                        pe.wait_ge(pair_ready, pairs)
                        for c in range(TT):
                            cs = slice(c * P, (c + 1) * P)
                            kt, qt = (hk, hq[hd % 2]) if n == 0 else (km[(n - 1) % 2], qm[(n - 1) % 2])
                            last = mm(out[:, cs], kt[:, cs], qt[:, cs], start=True, stop=True)
                        last.then_inc(side_full, 1)
                        if n == 0 and hd > 0:
                            outputs(hd - 1)
                    pairs += 1
                    pe.wait_ge(pair_ready, pairs)
                    out = open_side(l, "kbT", hd)
                    for c in range(TT):
                        cs = slice(c * P, (c + 1) * P)
                        last = nc.tensor.transpose(out[:, cs], km[fin][:, cs], ident[:])
                    last.then_inc(side_full, 1)
                    vs = slice(hd * HV, (hd + 1) * HV)
                    out = open_side(l, "delta", hd)
                    wait_side_taken(pe, l, "kbT", hd)
                    for c in range(TT):
                        last = mm(out[:, c * HV:(c + 1) * HV], kbT[:, c, :], h_i[:, c, vs], start=True, stop=True)
                    last.then_inc(side_full, 1)
                outputs(HH - 1)
                pe.wait_ge(state_loaded, 32 * (l + 1))
                for j in range(4):
                    out = open_side(l, "i_bcast", j)
                    for i in range(2):
                        last = mm(out[:, i * HIW:(i + 1) * HIW], row_select[:, 2 * j + i, :], h_i[0:NB, TT, :],
                                  start=True, stop=True)
                    last.then_inc(side_full, 1)
                out = open_side(l, "o_sample")
                pe.wait_ge(state_q_ready, l + 1)
                for b in range(NB):
                    last = mm(out[0:NB, 0:HIW], col_select[:, NB - 1 - b:2 * NB - 1 - b],
                              state_q[:, b].rearrange("p h v -> p (h v)"), start=(b == 0), stop=(b == NB - 1))
                last.then_inc(side_full, 1)
                pe.wait_ge(yb_ready, l + 1)
                for c in range(2):
                    out = open_side(l, "ybT", c)
                    for t in range(TT):
                        src = h_o[:, t].rearrange("p h v -> p (h v)")
                        last = nc.tensor.transpose(out[:, t * P:(t + 1) * P], src[:, c * P:(c + 1) * P], ident[:])
                    last.then_inc(side_full, 1)
                out = open_side(l, "ybT", 2)
                for c in range(2):
                    src = h_o[0:NB, TT].rearrange("p h v -> p (h v)")
                    last = nc.tensor.transpose(out[:, c * NB:(c + 1) * NB], src[:, c * P:(c + 1) * P], ident[0:NB, 0:NB])
                last.then_inc(side_full, 1)

            def prompt_index(l, t):
                nk = (t + 1) * P
                for h in range(IDXH):
                    out = open_side(l, "index", t, h)
                    rows = slice((h % 2) * HD, (h % 2 + 1) * HD)
                    mm(out[:, 0:nk], rotT[rows, 5 + h // 2, t * P:(t + 1) * P], rotT[rows, 7, 0:nk],
                       start=True, stop=True).then_inc(side_full, 1)

            def prompt_attention(l, t):
                nk = (t + 1) * P
                sub, hh = N_SUB * l + 2 + t // 2, t % 2
                for kind, h in attention_order():
                    out = open_side(l, kind, t, h)
                    if kind == "logits":
                        n, g = divmod(h, 4)
                        rows = slice(n * HD, (n + 1) * HD)
                        last = mm(out[:, 0:nk], rotT[rows, g, t * P:(t + 1) * P], rotT[rows, 4, 0:nk], start=True, stop=True)
                    elif kind == "probT":
                        pe.wait_ge(probs_ready, NH * (TT * l + t) + h + 1)
                        for kb in range(t + 1):
                            ks = slice(kb * P, (kb + 1) * P)
                            last = nc.tensor.transpose(out[:, ks], probs[h % 2][:, ks], ident[:])
                    else:
                        wait_side_taken(pe, l, "probT", t, 2 * h)
                        wait_side_taken(pe, l, "probT", t, 2 * h + 1)
                        for i in range(2):
                            head = 2 * h + i
                            n = head // 4
                            for kb in range(t + 1):
                                last = mm(out[:, i * HD:(i + 1) * HD], probT[head % 4][:, kb, :],
                                          vals[:, kb, n * HD:(n + 1) * HD], start=(kb == 0), stop=(kb == t))
                    last.then_inc(side_full, 1)
                    if kind == "logits" and sub in mixer_adas(l):
                        ada(sub, KT * hh + h)
                out = open_side(l, "ycT", t)
                wait_side_taken(pe, l, "pv", t, NH // 2 - 1)
                for c in range(4):
                    last = nc.tensor.transpose(out[:, c * P:(c + 1) * P],
                                               o_tok[:, 2 * c:2 * c + 2, :].rearrange("p a n -> p (a n)"), ident[:])
                last.then_inc(side_full, 1)
                if sub in mixer_adas(l):
                    ada_turn(sub, hh)

            def sample_attention(l):
                pe.wait_ge(ki_loaded, 16 * NB * PAGES * (l + 1))
                for j in range(2):
                    out = open_side(l, "kiT_page", j)
                    for i in range(4):
                        last = nc.tensor.transpose(out[:, i * P:(i + 1) * P],
                                                   ki_page[:, 4 * j + i].rearrange("p a n -> p (a n)"), ident[:])
                    last.then_inc(side_full, 1)
                out = open_side(l, "s_index")
                pe.wait_ge(q_blk_ready, l + 1)
                wait_side_taken(pe, l, "kiT_page", 1)
                for b in range(NB):
                    last = mm(out[0:NB * IDXH, 0:LVIS], qi_blk[:, b].rearrange("p b h -> p (b h)"), kiT_s[:, b, :],
                              start=(b == 0), stop=(b == NB - 1))
                last.then_inc(side_full, 1)
                out = open_side(l, "s_wsel")
                pe.wait_ge(wi_exp_ready, l + 1)
                nc.tensor.transpose(out[0:NB * IDXH, 0:NB], wi_exp[:].rearrange("p b h -> p (b h)"), ident[0:NB, 0:NB])\
                    .then_inc(side_full, 1)
                out = open_side(l, "s_score")
                wait_side_taken(pe, l, "s_index")
                wait_side_taken(pe, l, "s_wsel")
                mm(out[0:NB, 0:LVIS], wi_sel[:], rel_s[:], start=True, stop=True).then_inc(side_full, 1)
                pe.wait_ge(k_loaded, 16 * NB * PAGES * (l + 1))
                for j in range(4):
                    out = open_side(l, "kT_page", j)
                    for i in range(4):
                        b, pg = 2 * j + i // 2, i % 2
                        last = nc.tensor.transpose(out[:, i * P:(i + 1) * P], k_page[:, b, pg, :], ident[:])
                    last.then_inc(side_full, 1)
                out = open_side(l, "s_logits")
                wait_side_taken(pe, l, "kT_page", 3)
                for b in range(NB):
                    mm(out[0:NB * NH, 0:LVIS], q_blk[:, b].rearrange("p b n g -> p (b n g)"), kT_s[:, b, :],
                       start=(b == 0), stop=False)
                merge_gates(l, 0, 0)
                pe.wait_ge(mask_s_ready, l + 1)
                mm(out[0:NB * NH, 0:LVIS], spread_heads[:], mask_s[:], start=False, stop=True).then_inc(side_full, 1)
                out = open_side(l, "s_probT")
                pe.wait_ge(s_probs_ready, l + 1)
                for pg in range(PAGES):
                    nc.tensor.transpose(out[:, pg * NB * NH:(pg + 1) * NB * NH], prob_s[:, pg * P:(pg + 1) * P],
                                        ident[0:NB * NH, 0:NB * NH])
                pe.wait_ge(own_diag_ready, l + 1)
                mm(out[0:NB, 2 * NB * NH:3 * NB * NH], gather_heads[:], own_diag[:], start=True, stop=True)\
                    .then_inc(side_full, 1)
                out = open_side(l, "s_o")
                wait_side_taken(pe, l, "s_probT")
                pe.wait_ge(v_loaded, 16 * NB * PAGES * (l + 1))
                for b in range(NB):
                    for pg in range(PAGES):
                        mm(out[0:NB * NH, 0:P], probT_blk[:, pg, b, :], v_page[:, b, pg, :],
                           start=(b == 0 and pg == 0), stop=False)
                mm(out[0:NB * NH, 0:P], own_prob[:], vals[0:NB, TT, :], start=False, stop=True).then_inc(side_full, 1)
                out = open_side(l, "s_oT")
                wait_side_taken(pe, l, "s_o")
                nc.tensor.transpose(out[:, 0:NB * NH], o_s[:], ident[0:NB * NH, 0:NB * NH]).then_inc(side_full, 1)

            def merge_gates(l, r, slot):
                j = slot % 2
                wait_slot(l, "merge", 2 * r + slot // 2, j)
                for a in range(2):
                    for hf in range(2):
                        b = 2 * a + hf
                        take_main(b, main_use(l, "merge", 6 * r + slot))
                        product(bank[b][:, 0:HALF], [(a * KT + k, k) for k in range(KT)], weights(j),
                                moving(h_hi, h_lo, hf)).then_inc(main_full, 1)

            def merge(l):
                def turn(r, first):
                    for slot in range(first, 3):
                        merge_gates(l, r, slot)
                    if first > 0:
                        wait_side_taken(pe, l, "s_oT")
                    wait_slot(l, "merge", 2 * r + 1, 1)
                    for n in range(2):
                        for hf in range(2):
                            for br, (first, count) in enumerate(((0, 2), (2, 2), (4, 4))):
                                g = 12 + 6 * n + 3 * hf + br
                                take_main(g % 4, main_use(l, "merge", 6 * r + g // 4))
                                hi, lo, off = (yab_hi, yab_lo, 0) if br < 2 else (yc_hi, yc_lo, 4)
                                product(bank[g % 4][:, 0:HALF],
                                        [(n * KT + first + k, first + k - off) for k in range(count)],
                                        weights(1), moving(hi, lo, hf)).then_inc(main_full, 1)

                turn(0, 1)
                with pe.Fori(1, 4) as r:
                    turn(r, 0)
                pe.wait_ge(mrg_lo_ready, 16 * (l + 1))
                with pe.Fori(0, 2) as r:
                    for j in range(2):
                        wait_slot(l, "out", r, j)
                        for a in range(2):
                            for hf in range(2):
                                b = 2 * a + hf
                                take_main(b, main_use(l, "out", 2 * r + j))
                                product(bank[b][:, 0:HALF], [(a * KT + k, k) for k in range(KT)], weights(j),
                                        moving(mrg_hi, mrg_lo, hf)).then_inc(main_full, 1)

            pe.wait_ge(const_loaded, 16 * 13)
            pe.wait_ge(cond_ready, 1)
            pe.wait_ge(setup_done, 3)
            for n in range(ADA_SLOTS):
                ada(0, n)
                if n % KT == KT - 1:
                    ada_turn(0, n // KT)
            mids = 0
            for l in range(DEPTH):
                for f in range(2):
                    sub = N_SUB * l + 2 * f
                    norm(sub)
                    for p_ in range(2):
                        ffn_up(l, f"up{f}{p_}", UP[p_], sub if p_ == 0 else None)
                        mids += 2 * UP[p_]
                        if f == 0 and p_ == 1:
                            ada_turn(sub + 1, 0)
                        down(l, f"down{f}{p_}", UP[p_], mids, sub + 1 if f == 0 else None, p_)
                    if f == 0:
                        ada_turn(sub + 1, 1)
                        norm(sub + 1)
                        token_major(l)
                        pool_branch(l)
                        for b in range(4):
                            hgrn_projection(l, 0, b)
                        rotary(l)
                        hgrn(l)
                        prompt_index(l, 0)
                        for t in range(TT):
                            if t + 1 < TT:
                                prompt_index(l, t + 1)
                            prompt_attention(l, t)
                        sample_attention(l)
                        merge(l)


def kernel(**inputs):
    import concourse.bacc as bacc
    from concourse.bass_utils import run_bass_kernel_spmd

    a = {k: np.asarray(v) for k, v in inputs.items()}

    def blocks(w):
        k, n = w.shape
        return w.reshape(k // P, P, n // P, P).transpose(1, 2, 0, 3)

    def per_slot(w, tiles):
        p, n, k, _ = w.shape
        return w.reshape(p, n // tiles, tiles * k * P).transpose(1, 0, 2)

    w = np.zeros((DEPTH * LAYER_SLOTS, P, SLOT), np.float32)
    for l in range(DEPTH):
        at = LAYER_SLOTS * l
        w_in = a["w_in"][l]
        cuts = np.cumsum((256, 512, 512, 256, 256, 512, 128, 128, 256, 64, 4))
        u, hq, hf, hi, hg, aq, ak, av, iq, ik, iw, gl = np.split(w_in, cuts, axis=1)
        for f in (0, 1):
            g_b, u_b = blocks(a["ffn_wg"][l, f]), blocks(a["ffn_wu"][l, f])
            down = blocks(a["ffn_wd"][l, f])
            first = 0
            for p_, tiles in enumerate(UP):
                s0 = at + SLOT0[f"up{f}{p_}"]
                both = np.stack([g_b[:, first:first + tiles], u_b[:, first:first + tiles]], 2)
                w[s0:s0 + tiles] = both.reshape(P, tiles, SLOT).transpose(1, 0, 2)
                s0 = at + SLOT0[f"down{f}{p_}"]
                w[s0:s0 + KT, :, 0:tiles * P] = per_slot(down[:, :, first:first + tiles], 1)
                first += tiles
        token = [u, hi, hg, aq[:, 0:256], aq[:, 256:512], np.concatenate([ak, av], 1), iq,
                 np.concatenate([ik, iw, np.zeros((D_MODEL, 256 - 68), np.float32)], 1)]
        s0 = at + SLOT0["token"]
        for n, t in enumerate(token):
            w[s0 + n] = t.reshape(KT, P, 256).transpose(1, 0, 2).reshape(P, SLOT)
        s0 = at + SLOT0["hgrn"]
        w[s0:s0 + HH] = np.stack([blocks(hq), blocks(hf)], 2).reshape(P, HH, SLOT).transpose(1, 0, 2)
        gates = blocks(gl).reshape(P, N_SUB, KT, KT, P).transpose(0, 2, 1, 3, 4)
        gates = gates.reshape(P, 12, SLOT)
        branches = np.concatenate([blocks(a["w_ba"][l]), blocks(a["w_bb"][l]), blocks(a["w_bc"][l])], 2)
        branches = branches.reshape(P, 4, SLOT)
        s0 = at + SLOT0["merge"]
        for r in range(4):
            for q in range(3):
                w[s0 + 4 * r + q] = gates[:, 3 * r + q]
            w[s0 + 4 * r + 3] = branches[:, r]
        s0 = at + SLOT0["out"]
        w[s0:s0 + 4] = per_slot(blocks(a["w_out"][l]), 2)

    ada = a["ada_w"].reshape(DEPTH, KT, P, N_SUB, ADA_CHUNKS, 2, ADA_N).transpose(0, 3, 5, 1, 2, 4, 6)
    ada = ada.reshape(DEPTH * N_SUB * ADA_SLOTS, P, ADA_CHUNKS * ADA_N)
    tokens = np.concatenate([a["x_prompt"][0], a["x_sample"][:, 0]])
    pool_w = np.zeros((DEPTH, P, 2, P), np.float32)
    for g in range(4):
        half = slice((g % 2) * POOL_G, (g % 2 + 1) * POOL_G)
        pool_w[:, half, g // 2, half] = a["pool_w"][:, g]
    gamma = np.ones((DEPTH, ROT, HD), np.float32)
    gamma[:, 0:8] = a["q_norm"][:, None]
    gamma[:, 8:10] = a["k_norm"][:, None]
    n_phys = a["cache_k"].shape[1]
    arrays = {
        "w": w,
        "ada": ada,
        "x": tokens.T.reshape(KT, P, COLS).transpose(1, 0, 2),
        "cond": np.concatenate([a["c_prompt"], a["c_sample"]]).T.reshape(KT, P, CC).transpose(1, 0, 2),
        "ada_b": a["ada_b"].reshape(DEPTH * N_SUB, 24, P).transpose(2, 0, 1),
        "norm_g": a["norm_g"].reshape(DEPTH * N_SUB, KT, P).transpose(2, 0, 1),
        "hgrn_lb": a["hgrn_lb"].reshape(DEPTH, HH, P).transpose(2, 0, 1),
        "hgrn_onorm": a["hgrn_onorm"],
        "pool_scale": a["pool_scale"].reshape(DEPTH, 2, P).transpose(2, 0, 1),
        "pool_w": pool_w,
        "gamma": gamma,
        "page_table": a["page_table"].reshape(1, NB * PAGES),
        "cache_k": a["cache_k"].reshape(DEPTH, n_phys, P, P),
        "cache_v": a["cache_v"].reshape(DEPTH, n_phys, P, P),
        "cache_ki": a["cache_ki"],
        "state_pool": a["state_pool"].reshape(DEPTH, NB * POOL_STATE, 256),
        "state_hgrn": a["state_hgrn"].transpose(0, 3, 1, 2, 4).reshape(DEPTH, P, NB * HIW),
    }
    arrays.update(constants())
    arrays = {k: np.ascontiguousarray(v) for k, v in arrays.items()}
    outputs = {
        "y": (P, KT, COLS),
        "k_out": (DEPTH, P, TT + 1, NKV * HD),
        "v_out": (DEPTH, P, TT + 1, NKV * HD),
        "ki_out": (DEPTH, P, TT + 1, HD),
        "pool_p": (DEPTH, POOL_STATE, 256),
        "pool_s": (DEPTH, NB, POOL_STATE, 256),
        "hgrn_p": (DEPTH, P, HH, HV),
        "hgrn_s": (DEPTH, P, NB * HIW),
    }
    nc = bacc.Bacc("TRN2", target_bir_lowering=False, num_devices=1)
    d = {}
    for k, v in arrays.items():
        d[k] = nc.dram_tensor(f"in_{k}", v.shape, mybir.dt.from_np(v.dtype), kind="ExternalInput").ap()
    for k, shape in outputs.items():
        d[k] = nc.dram_tensor(f"out_{k}", shape, F32, kind="ExternalOutput").ap()
    build(nc, d)
    res = run_bass_kernel_spmd(nc, [{f"in_{k}": v for k, v in arrays.items()}], core_ids=[0])
    o = {k: np.asarray(res.results[0][f"out_{k}"]) for k in outputs}

    y = o["y"].transpose(2, 1, 0).reshape(COLS, D_MODEL)

    def tokens_of(t):
        n = t.shape[-1]
        return (t[:, :, 0:TT].transpose(0, 2, 1, 3).reshape(DEPTH, 1, SEQ, n),
                t[:, 0:NB, TT].reshape(DEPTH, NB, 1, n))

    k_p, k_s = tokens_of(o["k_out"])
    v_p, v_s = tokens_of(o["v_out"])
    ki_p, ki_s = tokens_of(o["ki_out"])
    heads = (NKV, HD)
    hgrn_s = o["hgrn_s"].reshape(DEPTH, P, NB, HH, HV).transpose(0, 2, 3, 1, 4)
    c = np.ascontiguousarray
    return (c(y[0:SEQ][None]), c(y[SEQ:][:, None]),
            c(k_p.reshape(DEPTH, 1, SEQ, *heads)), c(v_p.reshape(DEPTH, 1, SEQ, *heads)), c(ki_p),
            c(o["pool_p"][:, None]), c(o["hgrn_p"].transpose(0, 2, 1, 3)[:, None]),
            c(k_s.reshape(DEPTH, NB, 1, *heads)), c(v_s.reshape(DEPTH, NB, 1, *heads)), c(ki_s),
            c(o["pool_s"]), c(hgrn_s))
```

```python
import numpy as np
import concourse.bass as bass
from concourse import mybir
from contextlib import ExitStack

F32 = mybir.dt.float32
F32R = mybir.dt.float32r
U32 = mybir.dt.uint32
I32 = mybir.dt.int32
ACT = mybir.ActivationFunctionType
ALU = mybir.AluOpType
AX = mybir.AxisListType

P = 128
DEPTH = 2
D_MODEL = 1024
KT = D_MODEL // P
SEQ = 512
NB = 8
COLS = SEQ + NB
HALF = COLS // 2
TT = SEQ // P
D_FF = 2816
UP = (12, 10)
assert sum(UP) * P == D_FF
N_SUB = 3
POOL_WINDOWS = (2, 4, 8, 16)
POOL_G = 64
POOL_STATE = 15
HH, HK, HV = 4, 128, 64
HIW = HH * HV
NH, NKV, HD = 8, 2, 64
IDXH = 4
PAST = 256
PAGES = 2
LVIS = PAST + 1
TOP_PROMPT = 128
TOP_SAMPLE = LVIS // 4
ROPE_THETA = 10000.0
ATTN_SCALE = HD ** -0.5
IDX_SCALE = (HD * IDXH) ** -0.5
NEG_BIG = -1e30
TAKEN = -3e38
EPS = 1e-6
F_FLOOR = 1e-30
PRIMED = 1
SLOT = 2048
ROT = 15
CC = 1 + NB

SEGMENTS = []
for _f in (0, 1):
    _ffn = []
    for _h, _n in enumerate(UP):
        _ffn += [(f"up{_f}{_h}", _n, SLOT), (f"down{_f}{_h}", KT, _n * P)]
    SEGMENTS += _ffn
    if _f == 0:
        SEGMENTS += [("token", 8, SLOT), ("gates0", 2, SLOT), ("hgrn", 4, SLOT), ("gates1", 2, SLOT),
                     ("merge", 12, SLOT), ("out", 4, SLOT)]
SLOT0, _at = {}, 0
for _name, _n, _ in SEGMENTS:
    SLOT0[_name] = _at
    _at += _n
LAYER_SLOTS = _at
USED = {name: used for name, _, used in SEGMENTS}
SLOTS = {name: n for name, n, _ in SEGMENTS}
ADA_CHUNKS = 4
ADA_N = 384
ADA_SLOTS = 2 * KT
ADA_Q = ADA_N // P
ADA_NORM = 4

MAIN0, _at = {}, 0
for _name, _n in [("up00", 4 * UP[0]), ("down00", 2 * KT), ("up01", 4 * UP[1]), ("down01", 2 * KT),
                  ("token", 24), ("gates0", 8), ("hgrn", 16), ("gates1", 8), ("merge", 80), ("out", 16),
                  ("up10", 4 * UP[0]), ("down10", 2 * KT), ("up11", 4 * UP[1]), ("down11", 2 * KT)]:
    assert _at % 4 == 0
    MAIN0[_name] = _at
    _at += _n
LAYER_MAIN = _at


def slot_end(stage, s):
    if stage == "merge":
        return (4, 8, 20, 32)[s] if s < 4 else 32 + 24 * (s // 4 - 1) + (4, 8, 12, 24)[s % 4]
    return (s + 1) * {"do": 2, "to": 3}.get(stage[:2], 4)


ROT_DVE = 4
EARLY_GATES = 8


def projections_at(r):
    return 2 + 3 * r if isinstance(r, int) else 6 * r - 1


LEVELS = (0, 1, 2, 4, 8, 16, 32, 64)


INDEX_USES = IDXH * TT
PAIRS = HH * (len(LEVELS) + 1)
Y_HEADS = 4 + 3 + TT
STORES = 8
X_TILES = 5 * KT
SQUARES = 2 * KT - 1


def x_updates(sub):
    return X_TILES * (sub // N_SUB) + (0, 2 * KT, 3 * KT)[sub % N_SUB]


def mixer_adas(l):
    return [sub for sub in (N_SUB * l + 2, N_SUB * l + 3) if sub < DEPTH * N_SUB]


def side_order():
    keys = []
    for l in range(DEPTH):
        keys += [(l, "norm", 0, n) for n in (0, 1, 2)] + [(l, "norm", 1, n) for n in (0, 1, 2)]
        keys += [(l, "pooled", c) for c in (0, 1, 2)]
        keys += [(l, "ya", c, h) for c in (0, 1) for h in (0, 1)]
        keys += [(l, "rotT", t, part) for t in range(TT + 1) for part in (0, 1)]
        for hd in range(HH):
            keys.append((l, "level", hd, LEVELS[0]))
            if hd > 0:
                keys.append((l, "o", hd - 1))
            keys += [(l, "level", hd, lv) for lv in LEVELS[1:]]
            keys += [(l, "kbT", hd), (l, "delta", hd)]
        keys.append((l, "o", HH - 1))
        keys += [(l, "i_bcast", j) for j in range(4)] + [(l, "o_sample",)]
        keys += [(l, "ybT", c) for c in (0, 1, 2)]
        keys += [(l, "index", 0, h) for h in range(IDXH)]
        for t in range(TT):
            if t + 1 < TT:
                keys += [(l, "index", t + 1, h) for h in range(IDXH)]
            for kind, h in attention_order():
                keys.append((l, kind, t, h))
            keys.append((l, "ycT", t))
        keys += [(l, "kiT_page", j) for j in range(2)] + [(l, "s_index",), (l, "s_wsel",), (l, "s_score",)]
        keys += [(l, "kT_page", j) for j in range(4)] + [(l, "s_logits",)]
        keys += [(l, "s_probT",), (l, "s_o",), (l, "s_oT",)]
        keys += [(l, "norm", 2, n) for n in (0, 1, 2)]
    return keys


def attention_order():
    order = []
    for h in range(NH + 2):
        if h < NH:
            order.append(("logits", h))
        if 1 <= h <= NH:
            order.append(("probT", h - 1))
        if h >= 3 and h % 2 == 1:
            order.append(("pv", (h - 3) // 2))
    return order


SIDE = {key: n for n, key in enumerate(side_order())}


def constants():
    c = {}
    c["ident"] = np.eye(P, dtype=np.float32)
    s = np.arange(P)[:, None]
    t = np.arange(P)[None, :]
    levels = [(s == t)]
    for h in LEVELS[1:]:
        levels.append((s // (2 * h) == t // (2 * h)) & (s // h % 2 == 0) & (t // h % 2 == 1))
    c["levels"] = np.stack([m.astype(np.float32) for m in levels], 1)
    c["causal"] = np.concatenate([np.zeros((P, 3 * P)), np.where(t <= s, 0.0, NEG_BIG)], 1).astype(np.float32)
    win = np.zeros((P, 3, 4, P), np.float32)
    for g, w in enumerate(POOL_WINDOWS):
        inside = (s <= t) & (s > t - w)
        win[:, 0, g] = inside / np.float32(w) - (s == t)
        win[:, 1, g] = inside / np.minimum(t + 1, w).astype(np.float32) - (s == t)
        win[:, 2, g] = (s - P > t - w) / np.float32(w)
    c["windows"] = win
    past = np.zeros((NB, POOL_STATE, 4, NB), np.float32)
    own = np.zeros((NB, 4, NB), np.float32)
    for g, w in enumerate(POOL_WINDOWS):
        for b in range(NB):
            past[b, POOL_STATE - (w - 1):, g, b] = 1.0 / w
            own[b, g, b] = 1.0 / w - 1.0
    c["windows_past"] = past.reshape(NB * POOL_STATE, 4, NB)
    c["windows_own"] = own
    half = HD // 2
    inv = np.power(np.float32(ROPE_THETA), -np.arange(half, dtype=np.float32) / np.float32(half)).astype(np.float32)
    pos = np.concatenate([np.arange(SEQ), np.full(P, PAST)]).astype(np.float32)
    ang = (pos[:, None] * inv[None, :]).astype(np.float32)
    cos, sin = np.cos(ang), np.sin(ang)
    rope = np.stack([np.concatenate([cos, cos], 1), np.concatenate([-sin, sin], 1)], 1)
    c["rope"] = rope.reshape(TT + 1, P, 2, HD).transpose(1, 0, 2, 3).astype(np.float32)
    row = np.zeros((NB, NB, P), np.float32)
    row[np.arange(NB), np.arange(NB)] = 1.0
    c["row_select"] = row
    col = np.zeros((P, 2 * NB - 1), np.float32)
    col[:, NB - 1] = 1.0
    c["col_select"] = col
    sel = np.zeros((ADA_CHUNKS, 32, ADA_CHUNKS, CC), np.float32)
    for j in range(ADA_CHUNKS):
        sel[j, np.arange(CC), j, np.arange(CC)] = 1.0
    c["ada_select"] = sel.reshape(P, ADA_CHUNKS, CC)
    c["spread_idx"] = np.repeat(np.eye(NB, dtype=np.float32), IDXH, 1)
    c["spread_heads"] = np.repeat(np.eye(NB, dtype=np.float32), NH, 1)
    c["gather_heads"] = np.ascontiguousarray(c["spread_heads"].T)
    return {k: np.ascontiguousarray(v, dtype=np.float32) for k, v in c.items()}


def build(nc, d):
    ctx = ExitStack()
    with ctx:
        cursor = [16512]

        def sb(name, shape, dt=F32, at=None):
            size = 4 * int(np.prod(shape[1:]))
            if at is None:
                at = cursor[0]
                cursor[0] += -(-size // 32) * 32
            assert at + size <= 229368, (name, at + size)
            return nc.alloc_sbuf_tensor_at(name, list(shape), dt, offset=at)

        x_at = cursor[0]
        x = sb("x", [P, KT, COLS])
        h_hi = sb("h_hi", [P, KT, SEQ + P], F32R)
        h_lo = sb("h_lo", [P, KT, SEQ + P], F32R)
        raw = [sb(f"raw{j}", [P, SLOT]) for j in range(2)]
        w_hi = [sb(f"w_hi{j}", [P, SLOT], F32R) for j in range(2)]
        w_lo = [sb(f"w_lo{j}", [P, SLOT], F32R) for j in range(2)]
        ada_w = [sb(f"ada_w{j}", [P, ADA_CHUNKS, ADA_N]) for j in range(2)]
        ada_row = sb("ada_row", [P, ADA_N])
        mod = [sb(f"mod{j}", [P, 24, CC]) for j in range(N_SUB)]
        ada_select = sb("ada_select", [P, ADA_CHUNKS, CC])
        ada_b = sb("ada_b", [P, DEPTH * N_SUB, 24])
        norm_g = sb("norm_g", [P, DEPTH * N_SUB, KT])
        cond = sb("cond", [P, KT, CC])
        ident = sb("ident", [P, P])
        ones = sb("ones", [P, P])
        lb = sb("lb", [P, DEPTH, HH])
        lb_rest = sb("lb_rest", [P, DEPTH, HH])
        lb_tmp = sb("lb_tmp", [P, 4, HH])
        onorm = sb("onorm", [P, DEPTH, HV])
        pool_scale = sb("pool_scale", [P, DEPTH, 2])
        col_select = sb("col_select", [P, 2 * NB - 1])
        spread_idx = sb("spread_idx", [NB, NB, IDXH])
        spread_heads = sb("spread_heads", [NB, NB * NH])
        gather_heads = sb("gather_heads", [NB * NH, NB])
        page_ids = sb("page_ids", [1, NB * PAGES], I32)
        x_tmp = sb("x_tmp", [P, NB])
        sqrt_warm = sb("sqrt_warm", [P, 1])
        base = cursor[0]

        def area(name, shape, at, dt=F32):
            return sb(name, shape, dt, base + at)

        mid_hi = area("mid_hi", [P, UP[0], COLS], 0, F32R)
        mid_lo = area("mid_lo", [P, UP[0], COLS], 24960, F32R)
        silu_g = area("silu_g", [P, 2, HALF], 49920)
        prod = area("prod", [P, 2, HALF], 52000)
        ada_first = [area(f"ada_first{n}", [P, ADA_CHUNKS, ADA_N], at) for n, at in enumerate(
            [6144 * n for n in range(5)] + [41984 + 6144 * n for n in range(3)] + [70720, 76864])]
        sq = area("sq", [P, COLS], 66560)
        sq_sum = area("sq_sum", [P, COLS], 68640)
        scaled = area("scaled", [P, KT, SEQ], 16640)
        diag = area("diag", [P, COLS], 33024)
        norm_ms = area("norm_ms", [P, 4, TT + 1], 35104)
        rstd = area("rstd", [P, COLS], 39264)
        h_s = area("h_s", [P, KT, NB], 41344)
        yab_hi = area("yab_hi", [P, 4, COLS], 0, F32R)
        yab_lo = area("yab_lo", [P, 4, COLS], 8320, F32R)
        yc_hi = area("yc_hi", [P, 4, COLS], 16640, F32R)
        yc_lo = area("yc_lo", [P, 4, COLS], 24960, F32R)
        gamma = area("gamma", [P, ROT, HD], 4160)
        rope = area("rope", [P, TT + 1, 2, HD], 12480)
        rot = area("rot", [P, TT + 1, ROT, HD], 16640)
        vals = area("vals", [P, TT + 1, NKV * HD], 35840)
        wi = area("wi", [P, TT + 1, IDXH], 38400)
        rotT = area("rotT", [P, 8, COLS], 38528)
        h_i = area("h_i", [P, TT + 1, HIW], 55168)
        h_g = area("h_g", [P, TT + 1, HIW], 60288)
        thin = area("thin", [HD + IDXH, SEQ + P], 8000)
        pool_u = area("pool_u", [P, TT + 1, 256], 65408)
        windows = area("windows", [P, 3, 4, P], 70528)
        pooled = area("pooled", [P, 2, COLS], 76672)
        pool_past = area("pool_past", [NB * POOL_STATE, 256], 80832)
        pool_w = area("pool_w", [P, 2, P], 81856)
        windows_past = area("windows_past", [NB * POOL_STATE, 4, NB], 82880)
        windows_own = area("windows_own", [NB, 4, NB], 83008)
        rot_a = area("rot_a", [P, ROT, HD], 65408)
        rot_b = area("rot_b", [P, ROT, HD], 69248)
        rot_c = area("rot_c", [P, ROT, HD], 73088)
        rot_d = area("rot_d", [P, ROT, HD], 76928)
        rot_ms = area("rot_ms", [P, 4, TT + 1, ROT], 83200)
        hq = [area(f"hq{j}", [P, COLS], (16640, 33536)[j]) for j in range(2)]
        hf = area("hf", [P, COLS], 18720)
        hk = area("hk", [P, COLS], 20800)
        pre = area("pre", [P, SEQ], 22880)
        suf = area("suf", [P, SEQ], 24928)
        att = area("att", [P, TT, P], 26976)
        kbT = area("kbT", [P, TT, P], 29024)
        chain = area("chain", [P, TT, HV], 31072)
        qm = [area(f"qm{j}", [P, SEQ], 65408 + 2048 * j) for j in range(2)]
        km = [area(f"km{j}", [P, SEQ], 69504 + 2048 * j) for j in range(2)]
        h_o = area("h_o", [P, TT + 1, HH, HV], 73600)
        levels = area("levels", [P, len(LEVELS), P], 78720)
        f_s = area("f_s", [P, HH, NB], 82816)
        k_s = area("k_s", [P, HH, NB], 82944)
        q_s = area("q_s", [P, HH, NB], 83072)
        decay = area("decay", [P, TT], 84224)
        state_p = area("state_p", [P, HH, HV], 83200)
        state_in = area("state_in", [P, NB, HH, HV], 16640)
        state_s = area("state_s", [P, NB, HH, HV], 24832)
        state_q = area("state_q", [P, NB, HH, HV], 65408)
        row_select = area("row_select", [NB, NB, P], 78720)
        o_sq = area("o_sq", [P, TT + 1, HH, HV], 65408)
        o_ms = area("o_ms", [P, 4, TT + 1, HH], 82816)
        rel = [area(f"rel{j}", [P, SEQ], 55168 + 2048 * j) for j in range(2)]
        score = area("score", [P, SEQ], 59264)
        work = area("work", [P, SEQ], 61312)
        mask = [area(f"mask{j}", [P, SEQ], 63360 + 2048 * j) for j in range(2)]
        probs = [area(f"probs{j}", [P, SEQ], 67456 + 2048 * j) for j in range(2)]
        probT = [area(f"probT{j}", [P, TT, P], 71552 + 2048 * j) for j in range(4)]
        o_tok = area("o_tok", [P, NH, HD], 79744)
        causal = area("causal", [P, SEQ], 81792)
        top8 = area("top8", [P, 8], 83840)
        row_max = area("row_max", [P, NH], 83872)
        neg_max = area("neg_max", [P, NH], 83904)
        row_sum = area("row_sum", [P, NH], 83936)
        row_inv = area("row_inv", [P, NH], 83968)
        k_page = area("k_page", [P, NB, PAGES, P], 38528)
        v_page = area("v_page", [P, NB, PAGES, P], 46720)
        ki_page = area("ki_page", [P, NB, PAGES, HD], 55168)
        kT_s = area("kT_s", [P, NB, LVIS], 59264)
        kiT_s = area("kiT_s", [HD, NB, LVIS], 67488)
        q_blk = area("q_blk", [P, NB, NB, NKV, 4], 75712)
        qi_blk = area("qi_blk", [HD, NB, NB, IDXH], 77760)
        prob_s = area("prob_s", [NB * NH, LVIS], 78784)
        rel_s = area("rel_s", [NB * IDXH, LVIS], 78784)
        score_s = area("score_s", [NB, LVIS], 79840)
        work_s = area("work_s", [NB, LVIS], 80896)
        mask_s = area("mask_s", [NB, LVIS], 81952)
        probT_blk = area("probT_blk", [P, PAGES, NB, NB * NH], 79840)
        rotT_s = area("rotT_s", [P, 8, NB], 33280)
        top8_s = area("top8_s", [NB, 8], 84192)
        st_s = area("st_s", [NB * NH, 4], 84224)
        wi_exp = area("wi_exp", [NB, NB, IDXH], 83008)
        wi_sel = area("wi_sel", [NB * IDXH, NB], 84256)
        own_diag = area("own_diag", [NB * NH, NB * NH], 75712)
        own_prob = area("own_prob", [NB, NB * NH], 75968)
        o_s = area("o_s", [NB * NH, P], 76224)
        mrg_hi = area("mrg_hi", [P, KT, COLS], 33280, F32R)
        mrg_lo = area("mrg_lo", [P, KT, COLS], 49920, F32R)
        gate_s = area("gate_s", [P, 6, COLS], 66560)
        gate_e = sb("gate_e", [P, EARLY_GATES, COLS], at=x_at)
        part = area("part", [P, 3, HALF], 79040)

        bank = [ctx.enter_context(nc.psum_tensor(f"bank{b}", [P, 512], F32)) for b in range(8)]
        ada_bank = bank[7]

        def sem(name):
            return ctx.enter_context(nc.semaphore(name))

        const_loaded = sem("const_loaded")
        x_loaded = sem("x_loaded")
        x_stored = sem("x_stored")
        x_restored = sem("x_restored")
        w_loaded = [sem(f"w_loaded{j}") for j in range(2)]
        head_split = [sem(f"head_split{j}") for j in range(2)]
        w_split = [sem(f"w_split{j}") for j in range(2)]
        ada_loaded = [sem(f"ada_loaded{j}") for j in range(2)]
        ada_first_loaded = [sem(f"ada_first_loaded{n}") for n in range(len(ada_first))]
        ada_used = [sem(f"ada_used{j}") for j in range(2)]
        ada_taken0 = sem("ada_taken0")
        ada_row_ready = sem("ada_row_ready")
        ada_turned = sem("ada_turned")
        ada_taken = sem("ada_taken")
        main_full = sem("main_full")
        main_taken = [sem(f"main_taken{b}") for b in range(4)]
        side_full = sem("side_full")
        side_taken = [sem(f"side_taken{b}") for b in range(3)]
        setup_done = sem("setup_done")
        cond_loaded = sem("cond_loaded")
        cond_ready = sem("cond_ready")
        lb_exp = sem("lb_exp")
        x_updated = sem("x_updated")
        diag_ready = sem("diag_ready")
        squared = sem("squared")
        root_ready = sem("root_ready")
        ms_ready = sem("ms_ready")
        scaled_ready = sem("scaled_ready")
        h_hi_ready = sem("h_hi_ready")
        h_lo_ready = sem("h_lo_ready")
        mid_hi_ready = sem("mid_hi_ready")
        mid_lo_ready = sem("mid_lo_ready")
        pool_loaded = sem("pool_loaded")
        rope_loaded = sem("rope_loaded")
        rot_squared = sem("rot_squared")
        rot_reduced = sem("rot_reduced")
        rot_scaled = sem("rot_scaled")
        rot_scale_ready = sem("rot_scale_ready")
        rotated = sem("rotated")
        rotated_pool = sem("rotated_pool")
        stored = sem("stored")
        y_hi_ready = sem("y_hi_ready")
        levels_loaded = sem("levels_loaded")
        pair_ready = sem("pair_ready")
        hf_used = sem("hf_used")
        chain_ready = sem("chain_ready")
        state_loaded = sem("state_loaded")
        state_ready = sem("state_ready")
        state_q_ready = sem("state_q_ready")
        yb_ready = sem("yb_ready")
        index_used = sem("index_used")
        causal_loaded = sem("causal_loaded")
        neg_max_ready = sem("neg_max_ready")
        probs_ready = sem("probs_ready")
        rotT_copied = sem("rotT_copied")
        ki_loaded = sem("ki_loaded")
        k_loaded = sem("k_loaded")
        v_loaded = sem("v_loaded")
        q_blk_ready = sem("q_blk_ready")
        wi_exp_ready = sem("wi_exp_ready")
        mask_s_ready = sem("mask_s_ready")
        s_neg_ready = sem("s_neg_ready")
        s_probs_ready = sem("s_probs_ready")
        own_diag_ready = sem("own_diag_ready")
        mrg_ready = sem("mrg_ready")
        mrg_hi_ready = sem("mrg_hi_ready")
        mrg_lo_ready = sem("mrg_lo_ready")
        vector_step = sem("vector_step")
        scalar_step = sem("scalar_step")
        pool_step = sem("pool_step")

        primed = main_taken + w_split + ada_used + [mrg_ready]

        def main_unit(l, stage, n=0):
            return LAYER_MAIN * l + MAIN0[stage] + n

        def side_unit(*key):
            n = SIDE[key]
            return n, n % 3, n // 3

        def wait_main(eng, unit):
            eng.wait_ge(main_full, unit + 1)

        def wait_side(eng, *key):
            n, b, _ = side_unit(*key)
            eng.wait_ge(side_full, n + 1)
            return bank[4 + b], side_taken[b]

        def wait_side_taken(eng, *key):
            n, b, use = side_unit(*key)
            eng.wait_ge(side_taken[b], use + 1)

        def main_use(l, stage, r=0):
            return (LAYER_MAIN * l + MAIN0[stage]) // 4 + r

        def slot_use(l, stage, r=0):
            return (LAYER_SLOTS * l + SLOT0[stage]) // 2 + r

        class Chain:

            def __init__(self, eng, semaphore):
                self.eng, self.sem, self.n, self.extra = eng, semaphore, 0, 0

            def link(self, ins):
                ins.then_inc(self.sem, 1)
                self.n += 1
                self.eng.wait_ge(self.sem, self.n + self.extra)

            def loop(self, i, per, count):
                self.extra = i * per
                self.per, self.count, self.start = per, count, self.n

            def end(self):
                assert self.n - self.start == self.per, (self.n - self.start, self.per)
                self.n = self.start + self.per * self.count
                self.extra = 0

        def half(hf):
            return slice(hf * HALF, (hf + 1) * HALF)

        def newton_rsqrt(chain_, mean, rt, tmp, out):
            v = nc.vector
            chain_.link(v.reciprocal(rt, rt))
            chain_.link(v.tensor_tensor(tmp, rt, rt, ALU.mult))
            chain_.link(v.scalar_tensor_tensor(out=tmp, in0=tmp, scalar=-0.5, in1=mean, op0=ALU.mult, op1=ALU.mult))
            chain_.link(v.scalar_tensor_tensor(out=out, in0=tmp, scalar=1.5, in1=rt, op0=ALU.add, op1=ALU.mult))

        def rotate(eng, chain_, t, a, b):
            hw = HD // 2
            chain_.link(eng.tensor_tensor(a[:], rot[:, t], rot_ms[:, 3, t, :].unsqueeze(2).to_broadcast([P, ROT, HD]),
                                          ALU.mult))
            eng.tensor_tensor(b[:, :, 0:hw], a[:, :, hw:HD],
                              rope[:, t, 1, 0:hw].unsqueeze(1).to_broadcast([P, ROT, hw]), ALU.mult)
            eng.tensor_tensor(b[:, :, hw:HD], a[:, :, 0:hw],
                              rope[:, t, 1, hw:HD].unsqueeze(1).to_broadcast([P, ROT, hw]), ALU.mult)
            chain_.link(eng.tensor_tensor(rot[:, t], a[:], rope[:, t, 0, :].unsqueeze(1).to_broadcast([P, ROT, HD]),
                                          ALU.mult))
            return eng.tensor_tensor(rot[:, t], rot[:, t], b[:], ALU.add)

        block = ctx.enter_context(nc.Block())

        @block.sync
        def _(sp):
            sp.dma_start(cond[:], d["cond"]).then_inc(cond_loaded, 16)

            def load_first(n):
                sp.dma_start(ada_first[n][:].rearrange("p a n -> p (a n)"), d["ada"][n]).then_inc(ada_first_loaded[n], 16)

            for n in range(2):
                load_first(n)
            for name, tile in (("ada_b", ada_b), ("norm_g", norm_g), ("ident", ident), ("hgrn_lb", lb),
                               ("pool_scale", pool_scale), ("col_select", col_select),
                               ("spread_idx", spread_idx), ("spread_heads", spread_heads),
                               ("gather_heads", gather_heads), ("page_table", page_ids),
                               ("ada_select", ada_select)):
                src = d[name]
                if name == "spread_idx":
                    src = src.rearrange("b (c h) -> b c h", h=IDXH)
                sp.dma_start(tile[:], src).then_inc(const_loaded, 16)
            sp.dma_start(onorm[:], d["hgrn_onorm"].partition_broadcast(P)).then_inc(const_loaded, 16)

            for k in range(2):
                sp.dma_start(x[:, 4 * k:4 * k + 4, :], d["x"][:, 4 * k:4 * k + 4, :]).then_inc(x_loaded, 16)
            for n in range(2, len(ada_first)):
                load_first(n)

            def load_ada(sub, r, j, place_is_new=False):
                use = sub * (ADA_SLOTS // 2) + r
                if not place_is_new:
                    sp.wait_ge(ada_used[j], use + PRIMED)
                sp.dma_start(ada_w[j][:].rearrange("p a n -> p (a n)"),
                             d["ada"][bass.ds(sub * ADA_SLOTS + 2 * r + j, 1)].rearrange("o p n -> p (o n)"))\
                  .then_inc(ada_loaded[j], 16)

            def load_w(l, stage, r, j):
                use = slot_use(l, stage, r)
                sp.wait_ge(w_split[j], use + PRIMED)
                n = USED[stage]
                sp.dma_start(raw[j][:, 0:n],
                             d["w"][bass.ds(l * LAYER_SLOTS + SLOT0[stage] + 2 * r + j, 1), :, 0:n]
                             .rearrange("o p n -> p (o n)")).then_inc(w_loaded[j], 16)

            for r in range(len(ada_first) // 2, ADA_SLOTS // 2):
                for j in range(2):
                    load_ada(0, r, j, place_is_new=(r == len(ada_first) // 2))
                if r == len(ada_first) // 2:
                    for j in range(2):
                        load_w(0, "up00", 0, j)

            sp.wait_ge(const_loaded, 16 * 12)
            pages = [sp.value_load(page_ids[0:1, n:n + 1], min_val=0, max_val=d["cache_k"].shape[1] - 1)
                     for n in range(NB * PAGES)]

            def load_pages(l, dst, src, loaded):
                for n, page in enumerate(pages):
                    sp.dma_start(dst[:, n // PAGES, n % PAGES, :],
                                 src[l, bass.ds(page, 1)].rearrange("o p n -> p (o n)")).then_inc(loaded, 16)

            def load_adas(sub, first, end):
                if sub < DEPTH * N_SUB:
                    with sp.Fori(first // 2, end // 2) as r:
                        for j in range(2):
                            load_ada(sub, r, j)

            for l in range(DEPTH):
                mix, after = N_SUB * l + 2, N_SUB * l + 3
                for stage, slots, _ in SEGMENTS:
                    early = 0
                    if stage in ("up00", "token", "up10", "merge"):
                        early = 1
                        for j in range(2):
                            if l > 0 or stage != "up00":
                                load_w(l, stage, 0, j)
                    if stage == "up00":
                        load_adas(N_SUB * l + 1, 0, ADA_NORM)
                    elif stage == "token":
                        load_adas(mix, 0, ADA_NORM)
                    elif stage == "up10":
                        load_adas(after, ADA_SLOTS - ADA_NORM, ADA_SLOTS)
                    elif stage == "merge":
                        load_adas(mix, KT, ADA_SLOTS)
                        load_adas(after, 0, KT + 2)
                        sp.wait_ge(index_used, INDEX_USES * (l + 1))
                        load_pages(l, ki_page, d["cache_ki"], ki_loaded)
                        load_adas(after, KT + 2, ADA_SLOTS - ADA_NORM)
                        sp.wait_ge(rotT_copied, l + 1)
                        sp.wait_ge(side_full, SIDE[(l, "logits", TT - 1, NH - 1)] + 1)
                        load_pages(l, k_page, d["cache_k"], k_loaded)
                        load_pages(l, v_page, d["cache_v"], v_loaded)
                    if stage == "down00":
                        for r in range(slots // 2):
                            for j in range(2):
                                load_w(l, stage, r, j)
                                if 2 * r >= ADA_NORM:
                                    load_ada(N_SUB * l + 1, r, j)
                        continue
                    with sp.Fori(early, slots // 2) as r:
                        for j in range(2):
                            load_w(l, stage, r, j)
                            if stage == "down01":
                                load_ada(N_SUB * l + 1, KT // 2 + r, j)
                    if stage == "gates1":
                        load_adas(mix, ADA_NORM, KT)
            sp.wait_ge(x_updated, x_updates(DEPTH * N_SUB))
            for k in range(2):
                sp.dma_start(d["y"][:, 4 * k:4 * k + 4, :], x[:, 4 * k:4 * k + 4, :]).then_inc(stored, 16)
            sp.wait_ge(stored, 16 * (2 + DEPTH * STORES))

        @block.gpsimd
        def _(pool):
            for semaphore in primed:
                pool.sem_inc(semaphore, PRIMED)
            pool.memset(ones[:], 1.0).then_inc(setup_done, 1)
            pool.memset(h_hi[:, :, COLS:].bitcast(F32), 0.0).then_inc(setup_done, 1)
            pool.memset(h_lo[:, :, COLS:].bitcast(F32), 0.0).then_inc(setup_done, 1)

            def split(l, stage, r, j):
                n = USED[stage]
                pool.wait_ge(head_split[j], slot_use(l, stage, r) + 1)
                pool.tensor_tensor(w_lo[j][:, 0:n], raw[j][:, 0:n], w_hi[j][:, 0:n].bitcast(F32),
                                   ALU.subtract).then_inc(w_split[j], 1)

            def square(sub, k):
                before = SQUARES * sub + 2 * k - 1
                if sub == 0:
                    if k == 0:
                        pool.wait_ge(x_loaded, 32)
                else:
                    pool.wait_ge(x_updated, x_updates(sub) - KT + k + 1)
                if k == 0:
                    pool.tensor_tensor(sq_sum[:], x[:, 0, :], x[:, 0, :], ALU.mult).then_inc(squared, 1)
                else:
                    pool.wait_ge(squared, before)
                    pool.tensor_tensor(sq[:], x[:, k, :], x[:, k, :], ALU.mult).then_inc(squared, 1)
                    pool.wait_ge(squared, before + 1)
                    pool.tensor_tensor(sq_sum[:], sq_sum[:], sq[:], ALU.add).then_inc(squared, 1)

            steps = Chain(pool, pool_step)

            def times_gamma(l):
                pool.wait_ge(rope_loaded, 32 * (l + 1))
                for t in range(TT + 1):
                    pool.wait_ge(rot_squared, 5 * l + t + 1)
                    pool.tensor_tensor(rot[:, t], rot[:, t], gamma[:], ALU.mult).then_inc(rot_scaled, 1)

            def rotary(l):
                pool.wait_ge(rot_scale_ready, l + 1)
                pool.wait_ge(rot_scaled, 5 * (l + 1))
                for t in range(ROT_DVE, TT + 1):
                    rotate(pool, steps, t, rot_c, rot_d).then_inc(rotated_pool, 1)
                    pool.wait_ge(rotated_pool, (TT + 1 - ROT_DVE) * l + t - ROT_DVE + 1)

            for k in range(KT):
                square(0, k)
            for l in range(DEPTH):
                for stage, slots, _ in SEGMENTS:
                    if stage == "hgrn":
                        times_gamma(l)
                        split(l, stage, 0, 0)
                        rotary(l)
                        for slot in range(1, slots):
                            split(l, stage, slot // 2, slot % 2)
                        continue
                    sub = N_SUB * l + {"down01": 1, "out": 2, "down11": 3}.get(stage, 0)
                    if sub == N_SUB * l or sub == N_SUB * DEPTH:
                        with pool.Fori(0, slots // 2) as r:
                            for j in range(2):
                                split(l, stage, r, j)
                        continue
                    per = KT // slots
                    for slot in range(slots + 2):
                        if slot < slots:
                            split(l, stage, slot // 2, slot % 2)
                        for k in range(per * (slot - 2), per * (slot - 1)):
                            if k >= 0:
                                square(sub, k)

        @block.scalar
        def _(act):
            steps = Chain(act, scalar_step)
            s = nc.scalar
            load_sp = act.dma_start

            act.wait_ge(setup_done, 3)
            act.wait_ge(cond_loaded, 16)
            s.activation(cond[:], cond[:], ACT.Silu).then_inc(cond_ready, 1)
            act.wait_ge(lb_exp, 1)
            s.activation(lb_tmp[:, 0:2, :], lb_tmp[:, 0:2, :], ACT.Exp).then_inc(lb_exp, 1)

            def head(l, stage, r, j, filled):
                act.wait_ge(w_loaded[j], 16 * (slot_use(l, stage, r) + 1))
                if filled is not None:
                    act.wait_ge(main_full, filled)
                n = USED[stage]
                s.copy(w_hi[j][:, 0:n], raw[j][:, 0:n]).then_inc(head_split[j], 1)

            stages = [(l, name, n) for l in range(DEPTH) for name, n, _ in SEGMENTS]

            def head_after(l, stage, slot):
                filled = LAYER_MAIN * l + MAIN0[stage] + slot_end(stage, slot)
                at = [i for i, (l_, name, _) in enumerate(stages) if (l_, name) == (l, stage)][0]
                ahead = slot + 2
                if ahead >= stages[at][2]:
                    ahead -= stages[at][2]
                    at += 1
                if at < len(stages):
                    head(stages[at][0], stages[at][1], ahead // 2, ahead % 2, filled)

            def down(l, stage):
                first = LAYER_MAIN * l + MAIN0[stage]
                per = slot_end(stage, 0)
                with act.Fori(0, SLOTS[stage] // 2 - 1) as r:
                    for j in range(2):
                        head(l, stage, r + 1, j, first + per * (2 * r + j + 1))
                for slot in (SLOTS[stage] - 2, SLOTS[stage] - 1):
                    head_after(l, stage, slot)

            def ffn_up(l, stage, tiles):
                first = LAYER_MAIN * l + MAIN0[stage]

                def turn(r, last):
                    for j in range(2):
                        for hf in range(2):
                            use = main_use(l, stage, 2 * r + j)
                            wait_main(act, main_unit(l, stage, 8 * r + 4 * j + 2 * hf))
                            act.wait_ge(main_taken[2 * hf + 1], use + PRIMED)
                            s.activation(silu_g[:, hf, :], bank[2 * hf][:, 0:HALF], ACT.Silu)\
                             .then_inc(main_taken[2 * hf], 1)
                            act.wait_ge(main_taken[2 * hf + 1], use + 1 + PRIMED)
                            s.copy(mid_hi[:, bass.ds(2 * r + j, 1), half(hf)].rearrange("p o n -> p (o n)"),
                                   prod[:, hf, :]).then_inc(mid_hi_ready, 1)
                        if last:
                            head_after(l, stage, 2 * r + j)
                        else:
                            head(l, stage, r + 1, j, first + 4 * (2 * r + j + 1))

                with act.Fori(0, tiles // 2 - 1) as r:
                    turn(r, False)
                turn(tiles // 2 - 1, True)

            def norm(sub):
                l, j3 = divmod(sub, N_SUB)
                md = mod[sub % N_SUB]
                s.activation(sqrt_warm[:], ones[:, 0:1], ACT.Sqrt)
                wait_side_taken(act, l, "norm", j3, 0)
                s.activation(norm_ms[:, 1], norm_ms[:, 0], ACT.Sqrt).then_inc(root_ready, 1)
                if sub == 0:
                    for j in range(2):
                        head(0, "up00", 0, j, None)
                roots[0] += 1
                if j3 == 1:
                    mixer_loads(l)
                act.wait_ge(scaled_ready, 9 * sub + 1)
                s.copy(h_hi[:, :, SEQ:COLS], h_s[:]).then_inc(h_hi_ready, 1)
                for k in range(KT):
                    act.wait_ge(scaled_ready, 9 * sub + 2 + k)
                    s.activation(h_hi[:, k, 0:SEQ], scaled[:, k, :], ACT.Identity,
                                 bias=md[:, k, 0:1]).then_inc(h_hi_ready, 1)
                if j3 == 1:
                    act.wait_ge(h_lo_ready, 9 * (sub + 1))
                    for k in range(2):
                        load_sp(d["y"][:, 4 * k:4 * k + 4, :], x[:, 4 * k:4 * k + 4, :]).then_inc(x_stored, 16)

            roots = [0]

            def mixer_loads(l):
                for dst, src in ((windows[:], d["windows"]), (pool_past[:], d["state_pool"][l]),
                                 (pool_w[:], d["pool_w"][l]), (windows_past[:], d["windows_past"]),
                                 (windows_own[:], d["windows_own"])):
                    load_sp(dst, src).then_inc(pool_loaded, 16)
                load_sp(gamma[:], d["gamma"][l].partition_broadcast(P)).then_inc(rope_loaded, 16)
                load_sp(rope[:], d["rope"]).then_inc(rope_loaded, 16)

            def token_major(l):
                heads = {3: slice(0, 8, 2), 4: slice(1, 8, 2), 6: slice(10, 14)}
                for slot in range(7):
                    for u in range(3):
                        n = 3 * slot + u
                        unit = main_unit(l, "token", n)
                        wait_main(act, unit)
                        tl = slice(2 * u, 2 * u + 2) if u < 2 else slice(TT, TT + 1)
                        nt = 2 if u < 2 else 1
                        src = bank[unit % 4][:, 0:256 * nt].rearrange("p (t n) -> p t n", t=nt)
                        done = main_taken[unit % 4]
                        if slot == 0:
                            s.copy(pool_u[:, tl, :], src).then_inc(done, 1)
                        elif slot == 1:
                            s.copy(h_i[:, tl, :], src).then_inc(done, 1)
                        elif slot == 2:
                            s.activation(h_g[:, tl, :], src, ACT.Silu).then_inc(done, 1)
                        elif slot in heads:
                            s.copy(rot[:, tl, heads[slot], :], src.rearrange("p t (h n) -> p t h n", n=HD)).then_inc(done, 1)
                        else:
                            s.copy(rot[:, tl, 8:10, :].rearrange("p t h n -> p t (h n)"), src[:, :, 0:P])
                            s.copy(vals[:, tl, :], src[:, :, P:2 * P]).then_inc(done, 1)
                    head_after(l, "token", slot)
                s.copy(thin[:, COLS:], h_hi[0:HD + IDXH, 0, COLS:].bitcast(F32))
                for hf in range(2):
                    unit = main_unit(l, "token", 21 + hf)
                    wait_main(act, unit)
                    s.copy(thin[:, half(hf)], bank[unit % 4][0:HD + IDXH, 0:HALF]).then_inc(main_taken[unit % 4], 1)
                unit = main_unit(l, "token", 23)
                wait_main(act, unit)
                src = bank[unit % 4][:, 0:(TT + 1) * (HD + IDXH)].rearrange("p (t n) -> p t n", t=TT + 1)
                s.copy(rot[:, :, 14, :], src[:, :, 0:HD])
                s.copy(wi[:], src[:, :, HD:HD + IDXH]).then_inc(main_taken[unit % 4], 1)
                head_after(l, "token", 7)

            def last_token_unit(eng, l, n=23):
                unit = main_unit(l, "token", n)
                eng.wait_ge(main_taken[unit % 4], unit // 4 + 1 + PRIMED)

            def pool_branch(l):
                last_token_unit(act, l, 2)
                act.dma_start(d["pool_p"][l], pool_u[P - POOL_STATE:P, TT - 1, :]).then_inc(stored, 16)
                act.dma_start(d["pool_s"][l, :, POOL_STATE - 1, :], pool_u[0:NB, TT, :]).then_inc(stored, 16)
                act.dma_start(d["pool_s"][l, :, 0:POOL_STATE - 1, :],
                              d["state_pool"][l].rearrange("(b j) c -> b j c", j=POOL_STATE)[:, 1:, :])\
                   .then_inc(stored, 16)
                for c in range(2):
                    src, done = wait_side(act, l, "pooled", c)
                    s.copy(pooled[:, c, 0:SEQ], src[:, :]).then_inc(done, 1)
                src, done = wait_side(act, l, "pooled", 2)
                s.copy(pooled[:, :, SEQ:COLS], src[:, 0:2 * NB].rearrange("p (c n) -> p c n", c=2)).then_inc(done, 1)
                for c in range(2):
                    for hf in range(2):
                        src, _ = wait_side(act, l, "ya", c, hf)
                        s.activation(yab_hi[:, c, half(hf)], src[:, 0:HALF], ACT.Copy,
                                     scale=pool_scale[:, l, c:c + 1]).then_inc(y_hi_ready, 1)

            def rotary(l):
                act.wait_ge(stored, 16 * (STORES * l + 3))
                for t in range(TT + 1):
                    if t >= 2:
                        act.wait_ge(rot_reduced, 5 * l + t - 1)
                    s.activation((rot_a, rot_b)[t % 2][:], rot[:, t], ACT.Square).then_inc(rot_squared, 1)
                s.activation(sqrt_warm[:], ones[:, 0:1], ACT.Sqrt)
                act.wait_ge(ms_ready, 2 * l + 1)
                s.activation(rot_ms[:, 1], rot_ms[:, 0], ACT.Sqrt).then_inc(root_ready, 1)
                early_gates(l, "gates0", (0, 1))
                act.wait_ge(rotated, ROT_DVE * (l + 1))
                act.wait_ge(rotated_pool, (TT + 1 - ROT_DVE) * (l + 1))
                act.dma_start(d["k_out"][l], rot[:, :, 8:10, :].rearrange("p t h n -> p t (h n)")).then_inc(stored, 16)
                act.dma_start(d["ki_out"][l], rot[:, :, 14, :]).then_inc(stored, 16)
                act.dma_start(d["v_out"][l], vals[:]).then_inc(stored, 16)
                for t in range(TT + 1):
                    n = P if t < TT else NB
                    for part_ in range(2):
                        src, done = wait_side(act, l, "rotT", t, part_)
                        s.copy(rotT[:, 4 * part_:4 * part_ + 4, t * P:t * P + n],
                               src[:, 0:4 * n].rearrange("p (g n) -> p g n", g=4)).then_inc(done, 1)
                act.wait_ge(stored, 16 * (STORES * l + 6))
                load_sp(levels[:], d["levels"]).then_inc(levels_loaded, 16)

            def early_gates(l, stage, slots):
                act.wait_ge(x_stored, 32 * (l + 1))
                for slot in slots:
                    for g in range(4):
                        wait_main(act, main_unit(l, stage, 4 * slot + g))
                        tile = 2 * slot + g // 2 + (EARLY_GATES // 2 if stage == "gates1" else 0)
                        s.activation(gate_e[:, tile, half(g % 2)], bank[g][:, 0:HALF], ACT.Sigmoid)\
                         .then_inc(main_taken[g], 1)
                    head_after(l, stage, slot)

            def hgrn(l):
                def projections(hd):
                    for hf in range(2):
                        wait_main(act, main_unit(l, "hgrn", 4 * hd + hf))
                        s.copy(hq[hd % 2][:, half(hf)], bank[hf][:, 0:HALF]).then_inc(main_taken[hf], 1)
                    if hd > 0:
                        act.wait_ge(hf_used, HH * l + hd)
                    for hf in range(2):
                        wait_main(act, main_unit(l, "hgrn", 4 * hd + 2 + hf))
                        s.activation(hf_t[:, half(hf)], bank[2 + hf][:, 0:HALF], ACT.Sigmoid)\
                         .then_inc(main_taken[2 + hf], 1)
                    head_after(l, "hgrn", hd)

                def outputs(hd):
                    src, done = wait_side(act, l, "o", hd)
                    s.copy(h_o[:, 0:TT, hd, :], src[:, 0:TT * HV].rearrange("p (c n) -> p c n", c=TT)).then_inc(done, 1)

                projections(0)
                for hd in range(HH):
                    if hd > 0:
                        outputs(hd - 1)
                    if hd + 1 < HH:
                        projections(hd + 1)
                    src, done = wait_side(act, l, "kbT", hd)
                    s.copy(kbT[:], src[:, :].rearrange("p (c n) -> p c n", c=TT)).then_inc(done, 1)
                outputs(HH - 1)
                act.wait_ge(chain_ready, HH * (l + 1))
                act.dma_start(d["hgrn_p"][l], state_p[:]).then_inc(stored, 16)
                load_sp(row_select[:], d["row_select"]).then_inc(state_loaded, 16)
                load_sp(state_in[:].rearrange("p b h v -> p (b h v)"), d["state_hgrn"][l]).then_inc(state_loaded, 16)
                early_gates(l, "gates1", (0,))
                src, done = wait_side(act, l, "o_sample")
                s.copy(h_o[0:NB, TT, :, :].rearrange("p h v -> p (h v)"), src[0:NB, 0:HIW]).then_inc(done, 1)
                act.wait_ge(state_ready, l + 1)
                act.dma_start(d["hgrn_s"][l], state_s[:].rearrange("p b h v -> p (b h v)")).then_inc(stored, 16)
                act.wait_ge(ms_ready, 2 * l + 2)
                s.activation(o_ms[:, 1], o_ms[:, 0], ACT.Sqrt).then_inc(root_ready, 1)
                early_gates(l, "gates1", (1,))
                for c in range(3):
                    src, _ = wait_side(act, l, "ybT", c)
                    if c < 2:
                        s.copy(yab_hi[:, 2 + c, 0:SEQ], src[:, :]).then_inc(y_hi_ready, 1)
                    else:
                        s.copy(yab_hi[:, 2:4, SEQ:COLS], src[:, 0:2 * NB].rearrange("p (c n) -> p c n", c=2))\
                         .then_inc(y_hi_ready, 1)

            def prompt_index(l, t):
                nk = (t + 1) * P
                for h in range(IDXH):
                    src, done = wait_side(act, l, "index", t, h)
                    uses = INDEX_USES * l + IDXH * t + h
                    if uses >= 2:
                        act.wait_ge(index_used, uses - 1)
                    s.activation(rel[h % 2][:, 0:nk], src[:, 0:nk], ACT.Relu, scale=IDX_SCALE).then_inc(done, 1)

            def prompt_attention(l, t):
                nk = (t + 1) * P
                for kind, h in attention_order():
                    if kind == "logits":
                        act.wait_ge(neg_max_ready, NH * (TT * l + t) + h + 1)
                        s.activation(probs[h % 2][:, 0:nk], probs[h % 2][:, 0:nk], ACT.Exp, scale=ATTN_SCALE,
                                     bias=neg_max[:, h:h + 1], accum_out=row_sum[:, h:h + 1]).then_inc(probs_ready, 1)
                    elif kind == "probT":
                        src, done = wait_side(act, l, "probT", t, h)
                        s.copy(probT[h % 4][:, 0:t + 1, :],
                               src[:, 0:nk].rearrange("p (b n) -> p b n", b=t + 1)).then_inc(done, 1)
                src, _ = wait_side(act, l, "ycT", t)
                s.copy(yc_hi[:, :, t * P:(t + 1) * P], src[:, :].rearrange("p (c n) -> p c n", c=4)).then_inc(y_hi_ready, 1)

            def sample_attention(l):
                wait_side_taken(act, l, "ycT", TT - 1)
                for j in range(2):
                    src, done = wait_side(act, l, "kiT_page", j)
                    for pg in range(PAGES):
                        last = s.copy(kiT_s[:, 4 * j:4 * j + 4, pg * P:(pg + 1) * P],
                                      src[pg * HD:(pg + 1) * HD, :].rearrange("p (b n) -> p b n", b=4))
                    last.then_inc(done, 1)
                src, done = wait_side(act, l, "s_index")
                s.activation(rel_s[:], src[0:NB * IDXH, 0:LVIS], ACT.Relu, scale=IDX_SCALE).then_inc(done, 1)
                src, done = wait_side(act, l, "s_wsel")
                s.copy(wi_sel[:], src[0:NB * IDXH, 0:NB]).then_inc(done, 1)
                for j in range(4):
                    src, done = wait_side(act, l, "kT_page", j)
                    s.copy(kT_s[:, 2 * j:2 * j + 2, 0:PAST], src[:, :].rearrange("p (b n) -> p b n", b=2)).then_inc(done, 1)
                act.wait_ge(s_neg_ready, l + 1)
                s.activation(prob_s[:], prob_s[:], ACT.Exp, scale=ATTN_SCALE, bias=st_s[:, 1:2],
                             accum_out=st_s[:, 2:3]).then_inc(s_probs_ready, 1)

            def merge(l):
                def gates(unit0, tile0, slots, next_head):
                    for slot in range(slots):
                        for g in range(4):
                            wait_main(act, main_unit(l, "merge", unit0 + 4 * slot + g))
                            s.activation(gate_s[:, tile0 + 2 * slot + g // 2, half(g % 2)], bank[g][:, 0:HALF],
                                         ACT.Sigmoid).then_inc(main_taken[g], 1)
                        next_head(slot)

                def merged(r):
                    for n in range(2):
                        for hf in range(2):
                            act.wait_ge(mrg_ready, 16 * l + 4 * r + 2 * n + hf + 1 + PRIMED)
                            s.copy(mrg_hi[:, bass.ds(2 * r + n, 1), half(hf)].rearrange("p o n -> p (o n)"),
                                   part[:, 2, :]).then_inc(mrg_hi_ready, 1)

                act.wait_ge(mrg_ready, 16 * l + PRIMED)
                gates(0, 2, 2, lambda slot: head_after(l, "merge", slot))
                for r in range(2):
                    merged(r)
                    head_after(l, "merge", 2 + r)
                for k in range(2):
                    load_sp(x[:, 4 * k:4 * k + 4, :], d["y"][:, 4 * k:4 * k + 4, :]).then_inc(x_restored, 16)
                first = LAYER_MAIN * l + MAIN0["merge"]

                def turn(r, last):
                    def next_head(slot):
                        if last:
                            head_after(l, "merge", 4 * (r - 1) + slot)
                        else:
                            ahead = slot + 2
                            head(l, "merge", 2 * (r - 1) + ahead // 2, ahead % 2,
                                 first + 24 * r + 8 + (4, 8, 12, 24)[slot] - 24)

                    act.wait_ge(mrg_ready, 16 * l + 4 * r + PRIMED)
                    gates(24 * r - 16, 0, 3, next_head)
                    merged(r)
                    next_head(3)

                with act.Fori(2, 3) as r:
                    turn(r, False)
                turn(3, True)

            hf_t = hf
            for l in range(DEPTH):
                norm(N_SUB * l)
                for p_ in range(2):
                    ffn_up(l, f"up0{p_}", UP[p_])
                    down(l, f"down0{p_}")
                norm(N_SUB * l + 1)
                token_major(l)
                pool_branch(l)
                rotary(l)
                hgrn(l)
                wait_side_taken(act, l, "ybT", 2)
                act.wait_ge(stored, 16 * STORES * (l + 1))
                load_sp(causal[:], d["causal"]).then_inc(causal_loaded, 16)
                prompt_index(l, 0)
                for t in range(TT):
                    if t + 1 < TT:
                        prompt_index(l, t + 1)
                    prompt_attention(l, t)
                sample_attention(l)
                merge(l)
                down(l, "out")
                norm(N_SUB * l + 2)
                for p_ in range(2):
                    ffn_up(l, f"up1{p_}", UP[p_])
                    down(l, f"down1{p_}")

        @block.vector
        def _(dve):
            v = nc.vector
            steps = Chain(dve, vector_step)
            link = steps.link

            def bc(ap, shape):
                return ap.to_broadcast(shape)

            v.memset(ada_bank[:], 0.0).then_inc(ada_taken0, 1)
            dve.wait_ge(const_loaded, 16 * 12)
            link(v.tensor_tensor(lb_tmp[:, 2], lb[:, 0], lb[:, 1], ALU.max))
            link(v.tensor_tensor(lb_tmp[:, 0], lb[:, 0], lb_tmp[:, 2], ALU.subtract))
            v.tensor_tensor(lb_tmp[:, 1], lb[:, 1], lb_tmp[:, 2], ALU.subtract).then_inc(lb_exp, 1)
            dve.wait_ge(lb_exp, 2)
            link(v.tensor_tensor(lb_tmp[:, 2], lb_tmp[:, 0], lb_tmp[:, 1], ALU.add))
            link(v.reciprocal(lb_tmp[:, 3], lb_tmp[:, 2]))
            link(v.tensor_tensor(lb_tmp[:, 0], lb_tmp[:, 0], lb_tmp[:, 3], ALU.mult))
            link(v.tensor_tensor(lb_tmp[:, 1], lb_tmp[:, 1], lb_tmp[:, 3], ALU.mult))
            link(v.tensor_tensor(lb_tmp[:, 1], lb_tmp[:, 0], lb_tmp[:, 1], ALU.add))
            link(v.tensor_tensor(lb[:, 0], lb_tmp[:, 0], lb_tmp[:, 0], ALU.subtract))
            link(v.tensor_tensor(lb[:, 1], lb_tmp[:, 1], lb_tmp[:, 0], ALU.subtract))
            link(v.tensor_scalar(lb_rest[:], lb[:], -1.0, 1.0, ALU.mult, ALU.add))

            def ada_rows(sub, hh):
                dve.wait_ge(ada_used[1], (ADA_SLOTS * sub + KT * (hh + 1)) // 2 + PRIMED)
                v.tensor_copy(ada_row[:], ada_bank[:, 0:ADA_N]).then_inc(ada_row_ready, 1)

            def ada_take(sub, hh):
                dve.wait_ge(ada_turned, 2 * sub + hh + 1)
                src = ada_bank[:, ADA_N:ADA_N + ADA_Q * ADA_CHUNKS * CC]
                tiles = "p (a h q) -> p h q a"
                v.tensor_tensor(mod[sub % N_SUB][:].rearrange("p (a h q) c -> p h q a c", h=2, q=ADA_Q)[:, hh],
                                src.rearrange("p (q a c) -> p q a c", q=ADA_Q, a=ADA_CHUNKS),
                                bc(ada_b[:, sub, :].rearrange(tiles, h=2, q=ADA_Q)[:, hh].unsqueeze(3),
                                   [P, ADA_Q, ADA_CHUNKS, CC]), ALU.add).then_inc(ada_taken, 1)

            def norm(sub):
                l, j3 = divmod(sub, N_SUB)
                md = mod[sub % N_SUB]
                dve.wait_ge(ada_taken, 2 * (sub + 1))
                link(v.scalar_tensor_tensor(out=md[:, 8:16, :], in0=md[:, 8:16, :], scalar=1.0,
                                            in1=bc(norm_g[:, sub, :].unsqueeze(2), [P, KT, CC]),
                                            op0=ALU.add, op1=ALU.mult))
                if j3 != 1:
                    link(v.tensor_scalar(md[:, 16:24, :], md[:, 16:24, :], 0.5, None, ALU.mult))
                if sub > 0:
                    statistics(sub)
                link(v.tensor_tensor(h_s[:], x[:, :, SEQ:COLS], md[:, 8:16, 1:CC], ALU.mult))
                link(v.tensor_tensor(h_s[:], h_s[:], bc(rstd[:, SEQ:COLS].unsqueeze(1), [P, KT, NB]), ALU.mult))
                v.tensor_tensor(h_s[:], h_s[:], md[:, 0:8, 1:CC], ALU.add).then_inc(scaled_ready, 1)
                for k in range(KT + 1):
                    if k < KT:
                        v.scalar_tensor_tensor(out=scaled[:, k, :], in0=x[:, k, 0:SEQ], scalar=md[:, 8 + k, 0:1],
                                               in1=rstd[:, 0:SEQ], op0=ALU.mult, op1=ALU.mult)\
                         .then_inc(scaled_ready, 1)
                    if k == 0:
                        dve.wait_ge(h_hi_ready, 9 * sub + 1)
                        dve.wait_ge(scaled_ready, 9 * sub + 1)
                        v.tensor_tensor(h_lo[:, :, SEQ:COLS], h_s[:], h_hi[:, :, SEQ:COLS].bitcast(F32),
                                        ALU.subtract).then_inc(h_lo_ready, 1)
                    else:
                        dve.wait_ge(h_hi_ready, 9 * sub + 1 + k)
                        v.scalar_tensor_tensor(out=h_lo[:, k - 1, 0:SEQ], in0=scaled[:, k - 1, :],
                                               scalar=md[:, k - 1, 0:1], in1=h_hi[:, k - 1, 0:SEQ].bitcast(F32),
                                               op0=ALU.add, op1=ALU.subtract).then_inc(h_lo_ready, 1)

            def statistics(sub):
                l, j3 = divmod(sub, N_SUB)
                src, done = wait_side(dve, l, "norm", j3, 0)
                v.tensor_scalar(norm_ms[:, 0], src[:, 0:TT + 1], 1.0 / D_MODEL, EPS, ALU.mult, ALU.add)\
                 .then_inc(done, 1)
                wait_side_taken(dve, l, "norm", j3, 0)
                dve.wait_ge(root_ready, 5 * l + (1, 2, 5)[j3])
                newton_rsqrt(steps, norm_ms[:, 0], norm_ms[:, 1], norm_ms[:, 2], norm_ms[:, 3])
                v.tensor_tensor(diag[:, 0:SEQ].rearrange("p (t n) -> p t n", t=TT), bc(ident[:].unsqueeze(1), [P, TT, P]),
                                bc(norm_ms[:, 3, 0:TT].unsqueeze(2), [P, TT, P]), ALU.mult)
                v.tensor_scalar(diag[:, SEQ:COLS], ident[:, P - NB:P], norm_ms[:, 3, TT:TT + 1], None, ALU.mult)\
                 .then_inc(diag_ready, 1)
                src, done = wait_side(dve, l, "norm", j3, 2)
                v.tensor_copy(rstd[:, SEQ:COLS], src[:, 0:NB]).then_inc(done, 1)
                src, done = wait_side(dve, l, "norm", j3, 1)
                v.tensor_copy(rstd[:, 0:SEQ], src[:, 0:SEQ]).then_inc(done, 1)
                for n in (1, 2):
                    wait_side_taken(dve, l, "norm", j3, n)

            def ffn_up(l, stage, tiles, count0):
                with dve.Fori(0, tiles // 2) as r:
                    for j in range(2):
                        for hf in range(2):
                            use = main_use(l, stage, 2 * r + j)
                            n = count0 + 4 * r + 2 * j + hf
                            wait_main(dve, main_unit(l, stage, 8 * r + 4 * j + 2 * hf + 1))
                            dve.wait_ge(main_taken[2 * hf], use + 1 + PRIMED)
                            v.tensor_tensor(prod[:, hf, :], silu_g[:, hf, :], bank[2 * hf + 1][:, 0:HALF],
                                            ALU.mult).then_inc(main_taken[2 * hf + 1], 1)
                            dve.wait_ge(main_taken[2 * hf + 1], use + 1 + PRIMED)
                            dve.wait_ge(mid_hi_ready, n + 1)
                            at = bass.ds(2 * r + j, 1)
                            v.tensor_tensor(mid_lo[:, at, half(hf)].rearrange("p o n -> p (o n)"), prod[:, hf, :],
                                            mid_hi[:, at, half(hf)].rearrange("p o n -> p (o n)").bitcast(F32),
                                            ALU.subtract).then_inc(mid_lo_ready, 1)

            def residual(l, stage, sub, per_slot, slots):
                md = mod[sub % N_SUB]
                tiles = per_slot * 2
                x0 = x_updates(sub) + (KT if stage in ("down01", "down11") else 0)
                links = tiles
                with dve.Fori(0, slots // 2) as r:
                    steps.loop(r, links, slots // 2)
                    for n in range(tiles):
                        at = r * tiles + n
                        for hf in range(2):
                            b = (2 * n + hf) % 4
                            wait_main(dve, main_unit(l, stage, 2 * tiles * r + 2 * n + hf))
                            if hf == 0:
                                cols = slice(0, HALF)
                            else:
                                cols = slice(HALF, SEQ)
                                link(v.tensor_tensor(x_tmp[:], bank[b][:, SEQ - HALF:HALF],
                                                     md[:, bass.ds(at + 16, 1), 1:CC].rearrange("p o c -> p (o c)"),
                                                     ALU.mult))
                            xs = x[:, bass.ds(at, 1), cols].rearrange("p o n -> p (o n)")
                            v.scalar_tensor_tensor(out=xs, in0=bank[b][:, 0:cols.stop - cols.start],
                                                   scalar=md[:, bass.ds(at + 16, 1), 0:1].rearrange("p o c -> p (o c)"),
                                                   in1=xs, op0=ALU.mult, op1=ALU.add).then_inc(main_taken[b], 1)
                        xs = x[:, bass.ds(at, 1), SEQ:COLS].rearrange("p o n -> p (o n)")
                        v.tensor_tensor(xs, xs, x_tmp[:], ALU.add).then_inc(x_updated, 1)
                        dve.wait_ge(x_updated, x0 + at + 1)
                    steps.end()

            def rotary(l):
                unit = main_unit(l, "token", 23)
                dve.wait_ge(main_taken[unit % 4], unit // 4 + 1 + PRIMED)
                dve.wait_ge(rope_loaded, 32 * (l + 1))
                for c in range(2):
                    for hf in range(2):
                        wait_side_taken(dve, l, "ya", c, hf)
                for t in range(TT + 1):
                    dve.wait_ge(rot_squared, 5 * l + t + 1)
                    v.reduce_sum(rot_ms[:, 0, t, :], (rot_a, rot_b)[t % 2][:], axis=AX.X).then_inc(rot_reduced, 1)
                dve.wait_ge(rot_reduced, 5 * (l + 1))
                v.tensor_scalar(rot_ms[:, 0], rot_ms[:, 0], 1.0 / HD, EPS, ALU.mult, ALU.add).then_inc(ms_ready, 1)
                dve.wait_ge(root_ready, 5 * l + 3)
                dve.wait_ge(ms_ready, 2 * l + 1)
                newton_rsqrt(steps, rot_ms[:, 0], rot_ms[:, 1], rot_ms[:, 2], rot_ms[:, 3])
                v.memset(rot_ms[:, 3, :, 10:14], 1.0).then_inc(rot_scale_ready, 1)
                dve.wait_ge(rot_scale_ready, l + 1)
                for t in range(ROT_DVE):
                    dve.wait_ge(rot_scaled, 5 * l + t + 1)
                    rotate(v, steps, t, rot_a, rot_b).then_inc(rotated, 1)
                    dve.wait_ge(rotated, ROT_DVE * l + t + 1)

            def ya_tails(l):
                for c in range(2):
                    for hf in range(2):
                        src, done = wait_side(dve, l, "ya", c, hf)
                        dve.wait_ge(y_hi_ready, Y_HEADS * l + 2 * c + hf + 1)
                        v.scalar_tensor_tensor(out=yab_lo[:, c, half(hf)], in0=src[:, 0:HALF],
                                               scalar=pool_scale[:, l, c:c + 1],
                                               in1=yab_hi[:, c, half(hf)].bitcast(F32),
                                               op0=ALU.mult, op1=ALU.subtract).then_inc(done, 1)

            def hgrn(l):
                wait_side_taken(dve, l, "rotT", TT, 1)
                dve.wait_ge(stored, 16 * (STORES * l + 6))
                v.tensor_copy(rotT_s[:], rotT[:, :, SEQ:COLS]).then_inc(rotT_copied, 1)
                dve.wait_ge(rotT_copied, l + 1)
                link(v.memset(h_o[:, TT], 0.0))
                pairs = [PAIRS * l]
                mixing = LEVELS[1:] + (P,)

                def start(hd):
                    dve.wait_ge(main_taken[1], main_use(l, "hgrn", hd) + 1 + PRIMED)
                    dve.wait_ge(main_taken[3], main_use(l, "hgrn", hd) + 1 + PRIMED)
                    link(v.tensor_scalar(hf[:], hf[:], lb_rest[:, l, hd:hd + 1], lb[:, l, hd:hd + 1], ALU.mult, ALU.add))
                    v.tensor_scalar(hk[:], hf[:], -1.0, 1.0, ALU.mult, ALU.add).then_inc(pair_ready, 1)
                    pairs[0] += 1
                    v.tensor_scalar(pre[:], hf[:, 0:SEQ], F_FLOOR, None, ALU.max)
                    v.memset(suf[:], 1.0)
                    v.tensor_scalar(f_s[:, hd, :], hf[:, SEQ:COLS], F_FLOOR, None, ALU.max).then_inc(hf_used, 1)
                    dve.wait_ge(pair_ready, pairs[0])
                    v.tensor_copy(k_s[:, hd, :], hk[:, SEQ:COLS])
                    link(v.tensor_copy(q_s[:, hd, :], hq[hd % 2][:, SEQ:COLS]))

                def pair(hd, n):
                    if n == 1 and hd > 0:
                        dve.wait_ge(side_full, SIDE[(l, "kbT", hd - 1)] + 1)
                    elif n >= 2:
                        dve.wait_ge(side_full, SIDE[(l, "level", hd, LEVELS[n - 1])] + 1)
                    to = hq[hd % 2][:, 0:SEQ] if mixing[n] == P else qm[n % 2][:]
                    v.tensor_tensor(to, hq[hd % 2][:, 0:SEQ], pre[:], ALU.mult)
                    v.tensor_tensor(km[n % 2][:], hk[:, 0:SEQ], suf[:], ALU.mult).then_inc(pair_ready, 1)
                    pairs[0] += 1

                def double(h):
                    pv = pre[:].rearrange("p (m a h) -> p m a h", a=2, h=h)
                    sv = suf[:].rearrange("p (m a h) -> p m a h", a=2, h=h)
                    m = SEQ // (2 * h)
                    dve.wait_ge(pair_ready, pairs[0])
                    link(v.tensor_tensor(sv[:, :, 0, :], sv[:, :, 0, :], bc(pv[:, :, 1, h - 1:h], [P, m, h]), ALU.mult))
                    link(v.tensor_tensor(pv[:, :, 1, :], pv[:, :, 1, :], bc(pv[:, :, 0, h - 1:h], [P, m, h]), ALU.mult))

                def scores(hd, n):
                    src, done = wait_side(dve, l, "level", hd, LEVELS[n])
                    sv = src[:, :].rearrange("p (c n) -> p c n", c=TT)
                    mk = bc(levels[:, n, :].unsqueeze(1), [P, TT, P])
                    if n == 0:
                        if hd == 0:
                            dve.wait_ge(levels_loaded, 16 * (l + 1))
                        else:
                            dve.wait_ge(side_full, SIDE[(l, "o", hd - 1)] + 1)
                        v.tensor_tensor(att[:], sv, mk, ALU.mult).then_inc(done, 1)
                    else:
                        wait_side_taken(dve, l, "level", hd, LEVELS[n - 1])
                        v.copy_predicated(att[:], mk.bitcast(U32), sv).then_inc(done, 1)

                def finish(hd):
                    scores(hd, len(LEVELS) - 1)
                    src, done = wait_side(dve, l, "delta", hd)
                    dl = src[:, 0:TT * HV].rearrange("p (c n) -> p c n", c=TT)
                    link(v.tensor_copy(chain[:, 0], dl[:, 0]))
                    for c in range(1, TT):
                        last = v.scalar_tensor_tensor(out=chain[:, c], in0=chain[:, c - 1], scalar=decay[:, c:c + 1],
                                                      in1=dl[:, c], op0=ALU.mult, op1=ALU.add)
                        if c < TT - 1:
                            link(last)
                    last.then_inc(done, 1)
                    wait_side_taken(dve, l, "delta", hd)
                    v.tensor_copy(state_p[:, hd], chain[:, TT - 1]).then_inc(chain_ready, 1)

                for hd in range(HH):
                    start(hd)
                    if hd > 0:
                        finish(hd - 1)
                    for n, h in enumerate(mixing):
                        pair(hd, n)
                        if h < P:
                            double(h)
                        else:
                            link(v.tensor_copy(decay[:], pre[:, P - 1:SEQ:P]))
                            dve.wait_ge(pair_ready, pairs[0])
                        if n > 0:
                            scores(hd, n - 1)
                finish(HH - 1)

                dve.wait_ge(state_loaded, 32 * (l + 1))
                dve.wait_ge(side_full, SIDE[(l, "o", HH - 1)] + 1)

                def over_v(tile, b0, nb):
                    return bc(tile[:, :, b0:b0 + nb].rearrange("p h b -> p b h").unsqueeze(3), [P, nb, HH, HV])

                for j in range(4):
                    bs = slice(2 * j, 2 * j + 2)
                    link(v.tensor_tensor(state_s[:, bs], state_in[:, bs], over_v(f_s, 2 * j, 2), ALU.mult))
                    src, done = wait_side(dve, l, "i_bcast", j)
                    v.tensor_tensor(state_in[:, bs], src[:, :].rearrange("p (b h v) -> p b h v", b=2, h=HH),
                                    over_v(k_s, 2 * j, 2), ALU.mult).then_inc(done, 1)
                    wait_side_taken(dve, l, "i_bcast", j)
                    last = v.tensor_tensor(state_s[:, bs], state_s[:, bs], state_in[:, bs], ALU.add)
                    if j < 3:
                        link(last)
                last.then_inc(state_ready, 1)
                dve.wait_ge(state_ready, l + 1)
                for j in range(4):
                    bs = slice(2 * j, 2 * j + 2)
                    last = v.tensor_tensor(state_q[:, bs], state_s[:, bs], over_v(q_s, 2 * j, 2), ALU.mult)
                last.then_inc(state_q_ready, 1)
                wait_side_taken(dve, l, "o_sample")
                wait_side_taken(dve, l, "o", HH - 1)
                link(v.tensor_tensor(o_sq[:], h_o[:], h_o[:], ALU.mult))
                link(v.reduce_sum(o_ms[:, 0], o_sq[:], axis=AX.X))
                v.tensor_scalar(o_ms[:, 0], o_ms[:, 0], 1.0 / HV, EPS, ALU.mult, ALU.add).then_inc(ms_ready, 1)
                dve.wait_ge(ms_ready, 2 * l + 2)
                dve.wait_ge(root_ready, 5 * l + 4)
                newton_rsqrt(steps, o_ms[:, 0], o_ms[:, 1], o_ms[:, 2], o_ms[:, 3])
                ov = h_o[:].rearrange("p t h v -> p (t h) v")
                link(v.tensor_tensor(ov, ov, bc(o_ms[:, 3].rearrange("p t h -> p (t h)").unsqueeze(2),
                                               [P, (TT + 1) * HH, HV]), ALU.mult))
                link(v.tensor_tensor(ov, ov, bc(onorm[:, l, :].unsqueeze(1), [P, (TT + 1) * HH, HV]), ALU.mult))
                v.tensor_tensor(h_o[:].rearrange("p t h v -> p t (h v)"), h_o[:].rearrange("p t h v -> p t (h v)"),
                                h_g[:], ALU.mult).then_inc(yb_ready, 1)
                for c in range(3):
                    src, done = wait_side(dve, l, "ybT", c)
                    dve.wait_ge(y_hi_ready, Y_HEADS * l + 4 + c + 1)
                    if c < 2:
                        v.tensor_tensor(yab_lo[:, 2 + c, 0:SEQ], src[:, :], yab_hi[:, 2 + c, 0:SEQ].bitcast(F32),
                                        ALU.subtract).then_inc(done, 1)
                    else:
                        v.tensor_tensor(yab_lo[:, 2:4, SEQ:COLS], src[:, 0:2 * NB].rearrange("p (c n) -> p c n", c=2),
                                        yab_hi[:, 2:4, SEQ:COLS].bitcast(F32), ALU.subtract).then_inc(done, 1)

            def prompt_index(l, t):
                nk = (t + 1) * P
                for h in range(IDXH):
                    wait_side_taken(dve, l, "index", t, h)
                    v.scalar_tensor_tensor(out=score[:, 0:nk], in0=rel[h % 2][:, 0:nk], scalar=wi[:, t, h:h + 1],
                                           in1=causal[:, SEQ - nk:SEQ] if h == 0 else score[:, 0:nk],
                                           op0=ALU.mult, op1=ALU.add).then_inc(index_used, 1)
                    dve.wait_ge(index_used, INDEX_USES * l + 4 * t + h + 1)

            def top_round(t, n):
                nk = (t + 1) * P
                src = score if n == 0 else work
                link(v.max(top8[:], src[:, 0:nk]))
                link(v.match_replace(out=work[:, 0:nk], in_to_replace=top8[:], in_values=src[:, 0:nk], imm_value=TAKEN))

            def make_mask(t):
                nk = (t + 1) * P
                if t == 0:
                    link(v.tensor_copy(mask[0][:, 0:nk], causal[:, SEQ - nk:SEQ]))
                else:
                    link(v.tensor_scalar(mask[t % 2][:, 0:nk], work[:, 0:nk], TAKEN, NEG_BIG, ALU.not_equal, ALU.mult))

            def prompt_attention(l, t):
                nk = (t + 1) * P
                rounds = list(range(TOP_PROMPT // 8)) if t + 1 < TT else []
                heads = NH * (TT * l + t)
                for kind, h in attention_order():
                    if kind == "logits":
                        src, done = wait_side(dve, l, "logits", t, h)
                        if h >= 2:
                            dve.wait_ge(side_full, SIDE[(l, "probT", t, h - 2)] + 1)
                        v.tensor_tensor_reduce(out=probs[h % 2][:, 0:nk], in0=src[:, 0:nk], in1=mask[t % 2][:, 0:nk],
                                               scale=1.0, scalar=TAKEN, op0=ALU.add, op1=ALU.max,
                                               accum_out=row_max[:, h:h + 1]).then_inc(done, 1)
                        wait_side_taken(dve, l, "logits", t, h)
                        v.tensor_scalar(neg_max[:, h:h + 1], row_max[:, h:h + 1], -ATTN_SCALE, None, ALU.mult)\
                         .then_inc(neg_max_ready, 1)
                        for _ in range(2):
                            if rounds:
                                top_round(t + 1, rounds.pop(0))
                    elif kind == "pv":
                        src, done = wait_side(dve, l, "pv", t, h)
                        dve.wait_ge(probs_ready, heads + 2 * h + 2)
                        link(v.reciprocal(row_inv[:, 2 * h:2 * h + 2], row_sum[:, 2 * h:2 * h + 2]))
                        v.tensor_tensor(o_tok[:, 2 * h:2 * h + 2, :], src[:, 0:2 * HD].rearrange("p (a n) -> p a n", a=2),
                                        bc(row_inv[:, 2 * h:2 * h + 2].unsqueeze(2), [P, 2, HD]), ALU.mult)\
                         .then_inc(done, 1)
                src, done = wait_side(dve, l, "ycT", t)
                dve.wait_ge(y_hi_ready, Y_HEADS * l + 7 + t + 1)
                v.tensor_tensor(yc_lo[:, :, t * P:(t + 1) * P], src[:, :].rearrange("p (c n) -> p c n", c=4),
                                yc_hi[:, :, t * P:(t + 1) * P].bitcast(F32), ALU.subtract).then_inc(done, 1)
                if t + 1 < TT:
                    make_mask(t + 1)
                sub, hh = N_SUB * l + 2 + t // 2, t % 2
                if sub in mixer_adas(l) and t < TT - 1:
                    ada_rows(sub, hh)
                    ada_take(sub, hh)

            def sample_attention(l):
                v.memset(q_blk[:], 0.0)
                link(v.memset(qi_blk[:], 0.0))
                qd = q_blk[:].rearrange("p c b n g -> p (c b) n g")
                for n in range(NKV):
                    ps = slice(n * HD, (n + 1) * HD)
                    v.tensor_copy(qd[ps, 0:NB * NB:NB + 1, n, :], rotT_s[ps, 0:4, :].rearrange("p g b -> p b g"))
                qi = qi_blk[:].rearrange("p c b h -> p (c b) h")
                for par in range(2):
                    last = v.tensor_copy(qi[:, 0:NB * NB:NB + 1, par:IDXH:2],
                                         rotT_s[par * HD:(par + 1) * HD, 5:7, :].rearrange("p g b -> p b g"))
                v.tensor_copy(kT_s[:, :, PAST], rotT_s[:, 4, :])
                v.tensor_copy(kiT_s[:, :, PAST], rotT_s[0:HD, 7, :]).then_inc(q_blk_ready, 1)
                v.tensor_tensor(wi_exp[:], spread_idx[:], bc(wi[0:NB, TT, :].unsqueeze(1), [NB, NB, IDXH]),
                                ALU.mult).then_inc(wi_exp_ready, 1)
                src, done = wait_side(dve, l, "s_score")
                v.tensor_copy(score_s[:], src[0:NB, 0:LVIS]).then_inc(done, 1)
                wait_side_taken(dve, l, "s_score")
                for n in range(TOP_SAMPLE // 8):
                    cur = score_s if n == 0 else work_s
                    link(v.max(top8_s[:], cur[:]))
                    link(v.match_replace(out=work_s[:], in_to_replace=top8_s[:], in_values=cur[:], imm_value=TAKEN))
                v.tensor_scalar(mask_s[:], work_s[:], TAKEN, NEG_BIG, ALU.not_equal, ALU.mult).then_inc(mask_s_ready, 1)
                src, done = wait_side(dve, l, "s_logits")
                v.tensor_copy(prob_s[:], src[0:NB * NH, 0:LVIS]).then_inc(done, 1)
                wait_side_taken(dve, l, "s_logits")
                link(v.reduce_max(st_s[:, 0:1], prob_s[:], axis=AX.X))
                v.tensor_scalar(st_s[:, 1:2], st_s[:, 0:1], -ATTN_SCALE, None, ALU.mult).then_inc(s_neg_ready, 1)
                link(v.memset(probT_blk[:], 0.0))
                dve.wait_ge(s_probs_ready, l + 1)
                link(v.reciprocal(st_s[:, 3:4], st_s[:, 2:3]))
                v.tensor_scalar(own_diag[:], ident[0:NB * NH, 0:NB * NH], prob_s[:, PAST:LVIS], None, ALU.mult)\
                 .then_inc(own_diag_ready, 1)
                src, done = wait_side(dve, l, "s_probT")
                for pg in range(PAGES):
                    dst = probT_blk[:, pg].rearrange("p c (b h) -> p (c b) h", h=NH)
                    v.tensor_copy(dst[:, 0:NB * NB:NB + 1, :],
                                  src[:, pg * NB * NH:(pg + 1) * NB * NH].rearrange("p (b h) -> p b h", h=NH))
                v.tensor_copy(own_prob[:], src[0:NB, 2 * NB * NH:3 * NB * NH]).then_inc(done, 1)
                src, done = wait_side(dve, l, "s_o")
                v.tensor_scalar(o_s[:], src[0:NB * NH, 0:P], st_s[:, 3:4], None, ALU.mult).then_inc(done, 1)
                src, done = wait_side(dve, l, "s_oT")
                sv = src[:, 0:NB * NH].rearrange("p (b n g) -> p b n g", n=NKV, g=4)
                for n in range(NKV):
                    for par in range(2):
                        dst = slice(par * HD, (par + 1) * HD)
                        frm = sv[n * HD:(n + 1) * HD, :, n, par:4:2].rearrange("p b g -> p g b")
                        link(v.tensor_copy(yc_hi[dst, 2 * n:2 * n + 2, SEQ:COLS], frm))
                for n in range(NKV):
                    for par in range(2):
                        dst = slice(par * HD, (par + 1) * HD)
                        frm = sv[n * HD:(n + 1) * HD, :, n, par:4:2].rearrange("p b g -> p g b")
                        last = v.tensor_tensor(yc_lo[dst, 2 * n:2 * n + 2, SEQ:COLS], frm,
                                               yc_hi[dst, 2 * n:2 * n + 2, SEQ:COLS].bitcast(F32), ALU.subtract)
                last.then_inc(done, 1)

            def merge(l):
                def turn(r, gate):
                    group = projections_at(r)
                    for n in range(2):
                        for hf in range(2):
                            for b in range(3):
                                g = 6 * n + 3 * hf + b
                                wait_main(dve, main_unit(l, "merge", 4 * group + g))
                                if b == 0:
                                    dve.wait_ge(main_taken[3], main_use(l, "merge", group) + PRIMED)
                                last = v.tensor_tensor(part[:, b, :], gate(3 * n + b)[:, half(hf)],
                                                       bank[g % 4][:, 0:HALF], ALU.mult)
                                last.then_inc(main_taken[g % 4], 1)
                                dve.wait_ge(main_taken[g % 4], main_use(l, "merge", group + g // 4) + 1 + PRIMED)
                            link(v.tensor_tensor(part[:, 0, :], part[:, 0, :], part[:, 1, :], ALU.add))
                            v.tensor_tensor(part[:, 2, :], part[:, 0, :], part[:, 2, :], ALU.add).then_inc(mrg_ready, 1)
                            dve.wait_ge(mrg_ready, 16 * l + 4 * r + 2 * n + hf + 1 + PRIMED)
                            dve.wait_ge(mrg_hi_ready, 16 * l + 4 * r + 2 * n + hf + 1)
                            at = bass.ds(2 * r + n, 1)
                            v.tensor_tensor(mrg_lo[:, at, half(hf)].rearrange("p o n -> p (o n)"), part[:, 2, :],
                                            mrg_hi[:, at, half(hf)].rearrange("p o n -> p (o n)").bitcast(F32),
                                            ALU.subtract).then_inc(mrg_lo_ready, 1)

                for r in range(2):
                    turn(r, lambda tile: (gate_e[:, 6 * r + tile] if 6 * r + tile < EARLY_GATES else gate_s[:, tile]))
                with dve.Fori(2, 4) as r:
                    steps.loop(r - 2, 4, 2)
                    turn(r, lambda tile: gate_s[:, tile])
                    steps.end()
                dve.wait_ge(x_restored, 32 * (l + 1))

            for hh in range(2):
                ada_rows(0, hh)
                ada_take(0, hh)
                if hh == 0:
                    statistics(0)
            mids = 0
            for l in range(DEPTH):
                for f in range(2):
                    sub = N_SUB * l + 2 * f
                    norm(sub)
                    if f == 1 and sub + 1 < DEPTH * N_SUB:
                        ada_rows(sub + 1, 1)
                    for p_ in range(2):
                        ffn_up(l, f"up{f}{p_}", UP[p_], mids)
                        mids += 2 * UP[p_]
                        if f == 0 and p_ == 1:
                            ada_take(sub + 1, 0)
                        if f == 1 and p_ == 0 and sub + 1 < DEPTH * N_SUB:
                            ada_take(sub + 1, 1)
                        residual(l, f"down{f}{p_}", sub, 1, KT)
                        if f == 0:
                            ada_rows(sub + 1, p_)
                    if f == 0:
                        ada_take(sub + 1, 1)
                        norm(sub + 1)
                        ya_tails(l)
                        rotary(l)
                        hgrn(l)
                        dve.wait_ge(causal_loaded, 16 * (l + 1))
                        prompt_index(l, 0)
                        make_mask(0)
                        for t in range(TT):
                            if t + 1 < TT:
                                prompt_index(l, t + 1)
                            prompt_attention(l, t)
                        sample_attention(l)
                        merge(l)
                        residual(l, "out", sub + 1, 2, 4)

        @block.tensor
        def _(pe):
            mm = nc.tensor.matmul
            order = [0]

            def open_side(*key):
                n, b, use = side_unit(*key)
                assert n == order[0], (key, n, order[0])
                order[0] += 1
                if use > 0:
                    pe.wait_ge(side_taken[b], use)
                return bank[4 + b]

            def product(out, blocks, ws, xs):
                (wh, wl), (xh, xl) = ws, xs
                for n, (wb, xb) in enumerate(blocks):
                    mm(out, wh(wb), xh(xb), start=(n == 0), stop=False)
                    mm(out, wl(wb), xh(xb), start=False, stop=False)
                    last = mm(out, wh(wb), xl(xb), start=False, stop=(n == len(blocks) - 1))
                return last

            def weights(j):
                def blk(tile):
                    return lambda n: tile[:, n * P:(n + 1) * P]
                return blk(w_hi[j]), blk(w_lo[j])

            def moving(hi, lo, hf):
                return (lambda k: hi[:, k, half(hf)]), (lambda k: lo[:, k, half(hf)])

            def wait_slot(l, stage, r, j):
                pe.wait_ge(w_split[j], slot_use(l, stage, r) + 1 + PRIMED)

            def take_main(b, use):
                pe.wait_ge(main_taken[b], use + PRIMED)

            def ada(sub, n):
                j, k = n % 2, n % KT
                if sub == 0 and n < len(ada_first):
                    pe.wait_ge(ada_first_loaded[n], 16)
                    src = ada_first[n]
                else:
                    pe.wait_ge(ada_loaded[j], 16 * (ADA_SLOTS * sub // 2 + n // 2 + 1 - len(ada_first) // 2))
                    src = ada_w[j]
                if sub + n == 0:
                    pe.wait_ge(ada_taken0, 1)
                elif k == 0:
                    pe.wait_ge(ada_taken, 2 * sub + n // KT)
                for a in range(ADA_CHUNKS):
                    last = mm(ada_bank[32 * a:32 * a + CC, 0:ADA_N], cond[:, k, :], src[:, a, :],
                              start=(k == 0), stop=(k == KT - 1))
                last.then_inc(ada_used[j], 1)

            def ada_turn(sub, hh):
                pe.wait_ge(ada_row_ready, 2 * sub + hh + 1)
                for q in range(ADA_Q):
                    at = ADA_N + q * ADA_CHUNKS * CC
                    last = mm(ada_bank[:, at:at + ADA_CHUNKS * CC], ada_row[:, q * P:(q + 1) * P],
                              ada_select[:].rearrange("p a c -> p (a c)"), start=True, stop=True)
                last.then_inc(ada_turned, 1)

            def norm(sub):
                first = ADA_SLOTS - ADA_NORM if sub % N_SUB == 2 else 0
                beside = [n for n in range(first, first + ADA_NORM) if sub + 1 < DEPTH * N_SUB]
                for n in beside[:2]:
                    ada(sub + 1, n)
                if sub > 0:
                    statistics(sub)
                for n in beside[2:]:
                    ada(sub + 1, n)

            def statistics(sub):
                l, j3 = divmod(sub, N_SUB)
                out = open_side(l, "norm", j3, 0)
                pe.wait_ge(squared, SQUARES * (sub + 1))
                for t in range(TT + 1):
                    cols = slice(t * P, (t + 1) * P) if t < TT else slice(COLS - P, COLS)
                    last = mm(out[:, t:t + 1], sq_sum[:, cols], ones[:, 0:1], start=True, stop=True)
                last.then_inc(side_full, 1)
                outs = [open_side(l, "norm", j3, n) for n in (1, 2)]
                pe.wait_ge(diag_ready, sub + 1)
                for out, cols in zip(outs, (slice(0, SEQ), slice(SEQ, COLS))):
                    mm(out[:, 0:cols.stop - cols.start], ones[:], diag[:, cols], start=True, stop=True)\
                        .then_inc(side_full, 1)

            def wait_h(sub, k):
                pe.wait_ge(h_lo_ready, 9 * sub + k + 2)

            def split_products(outs, ks, w, xs):
                for out, k, (wh, wl), (xh, xl) in zip(outs, ks, w, xs):
                    mm(out, wh, xh, start=(k == 0), stop=False)
                    mm(out, wl, xh, start=False, stop=False)
                    last = mm(out, wh, xl, start=False, stop=(k == KT - 1))
                    if k == KT - 1:
                        last.then_inc(main_full, 1)

            def ffn_up(l, stage, tiles, sub=None):
                if sub is not None:
                    wait_slot(l, stage, 0, 0)
                    for b in range(4):
                        take_main(b, main_use(l, stage))
                    for k in range(KT):
                        wait_h(sub, k)
                        outs = [bank[b][:, 0:HALF] for b in range(4)]
                        w = [tuple(tile((b % 2) * KT + k) for tile in weights(0)) for b in range(4)]
                        xs = [tuple(tile(k) for tile in moving(h_hi, h_lo, b // 2)) for b in range(4)]
                        split_products(outs, [k] * 4, w, xs)
                    up_slot(l, stage, 0, 1)
                with pe.Fori(0 if sub is None else 1, tiles // 2) as r:
                    for j in range(2):
                        up_slot(l, stage, r, j)

            def up_slot(l, stage, r, j):
                wait_slot(l, stage, r, j)
                use = main_use(l, stage, 2 * r + j)
                for hf in range(2):
                    for which in range(2):
                        take_main(2 * hf + which, use)
                        product(bank[2 * hf + which][:, 0:HALF], [(which * KT + k, k) for k in range(KT)],
                                (lambda n: weights(j)[0](n), lambda n: weights(j)[1](n)),
                                moving(h_hi, h_lo, hf)).then_inc(main_full, 1)

            def down(l, stage, tiles, mids, ada_sub, hh):
                pe.wait_ge(mid_lo_ready, mids)

                def slot(r, j):
                    wait_slot(l, stage, r, j)
                    for hf in range(2):
                        take_main(2 * j + hf, main_use(l, stage, r))
                        product(bank[2 * j + hf][:, 0:HALF], [(k, k) for k in range(tiles)], weights(j),
                                moving(mid_hi, mid_lo, hf)).then_inc(main_full, 1)

                if ada_sub is None:
                    with pe.Fori(0, KT // 2) as r:
                        for j in range(2):
                            slot(r, j)
                else:
                    for n in range(KT):
                        slot(n // 2, n % 2)
                        if hh == 1 or n >= ADA_NORM:
                            ada(ada_sub, KT * hh + n)

            def token_major(l):
                def tile(slot, u, i, k):
                    j = slot % 2
                    t = 2 * u + i
                    out = bank[main_unit(l, "token", 3 * slot + u) % 4][:, 256 * i:256 * (i + 1)]
                    cols = slice(t * P, (t + 1) * P)
                    wcols = slice(k * 256, (k + 1) * 256)
                    mm(out, h_hi[:, k, cols], w_hi[j][:, wcols], start=(k == 0), stop=False)
                    mm(out, h_lo[:, k, cols], w_hi[j][:, wcols], start=False, stop=False)
                    return mm(out, h_hi[:, k, cols], w_lo[j][:, wcols], start=False, stop=(k == KT - 1))

                for slot in range(7):
                    wait_slot(l, "token", slot // 2, slot % 2)
                    if slot == 0:
                        for u in range(3):
                            take_main(u, main_use(l, "token"))
                        for k in range(KT):
                            wait_h(N_SUB * l + 1, k)
                            for u in range(3 if k < KT - 1 else 2):
                                tile(0, u, 0, k)
                    for u in range(3):
                        unit = main_unit(l, "token", 3 * slot + u)
                        if slot > 0:
                            take_main(unit % 4, unit // 4)
                        for i in range(2 if u < 2 else 1):
                            first_k = 0 if slot > 0 or i > 0 else KT - (u == 2)
                            for k in range(first_k, KT):
                                last = tile(slot, u, i, k)
                        last.then_inc(main_full, 1)
                wait_slot(l, "token", 3, 1)
                thin_cols = lambda w: (lambda k: w[:, k * 256:k * 256 + HD + IDXH])
                for hf in range(2):
                    unit = main_unit(l, "token", 21 + hf)
                    take_main(unit % 4, unit // 4)
                    product(bank[unit % 4][0:HD + IDXH, 0:HALF], [(k, k) for k in range(KT)],
                            (thin_cols(w_hi[1]), thin_cols(w_lo[1])), moving(h_hi, h_lo, hf)).then_inc(main_full, 1)
                unit = main_unit(l, "token", 23)
                take_main(unit % 4, unit // 4)
                for n in (21, 22):
                    token_tile_wait(l, n)
                for t in range(TT + 1):
                    last = nc.tensor.transpose(bank[unit % 4][:, t * (HD + IDXH):(t + 1) * (HD + IDXH)],
                                               thin[:, t * P:(t + 1) * P], ident[0:HD + IDXH, 0:HD + IDXH])
                last.then_inc(main_full, 1)

            def token_tile_wait(l, n):
                unit = main_unit(l, "token", n)
                pe.wait_ge(main_taken[unit % 4], unit // 4 + 1 + PRIMED)

            def pool_branch(l):
                pe.wait_ge(pool_loaded, 80 * (l + 1))
                token_tile_wait(l, 2)
                for c in range(2):
                    out = open_side(l, "pooled", c)
                    for g in (2 * c, 2 * c + 1):
                        rows = slice((g % 2) * 64, (g % 2) * 64 + 64)
                        ch = slice(g * POOL_G, (g + 1) * POOL_G)
                        for t in range(TT):
                            o = out[rows, t * P:(t + 1) * P]
                            last = mm(o, pool_u[:, t, ch], windows[:, 1 if t == 0 else 0, g, :], start=True, stop=(t == 0))
                            if t > 0:
                                last = mm(o, pool_u[:, t - 1, ch], windows[:, 2, g, :], start=False, stop=True)
                    last.then_inc(side_full, 1)
                out = open_side(l, "pooled", 2)
                for g in range(4):
                    rows = slice((g % 2) * 64, (g % 2) * 64 + 64)
                    ch = slice(g * POOL_G, (g + 1) * POOL_G)
                    o = out[rows, (g // 2) * NB:(g // 2 + 1) * NB]
                    mm(o, pool_past[:, ch], windows_past[:, g, :], start=True, stop=False)
                    last = mm(o, pool_u[0:NB, TT, ch], windows_own[:, g, :], start=False, stop=True)
                last.then_inc(side_full, 1)
                for c in range(2):
                    wait_side_taken(pe, l, "pooled", c)
                wait_side_taken(pe, l, "pooled", 2)
                for c in range(2):
                    for hf in range(2):
                        out = open_side(l, "ya", c, hf)
                        mm(out[:, 0:HALF], pool_w[:, c, :], pooled[:, c, half(hf)], start=True, stop=True)\
                            .then_inc(side_full, 1)

            def rotary(l):
                for t in range(TT + 1):
                    n = P if t < TT else NB
                    if t < ROT_DVE:
                        pe.wait_ge(rotated, ROT_DVE * l + t + 1)
                    else:
                        pe.wait_ge(rotated_pool, (TT + 1 - ROT_DVE) * l + t - ROT_DVE + 1)
                    rt = rot[0:n, t]
                    for part_ in range(2):
                        out = open_side(l, "rotT", t, part_)
                        for i in range(4 if part_ == 0 else 3):
                            row = 8 * part_ + 2 * i
                            last = nc.tensor.transpose(out[:, i * n:(i + 1) * n],
                                                       rt[:, row:row + 2, :].rearrange("p a e -> p (a e)"), ident[0:n, 0:n])
                        if part_ == 1:
                            for a in range(2):
                                last = mm(out[a * HD:(a + 1) * HD, 3 * n:4 * n], rt[:, ROT - 1, :], ident[0:n, 0:n],
                                          start=True, stop=True)
                        last.then_inc(side_full, 1)

            def hgrn_projection(l, hd, b):
                which, hf = divmod(b, 2)
                wait_slot(l, "hgrn", hd // 2, hd % 2)
                take_main(b, main_use(l, "hgrn", hd))
                product(bank[b][:, 0:HALF], [(which * KT + k, k) for k in range(KT)], weights(hd % 2),
                        moving(h_hi, h_lo, hf)).then_inc(main_full, 1)

            def hgrn(l):
                pairs = PAIRS * l
                fin = len(LEVELS[1:]) % 2

                def outputs(hd):
                    vs = slice(hd * HV, (hd + 1) * HV)
                    out = open_side(l, "o", hd)
                    wait_side_taken(pe, l, "delta", hd)
                    wait_side_taken(pe, l, "level", hd, LEVELS[-1])
                    for c in range(TT):
                        o = out[:, c * HV:(c + 1) * HV]
                        last = mm(o, att[:, c, :], h_i[:, c, vs], start=True, stop=(c == 0))
                        if c > 0:
                            last = mm(o, hq[hd % 2][:, c * P:(c + 1) * P], chain[:, c - 1, :], start=False, stop=True)
                    last.then_inc(side_full, 1)

                for hd in range(HH):
                    for n, h in enumerate(LEVELS):
                        if hd + 1 < HH and 4 <= n < 8:
                            hgrn_projection(l, hd + 1, n - 4)
                        out = open_side(l, "level", hd, h)
                        pairs += 1
                        pe.wait_ge(pair_ready, pairs)
                        for c in range(TT):
                            cs = slice(c * P, (c + 1) * P)
                            kt, qt = (hk, hq[hd % 2]) if n == 0 else (km[(n - 1) % 2], qm[(n - 1) % 2])
                            last = mm(out[:, cs], kt[:, cs], qt[:, cs], start=True, stop=True)
                        last.then_inc(side_full, 1)
                        if n == 0 and hd > 0:
                            outputs(hd - 1)
                        if hd == HH - 1 and 4 <= n < 4 + KT - ADA_NORM:
                            ada(N_SUB * l + 2, ADA_NORM + n - 4)
                    pairs += 1
                    pe.wait_ge(pair_ready, pairs)
                    out = open_side(l, "kbT", hd)
                    for c in range(TT):
                        cs = slice(c * P, (c + 1) * P)
                        last = nc.tensor.transpose(out[:, cs], km[fin][:, cs], ident[:])
                    last.then_inc(side_full, 1)
                    vs = slice(hd * HV, (hd + 1) * HV)
                    out = open_side(l, "delta", hd)
                    wait_side_taken(pe, l, "kbT", hd)
                    for c in range(TT):
                        last = mm(out[:, c * HV:(c + 1) * HV], kbT[:, c, :], h_i[:, c, vs], start=True, stop=True)
                    last.then_inc(side_full, 1)
                outputs(HH - 1)
                gates(l, "gates1", 0, 0, 0, (0,))
                pe.wait_ge(state_loaded, 32 * (l + 1))
                for j in range(4):
                    out = open_side(l, "i_bcast", j)
                    for i in range(2):
                        last = mm(out[:, i * HIW:(i + 1) * HIW], row_select[:, 2 * j + i, :], h_i[0:NB, TT, :],
                                  start=True, stop=True)
                    last.then_inc(side_full, 1)
                gates(l, "gates1", 0, 0, 0, (1,))
                out = open_side(l, "o_sample")
                pe.wait_ge(state_q_ready, l + 1)
                for b in range(NB):
                    last = mm(out[0:NB, 0:HIW], col_select[:, NB - 1 - b:2 * NB - 1 - b],
                              state_q[:, b].rearrange("p h v -> p (h v)"), start=(b == 0), stop=(b == NB - 1))
                last.then_inc(side_full, 1)
                gates(l, "gates1", 0, 1, 1)
                pe.wait_ge(yb_ready, l + 1)
                for c in range(2):
                    out = open_side(l, "ybT", c)
                    for t in range(TT):
                        src = h_o[:, t].rearrange("p h v -> p (h v)")
                        last = nc.tensor.transpose(out[:, t * P:(t + 1) * P], src[:, c * P:(c + 1) * P], ident[:])
                    last.then_inc(side_full, 1)
                out = open_side(l, "ybT", 2)
                for c in range(2):
                    src = h_o[0:NB, TT].rearrange("p h v -> p (h v)")
                    last = nc.tensor.transpose(out[:, c * NB:(c + 1) * NB], src[:, c * P:(c + 1) * P], ident[0:NB, 0:NB])
                last.then_inc(side_full, 1)

            def prompt_index(l, t):
                nk = (t + 1) * P
                for h in range(IDXH):
                    out = open_side(l, "index", t, h)
                    rows = slice((h % 2) * HD, (h % 2 + 1) * HD)
                    mm(out[:, 0:nk], rotT[rows, 5 + h // 2, t * P:(t + 1) * P], rotT[rows, 7, 0:nk],
                       start=True, stop=True).then_inc(side_full, 1)

            def prompt_attention(l, t):
                nk = (t + 1) * P
                sub, hh = N_SUB * l + 2 + t // 2, t % 2
                for kind, h in attention_order():
                    out = open_side(l, kind, t, h)
                    if kind == "logits":
                        n, g = divmod(h, 4)
                        rows = slice(n * HD, (n + 1) * HD)
                        last = mm(out[:, 0:nk], rotT[rows, g, t * P:(t + 1) * P], rotT[rows, 4, 0:nk], start=True, stop=True)
                    elif kind == "probT":
                        pe.wait_ge(probs_ready, NH * (TT * l + t) + h + 1)
                        for kb in range(t + 1):
                            ks = slice(kb * P, (kb + 1) * P)
                            last = nc.tensor.transpose(out[:, ks], probs[h % 2][:, ks], ident[:])
                    else:
                        wait_side_taken(pe, l, "probT", t, 2 * h)
                        wait_side_taken(pe, l, "probT", t, 2 * h + 1)
                        for i in range(2):
                            head = 2 * h + i
                            n = head // 4
                            for kb in range(t + 1):
                                last = mm(out[:, i * HD:(i + 1) * HD], probT[head % 4][:, kb, :],
                                          vals[:, kb, n * HD:(n + 1) * HD], start=(kb == 0), stop=(kb == t))
                    last.then_inc(side_full, 1)
                    n = KT * hh + h
                    if kind == "logits" and sub in mixer_adas(l) and t > 0 and \
                            not (t == TT - 1 and n >= ADA_SLOTS - ADA_NORM):
                        ada(sub, n)
                out = open_side(l, "ycT", t)
                wait_side_taken(pe, l, "pv", t, NH // 2 - 1)
                for c in range(4):
                    last = nc.tensor.transpose(out[:, c * P:(c + 1) * P],
                                               o_tok[:, 2 * c:2 * c + 2, :].rearrange("p a n -> p (a n)"), ident[:])
                last.then_inc(side_full, 1)
                if sub in mixer_adas(l) and t < TT - 1:
                    ada_turn(sub, hh)

            def sample_attention(l):
                pe.wait_ge(ki_loaded, 16 * NB * PAGES * (l + 1))
                for j in range(2):
                    out = open_side(l, "kiT_page", j)
                    for i in range(4):
                        last = nc.tensor.transpose(out[:, i * P:(i + 1) * P],
                                                   ki_page[:, 4 * j + i].rearrange("p a n -> p (a n)"), ident[:])
                    last.then_inc(side_full, 1)
                out = open_side(l, "s_index")
                pe.wait_ge(q_blk_ready, l + 1)
                wait_side_taken(pe, l, "kiT_page", 1)
                for b in range(NB):
                    last = mm(out[0:NB * IDXH, 0:LVIS], qi_blk[:, b].rearrange("p b h -> p (b h)"), kiT_s[:, b, :],
                              start=(b == 0), stop=(b == NB - 1))
                last.then_inc(side_full, 1)
                out = open_side(l, "s_wsel")
                pe.wait_ge(wi_exp_ready, l + 1)
                nc.tensor.transpose(out[0:NB * IDXH, 0:NB], wi_exp[:].rearrange("p b h -> p (b h)"), ident[0:NB, 0:NB])\
                    .then_inc(side_full, 1)
                out = open_side(l, "s_score")
                wait_side_taken(pe, l, "s_index")
                wait_side_taken(pe, l, "s_wsel")
                mm(out[0:NB, 0:LVIS], wi_sel[:], rel_s[:], start=True, stop=True).then_inc(side_full, 1)
                pe.wait_ge(k_loaded, 16 * NB * PAGES * (l + 1))
                for j in range(4):
                    out = open_side(l, "kT_page", j)
                    for i in range(4):
                        b, pg = 2 * j + i // 2, i % 2
                        last = nc.tensor.transpose(out[:, i * P:(i + 1) * P], k_page[:, b, pg, :], ident[:])
                    last.then_inc(side_full, 1)
                out = open_side(l, "s_logits")
                wait_side_taken(pe, l, "kT_page", 3)
                for b in range(NB):
                    mm(out[0:NB * NH, 0:LVIS], q_blk[:, b].rearrange("p b n g -> p (b n g)"), kT_s[:, b, :],
                       start=(b == 0), stop=False)
                gates(l, "merge", 0, 0, 0)
                pe.wait_ge(mask_s_ready, l + 1)
                mm(out[0:NB * NH, 0:LVIS], spread_heads[:], mask_s[:], start=False, stop=True).then_inc(side_full, 1)
                out = open_side(l, "s_probT")
                pe.wait_ge(s_probs_ready, l + 1)
                for pg in range(PAGES):
                    nc.tensor.transpose(out[:, pg * NB * NH:(pg + 1) * NB * NH], prob_s[:, pg * P:(pg + 1) * P],
                                        ident[0:NB * NH, 0:NB * NH])
                pe.wait_ge(own_diag_ready, l + 1)
                mm(out[0:NB, 2 * NB * NH:3 * NB * NH], gather_heads[:], own_diag[:], start=True, stop=True)\
                    .then_inc(side_full, 1)
                out = open_side(l, "s_o")
                wait_side_taken(pe, l, "s_probT")
                pe.wait_ge(v_loaded, 16 * NB * PAGES * (l + 1))
                for b in range(NB):
                    for pg in range(PAGES):
                        mm(out[0:NB * NH, 0:P], probT_blk[:, pg, b, :], v_page[:, b, pg, :],
                           start=(b == 0 and pg == 0), stop=False)
                mm(out[0:NB * NH, 0:P], own_prob[:], vals[0:NB, TT, :], start=False, stop=True).then_inc(side_full, 1)
                out = open_side(l, "s_oT")
                wait_side_taken(pe, l, "s_o")
                nc.tensor.transpose(out[:, 0:NB * NH], o_s[:], ident[0:NB * NH, 0:NB * NH]).then_inc(side_full, 1)

            def gates(l, stage, r, j, group, tiles=(0, 1)):
                wait_slot(l, stage, r, j)
                for a in tiles:
                    for hf in range(2):
                        b = 2 * a + hf
                        take_main(b, main_use(l, stage, group))
                        product(bank[b][:, 0:HALF], [(a * KT + k, k) for k in range(KT)], weights(j),
                                moving(h_hi, h_lo, hf)).then_inc(main_full, 1)

            def merge(l):
                def projections(r, j):
                    for n in range(2):
                        for hf in range(2):
                            for br, (first, count) in enumerate(((0, 2), (2, 2), (4, 4))):
                                g = 6 * n + 3 * hf + br
                                take_main(g % 4, main_use(l, "merge", projections_at(r) + g // 4))
                                hi, lo, off = (yab_hi, yab_lo, 0) if br < 2 else (yc_hi, yc_lo, 4)
                                product(bank[g % 4][:, 0:HALF],
                                        [(n * KT + first + k, first + k - off) for k in range(count)],
                                        weights(j), moving(hi, lo, hf)).then_inc(main_full, 1)

                gates(l, "merge", 0, 1, 1)
                wait_side_taken(pe, l, "s_oT")
                for r in range(2):
                    wait_slot(l, "merge", 1, r)
                    projections(r, r)
                with pe.Fori(2, 4) as r:
                    for slot in range(3):
                        gates(l, "merge", 2 * (r - 1) + slot // 2, slot % 2, 6 * r - 4 + slot)
                    wait_slot(l, "merge", 2 * (r - 1) + 1, 1)
                    projections(r, 1)
                def out_products(j, b, ks):
                    blk_hi, blk_lo = weights(j)
                    x_hi, x_lo = moving(mrg_hi, mrg_lo, b % 2)
                    n = b // 2 * KT
                    split_products([bank[b][:, 0:HALF]] * len(ks), ks,
                                   [(blk_hi(n + k), blk_lo(n + k)) for k in ks], [(x_hi(k), x_lo(k)) for k in ks])

                wait_slot(l, "out", 0, 0)
                pe.wait_ge(mrg_lo_ready, 16 * l + 12)
                for b in range(4):
                    take_main(b, main_use(l, "out"))
                    out_products(0, b, range(6))
                for k in (6, 7):
                    pe.wait_ge(mrg_lo_ready, 16 * l + 2 * k + 2)
                    for b in range(4):
                        out_products(0, b, [k])

                def out_slot(r, j):
                    wait_slot(l, "out", r, j)
                    for b in range(4):
                        take_main(b, main_use(l, "out", 2 * r + j))
                        out_products(j, b, range(KT))

                out_slot(0, 1)
                for j in range(2):
                    out_slot(1, j)

            pe.wait_ge(cond_ready, 1)
            for n in range(ADA_SLOTS):
                ada(0, n)
                if n == KT - 1:
                    pe.wait_ge(const_loaded, 16 * 12)
                    pe.wait_ge(setup_done, 3)
                if n % KT == KT - 1:
                    ada_turn(0, n // KT)
                if n == ADA_SLOTS - ADA_NORM - 1:
                    statistics(0)
            mids = 0
            for l in range(DEPTH):
                for f in range(2):
                    sub = N_SUB * l + 2 * f
                    norm(sub)
                    for p_ in range(2):
                        ffn_up(l, f"up{f}{p_}", UP[p_], sub if p_ == 0 else None)
                        mids += 2 * UP[p_]
                        if f == 0 and p_ == 1:
                            ada_turn(sub + 1, 0)
                        if f == 1 and p_ == 0 and sub + 1 < DEPTH * N_SUB:
                            ada_turn(sub + 1, 1)
                        down(l, f"down{f}{p_}", UP[p_], mids, sub + 1 if f == 0 else None, p_)
                    if f == 0:
                        ada_turn(sub + 1, 1)
                        norm(sub + 1)
                        token_major(l)
                        pool_branch(l)
                        for slot in range(2):
                            gates(l, "gates0", 0, slot, slot)
                        for b in range(4):
                            hgrn_projection(l, 0, b)
                        rotary(l)
                        hgrn(l)
                        prompt_index(l, 0)
                        for t in range(TT):
                            if t + 1 < TT:
                                prompt_index(l, t + 1)
                            prompt_attention(l, t)
                        sample_attention(l)
                        merge(l)


def kernel(**inputs):
    import concourse.bacc as bacc
    from concourse.bass_utils import run_bass_kernel_spmd

    a = {k: np.asarray(v) for k, v in inputs.items()}

    def blocks(w):
        k, n = w.shape
        return w.reshape(k // P, P, n // P, P).transpose(1, 2, 0, 3)

    def per_slot(w, tiles):
        p, n, k, _ = w.shape
        return w.reshape(p, n // tiles, tiles * k * P).transpose(1, 0, 2)

    w = np.zeros((DEPTH * LAYER_SLOTS, P, SLOT), np.float32)
    for l in range(DEPTH):
        at = LAYER_SLOTS * l
        w_in = a["w_in"][l]
        cuts = np.cumsum((256, 512, 512, 256, 256, 512, 128, 128, 256, 64, 4))
        u, hq, hf, hi, hg, aq, ak, av, iq, ik, iw, gl = np.split(w_in, cuts, axis=1)
        for f in (0, 1):
            g_b, u_b = blocks(a["ffn_wg"][l, f]), blocks(a["ffn_wu"][l, f])
            down = blocks(a["ffn_wd"][l, f])
            first = 0
            for p_, tiles in enumerate(UP):
                s0 = at + SLOT0[f"up{f}{p_}"]
                both = np.stack([g_b[:, first:first + tiles], u_b[:, first:first + tiles]], 2)
                w[s0:s0 + tiles] = both.reshape(P, tiles, SLOT).transpose(1, 0, 2)
                s0 = at + SLOT0[f"down{f}{p_}"]
                w[s0:s0 + KT, :, 0:tiles * P] = per_slot(down[:, :, first:first + tiles], 1)
                first += tiles
        token = [u, hi, hg, aq[:, 0:256], aq[:, 256:512], np.concatenate([ak, av], 1), iq,
                 np.concatenate([ik, iw, np.zeros((D_MODEL, 256 - 68), np.float32)], 1)]
        s0 = at + SLOT0["token"]
        for n, t in enumerate(token):
            w[s0 + n] = t.reshape(KT, P, 256).transpose(1, 0, 2).reshape(P, SLOT)
        s0 = at + SLOT0["hgrn"]
        w[s0:s0 + HH] = np.stack([blocks(hq), blocks(hf)], 2).reshape(P, HH, SLOT).transpose(1, 0, 2)
        gates = blocks(gl).reshape(P, N_SUB, KT, KT, P).transpose(0, 2, 1, 3, 4)
        gates = gates.reshape(P, 12, SLOT)
        branches = np.concatenate([blocks(a["w_ba"][l]), blocks(a["w_bb"][l]), blocks(a["w_bc"][l])], 2)
        branches = branches.reshape(P, 4, SLOT)
        order = {"gates0": "g0 g1", "gates1": "g2 g3", "merge": "g4 g5 p0 p1 g6 g7 g8 p2 g9 g10 g11 p3"}
        for stage, slots in order.items():
            for n, slot in enumerate(slots.split()):
                w[at + SLOT0[stage] + n] = (gates if slot[0] == "g" else branches)[:, int(slot[1:])]
        s0 = at + SLOT0["out"]
        w[s0:s0 + 4] = per_slot(blocks(a["w_out"][l]), 2)

    ada = a["ada_w"].reshape(DEPTH, KT, P, N_SUB, ADA_CHUNKS, 2, ADA_N).transpose(0, 3, 5, 1, 2, 4, 6)
    ada = ada.reshape(DEPTH * N_SUB * ADA_SLOTS, P, ADA_CHUNKS * ADA_N)
    tokens = np.concatenate([a["x_prompt"][0], a["x_sample"][:, 0]])
    pool_w = np.zeros((DEPTH, P, 2, P), np.float32)
    for g in range(4):
        half = slice((g % 2) * POOL_G, (g % 2 + 1) * POOL_G)
        pool_w[:, half, g // 2, half] = a["pool_w"][:, g]
    gamma = np.ones((DEPTH, ROT, HD), np.float32)
    gamma[:, 0:8] = a["q_norm"][:, None]
    gamma[:, 8:10] = a["k_norm"][:, None]
    n_phys = a["cache_k"].shape[1]
    arrays = {
        "w": w,
        "ada": ada,
        "x": tokens.T.reshape(KT, P, COLS).transpose(1, 0, 2),
        "cond": np.concatenate([a["c_prompt"], a["c_sample"]]).T.reshape(KT, P, CC).transpose(1, 0, 2),
        "ada_b": a["ada_b"].reshape(DEPTH * N_SUB, 24, P).transpose(2, 0, 1),
        "norm_g": a["norm_g"].reshape(DEPTH * N_SUB, KT, P).transpose(2, 0, 1),
        "hgrn_lb": a["hgrn_lb"].reshape(DEPTH, HH, P).transpose(2, 0, 1),
        "hgrn_onorm": a["hgrn_onorm"],
        "pool_scale": a["pool_scale"].reshape(DEPTH, 2, P).transpose(2, 0, 1),
        "pool_w": pool_w,
        "gamma": gamma,
        "page_table": a["page_table"].reshape(1, NB * PAGES),
        "cache_k": a["cache_k"].reshape(DEPTH, n_phys, P, P),
        "cache_v": a["cache_v"].reshape(DEPTH, n_phys, P, P),
        "cache_ki": a["cache_ki"],
        "state_pool": a["state_pool"].reshape(DEPTH, NB * POOL_STATE, 256),
        "state_hgrn": a["state_hgrn"].transpose(0, 3, 1, 2, 4).reshape(DEPTH, P, NB * HIW),
    }
    arrays.update(constants())
    arrays = {k: np.ascontiguousarray(v) for k, v in arrays.items()}
    outputs = {
        "y": (P, KT, COLS),
        "k_out": (DEPTH, P, TT + 1, NKV * HD),
        "v_out": (DEPTH, P, TT + 1, NKV * HD),
        "ki_out": (DEPTH, P, TT + 1, HD),
        "pool_p": (DEPTH, POOL_STATE, 256),
        "pool_s": (DEPTH, NB, POOL_STATE, 256),
        "hgrn_p": (DEPTH, P, HH, HV),
        "hgrn_s": (DEPTH, P, NB * HIW),
    }
    nc = bacc.Bacc("TRN2", target_bir_lowering=False, num_devices=1)
    d = {}
    for k, v in arrays.items():
        d[k] = nc.dram_tensor(f"in_{k}", v.shape, mybir.dt.from_np(v.dtype), kind="ExternalInput").ap()
    for k, shape in outputs.items():
        d[k] = nc.dram_tensor(f"out_{k}", shape, F32, kind="ExternalOutput").ap()
    build(nc, d)
    res = run_bass_kernel_spmd(nc, [{f"in_{k}": v for k, v in arrays.items()}], core_ids=[0])
    o = {k: np.asarray(res.results[0][f"out_{k}"]) for k in outputs}

    y = o["y"].transpose(2, 1, 0).reshape(COLS, D_MODEL)

    def tokens_of(t):
        n = t.shape[-1]
        return (t[:, :, 0:TT].transpose(0, 2, 1, 3).reshape(DEPTH, 1, SEQ, n),
                t[:, 0:NB, TT].reshape(DEPTH, NB, 1, n))

    k_p, k_s = tokens_of(o["k_out"])
    v_p, v_s = tokens_of(o["v_out"])
    ki_p, ki_s = tokens_of(o["ki_out"])
    heads = (NKV, HD)
    hgrn_s = o["hgrn_s"].reshape(DEPTH, P, NB, HH, HV).transpose(0, 2, 3, 1, 4)
    c = np.ascontiguousarray
    return (c(y[0:SEQ][None]), c(y[SEQ:][:, None]),
            c(k_p.reshape(DEPTH, 1, SEQ, *heads)), c(v_p.reshape(DEPTH, 1, SEQ, *heads)), c(ki_p),
            c(o["pool_p"][:, None]), c(o["hgrn_p"].transpose(0, 2, 1, 3)[:, None]),
            c(k_s.reshape(DEPTH, NB, 1, *heads)), c(v_s.reshape(DEPTH, NB, 1, *heads)), c(ki_s),
            c(o["pool_s"]), c(hgrn_s))
```
